# Optimizing a Trainium2 kernel written in Bass

```python
import math
import jax, jax.numpy as jnp
from jax import lax
import numpy as np

D_MODEL = 1024
BATCH = 1
SEQ = 256
DEPTH = 2

PLE_DIM = 256
D_FF = 2816
D_RNN = D_MODEL
RNN_BLOCKS = 16
RNN_BW = D_RNN // RNN_BLOCKS
CONV_W = 4
RG_C = 8.0
N_HEADS = 8
HEAD_DIM = 128
D_ATTN = N_HEADS * HEAD_DIM
Q_BLOCK = 128
N_IN = 2 * D_RNN + 3 * D_ATTN + N_HEADS + 2 * D_MODEL
EPS = 1e-6


def rms_norm(x, g):
    xf = x.astype(jnp.float32)
    y = xf * lax.rsqrt(jnp.mean(xf * xf, axis=-1, keepdims=True) + EPS)
    return (y * g.astype(jnp.float32)).astype(x.dtype)

def swiglu_ffn(h, w_in, w_out):
    g, u = jnp.split(h @ w_in, 2, axis=-1)
    return (jax.nn.silu(g) * u) @ w_out

def causal_dwconv(x, w, b):
    S = x.shape[1]
    xp = jnp.pad(x, ((0, 0), (CONV_W - 1, 0), (0, 0)))
    y = b + xp[:, 0:S] * w[0]
    for k in range(1, CONV_W):
        y = y + xp[:, k:k + S] * w[k]
    return y

def rg_lru(x, w_a, b_a, w_x, b_x, lam):
    B, S, C = x.shape
    xb = x.reshape(B, S, RNN_BLOCKS, RNN_BW)
    r = jax.nn.sigmoid(jnp.einsum('bsnc,ncd->bsnd', xb, w_a).reshape(B, S, C) + b_a)
    i = jax.nn.sigmoid(jnp.einsum('bsnc,ncd->bsnd', xb, w_x).reshape(B, S, C) + b_x)
    log_a = -RG_C * r.astype(jnp.float32) * jax.nn.softplus(-lam.astype(jnp.float32))
    a = jnp.exp(log_a)
    mult = jnp.sqrt(-jnp.expm1(2.0 * log_a))
    u = mult * (i * x).astype(jnp.float32)

    def combine(left, right):
        a1, b1 = left
        a2, b2 = right
        return a1 * a2, a2 * b1 + b2

    _, h = lax.associative_scan(combine, (a, u), axis=1)
    return h.astype(x.dtype)

def forgetting_attention(q, k, v, f_logit, f_b, q_g, k_g):
    B, S, _ = q.shape
    q = rms_norm(q.reshape(B, S, N_HEADS, HEAD_DIM), q_g)
    k = rms_norm(k.reshape(B, S, N_HEADS, HEAD_DIM), k_g)
    v = v.reshape(B, S, N_HEADS, HEAD_DIM)
    log_f = jax.nn.log_sigmoid((f_logit + f_b).astype(jnp.float32))
    dcum = jnp.cumsum(log_f, axis=1).transpose(0, 2, 1)
    qh = q.transpose(0, 2, 1, 3)
    kh = k.transpose(0, 2, 1, 3)
    vh = v.transpose(0, 2, 1, 3)
    nb = S // Q_BLOCK
    q_blocks = qh.reshape(B, N_HEADS, nb, Q_BLOCK, HEAD_DIM).transpose(2, 0, 1, 3, 4)
    d_blocks = dcum.reshape(B, N_HEADS, nb, Q_BLOCK).transpose(2, 0, 1, 3)
    kpos = jnp.arange(S)
    scale = 1.0 / math.sqrt(HEAD_DIM)

    def one_block(args):
        qb, dqb, blk = args
        s = jnp.einsum('bhqd,bhkd->bhqk', qb, kh).astype(jnp.float32) * scale
        s = s + dqb[..., None] - dcum[:, :, None, :]
        qpos = blk * Q_BLOCK + jnp.arange(Q_BLOCK)
        s = jnp.where(kpos[None, :] <= qpos[:, None], s, -jnp.inf)
        pr = jax.nn.softmax(s, axis=-1).astype(vh.dtype)
        return jnp.einsum('bhqk,bhkd->bhqd', pr, vh)

    o = lax.map(one_block, (q_blocks, d_blocks, jnp.arange(nb)))
    return o.transpose(1, 0, 3, 2, 4).reshape(B, S, D_ATTN)

def first_inputs(seed: int = 0) -> dict:
    key = jax.random.key(seed)
    ks = jax.random.split(key, 32)
    f32 = jnp.float32

    def nrm(k, shape, fan_in):
        return jax.random.normal(k, shape, f32) * (fan_in ** -0.5)

    def gain(k, shape):
        return 1.0 + 0.05 * jax.random.normal(k, shape, f32)

    def small(k, shape):
        return 0.02 * jax.random.normal(k, shape, f32)

    a_c = jax.random.uniform(ks[12], (DEPTH, D_RNN), f32, 0.9, 0.999)
    s = a_c ** (1.0 / RG_C)
    rg_lambda = jnp.log(s) - jnp.log1p(-s)

    return {
        "x": jax.random.normal(ks[0], (BATCH, SEQ, D_MODEL), f32),
        "p": jax.random.normal(ks[1], (DEPTH, BATCH, SEQ, PLE_DIM), f32),
        "ffn1_norm": gain(ks[2], (DEPTH, D_MODEL)),
        "ffn1_w_in": nrm(ks[3], (DEPTH, D_MODEL, 2 * D_FF), D_MODEL),
        "ffn1_w_out": nrm(ks[4], (DEPTH, D_FF, D_MODEL), D_FF),
        "mix_norm": gain(ks[5], (DEPTH, D_MODEL)),
        "w_in": nrm(ks[6], (DEPTH, D_MODEL, N_IN), D_MODEL),
        "merge_b": small(ks[7], (DEPTH, 2 * D_MODEL)),
        "conv_w": nrm(ks[8], (DEPTH, CONV_W, D_RNN), CONV_W),
        "conv_b": small(ks[9], (DEPTH, D_RNN)),
        "rg_wa": nrm(ks[10], (DEPTH, RNN_BLOCKS, RNN_BW, RNN_BW), RNN_BW),
        "rg_ba": small(ks[11], (DEPTH, D_RNN)),
        "rg_wx": nrm(ks[13], (DEPTH, RNN_BLOCKS, RNN_BW, RNN_BW), RNN_BW),
        "rg_bx": small(ks[14], (DEPTH, D_RNN)),
        "rg_lambda": rg_lambda,
        "f_b": jax.random.uniform(ks[15], (DEPTH, N_HEADS), f32, 1.0, 4.0),
        "q_norm": gain(ks[16], (DEPTH, HEAD_DIM)),
        "k_norm": gain(ks[17], (DEPTH, HEAD_DIM)),
        "w_rnn_out": nrm(ks[18], (DEPTH, D_RNN, D_MODEL), D_RNN),
        "w_attn_out": nrm(ks[19], (DEPTH, D_ATTN, D_MODEL), D_ATTN),
        "w_o": nrm(ks[20], (DEPTH, D_MODEL, D_MODEL), D_MODEL),
        "ffn2_norm": gain(ks[21], (DEPTH, D_MODEL)),
        "ffn2_w_in": nrm(ks[22], (DEPTH, D_MODEL, 2 * D_FF), D_MODEL),
        "ffn2_w_out": nrm(ks[23], (DEPTH, D_FF, D_MODEL), D_FF),
        "ple_norm": gain(ks[24], (DEPTH, D_MODEL)),
        "ple_w_gate": nrm(ks[25], (DEPTH, D_MODEL, D_MODEL), D_MODEL),
        "ple_b_gate": small(ks[26], (DEPTH, D_MODEL)),
        "ple_w_proj": nrm(ks[27], (DEPTH, PLE_DIM, D_MODEL), PLE_DIM),
        "final_norm": gain(ks[28], (D_MODEL,)),
    }

def first_block(x, p, ffn1_norm, ffn1_w_in, ffn1_w_out, mix_norm, w_in, merge_b,
              conv_w, conv_b, rg_wa, rg_ba, rg_wx, rg_bx, rg_lambda, f_b, q_norm, k_norm,
              w_rnn_out, w_attn_out, w_o, ffn2_norm, ffn2_w_in, ffn2_w_out,
              ple_norm, ple_w_gate, ple_b_gate, ple_w_proj, final_norm):
    split_idx = list(np.cumsum([D_RNN, D_RNN, D_ATTN, D_ATTN, D_ATTN, N_HEADS, D_MODEL]))
    for i in range(DEPTH):
        x = x + 0.5 * swiglu_ffn(rms_norm(x, ffn1_norm[i]), ffn1_w_in[i], ffn1_w_out[i])

        h = rms_norm(x, mix_norm[i])
        proj = h @ w_in[i]
        rx, rgate, q, k, v, f_logit, ga, gb = jnp.split(proj, split_idx, axis=-1)

        rx = causal_dwconv(rx, conv_w[i], conv_b[i])
        ya = rg_lru(rx, rg_wa[i], rg_ba[i], rg_wx[i], rg_bx[i], rg_lambda[i])
        ya = (ya * jax.nn.gelu(rgate)) @ w_rnn_out[i]

        yb = forgetting_attention(q, k, v, f_logit, f_b[i], q_norm[i], k_norm[i]) @ w_attn_out[i]

        mb_a, mb_b = jnp.split(merge_b[i], 2)
        merged = jax.nn.sigmoid(ga + mb_a) * ya + jax.nn.sigmoid(gb + mb_b) * yb
        x = x + merged @ w_o[i]

        x = x + 0.5 * swiglu_ffn(rms_norm(x, ffn2_norm[i]), ffn2_w_in[i], ffn2_w_out[i])

        gate = jax.nn.sigmoid(rms_norm(x, ple_norm[i]) @ ple_w_gate[i] + ple_b_gate[i])
        x = x + gate * (p[i] @ ple_w_proj[i])
    return rms_norm(x, final_norm)


GRID_W = 64
CTX_LEN = 256
CONV_WIDTH = 31
CONV_PAD = (CONV_WIDTH - 1) // 2
N_Q_HEADS = 16
N_KV_HEADS = 4
HEAD_DIM_2 = 64
WINDOW = 128
BLOCK = 128
ROPE_BASE = 10000.0
NORM_EPS = 1e-6
N_MOD = 9
N_CONV_LAYERS = (DEPTH + 1) // 2
N_ATTN_LAYERS = DEPTH // 2
Q_DIM = N_Q_HEADS * HEAD_DIM_2
KV_DIM = N_KV_HEADS * HEAD_DIM_2


def rmsnorm(x, g):
    xf = x.astype(jnp.float32)
    y = xf * lax.rsqrt(jnp.mean(xf * xf, axis=-1, keepdims=True) + NORM_EPS)
    return y.astype(x.dtype) * g

def modulate(x, g, shift, scale):
    return rmsnorm(x, g) * (1 + scale) + shift

def swiglu(h, w_in, w_out):
    gu = h @ w_in
    gate, up = jnp.split(gu, 2, axis=-1)
    return (jax.nn.silu(gate) * up) @ w_out

def conformer_conv(h, pw1_w, pw1_b, dw_w, dw_b, ln_g, ln_b, pw2_w, pw2_b):
    a = h @ pw1_w + pw1_b
    u, g = jnp.split(a, 2, axis=-1)
    u = u * jax.nn.sigmoid(g)
    u = lax.conv_general_dilated(
        u, dw_w[:, None, :].astype(u.dtype), window_strides=(1,),
        padding=[(CONV_PAD, CONV_PAD)], dimension_numbers=("NWC", "WIO", "NWC"),
        feature_group_count=D_MODEL) + dw_b
    uf = u.astype(jnp.float32)
    mu = jnp.mean(uf, axis=-1, keepdims=True)
    var = jnp.mean(jnp.square(uf - mu), axis=-1, keepdims=True)
    u = ((uf - mu) * lax.rsqrt(var + NORM_EPS)).astype(u.dtype) * ln_g + ln_b
    return jax.nn.silu(u) @ pw2_w + pw2_b

def axial_rope_tables(n_tok):
    n_rows = n_tok // GRID_W
    row = jnp.repeat(jnp.arange(n_rows), GRID_W).astype(jnp.float32)
    col = jnp.tile(jnp.arange(GRID_W), n_rows).astype(jnp.float32)
    n_freq = HEAD_DIM_2 // 4
    inv = ROPE_BASE ** (-jnp.arange(n_freq, dtype=jnp.float32) / n_freq)
    ang = jnp.stack([row[:, None] * inv, col[:, None] * inv], axis=1)
    return jnp.cos(ang), jnp.sin(ang)

def apply_rope(x, cos, sin):
    n_freq = HEAD_DIM_2 // 4
    xs = x.reshape(x.shape[:-1] + (2, 2, n_freq))
    x1 = xs[..., 0, :]
    x2 = xs[..., 1, :]
    bshape = (1, cos.shape[0]) + (1,) * (x.ndim - 3) + (2, n_freq)
    cs = cos.reshape(bshape).astype(x.dtype)
    sn = sin.reshape(bshape).astype(x.dtype)
    out = jnp.stack([x1 * cs - x2 * sn, x1 * sn + x2 * cs], axis=-2)
    return out.reshape(x.shape)

def windowed_gqa_sink(h_lat, h_ctx, w_qkv, w_o, sink, with_ctx_out):
    B, S, _ = h_lat.shape
    C = h_ctx.shape[1]
    G = N_Q_HEADS // N_KV_HEADS
    scale = HEAD_DIM_2 ** -0.5

    def proj(h):
        qkv = h @ w_qkv
        q = qkv[..., :Q_DIM].reshape(h.shape[:2] + (N_KV_HEADS, G, HEAD_DIM_2))
        k = qkv[..., Q_DIM:Q_DIM + KV_DIM].reshape(h.shape[:2] + (N_KV_HEADS, HEAD_DIM_2))
        v = qkv[..., Q_DIM + KV_DIM:].reshape(h.shape[:2] + (N_KV_HEADS, HEAD_DIM_2))
        return q, k, v

    ql, kl, vl = proj(h_lat)
    qc, kc, vc = proj(h_ctx)
    cos, sin = axial_rope_tables(S)
    ql = apply_rope(ql, cos, sin) * scale
    kl = apply_rope(kl, cos, sin)
    pad = ((0, 0), (WINDOW, WINDOW), (0, 0), (0, 0))
    k_pad = jnp.pad(kl, pad)
    v_pad = jnp.pad(vl, pad)
    sink_col = sink.reshape(N_KV_HEADS, G, 1, 1).astype(jnp.float32)
    kw = BLOCK + 2 * WINDOW

    def one_block(n):
        start = n * BLOCK
        qb = lax.dynamic_slice_in_dim(ql, start, BLOCK, axis=1)
        kb = lax.dynamic_slice_in_dim(k_pad, start, kw, axis=1)
        vb = lax.dynamic_slice_in_dim(v_pad, start, kw, axis=1)
        i_pos = start + jnp.arange(BLOCK)
        j_pos = start - WINDOW + jnp.arange(kw)
        valid = ((jnp.abs(j_pos[None, :] - i_pos[:, None]) <= WINDOW)
                 & (j_pos[None, :] >= 0) & (j_pos[None, :] < S))
        s_win = jnp.einsum('bqhgd,bkhd->bhgqk', qb, kb).astype(jnp.float32)
        s_win = jnp.where(valid, s_win, -jnp.inf)
        s_ctx = jnp.einsum('bqhgd,bchd->bhgqc', qb, kc).astype(jnp.float32)
        sinks = jnp.broadcast_to(sink_col, s_win.shape[:-1] + (1,))
        p = jax.nn.softmax(jnp.concatenate([s_win, s_ctx, sinks], axis=-1), axis=-1).astype(vb.dtype)
        o = (jnp.einsum('bhgqk,bkhd->bqhgd', p[..., :kw], vb)
             + jnp.einsum('bhgqc,bchd->bqhgd', p[..., kw:kw + C], vc))
        return o.reshape(B, BLOCK, Q_DIM)

    o = lax.map(one_block, jnp.arange(S // BLOCK))
    y_lat = jnp.moveaxis(o, 0, 1).reshape(B, S, Q_DIM) @ w_o

    y_ctx = None
    if with_ctx_out:
        s = jnp.einsum('bqhgd,bkhd->bhgqk', qc * scale, kc).astype(jnp.float32)
        sinks = jnp.broadcast_to(sink_col, s.shape[:-1] + (1,))
        p = jax.nn.softmax(jnp.concatenate([s, sinks], axis=-1), axis=-1).astype(vc.dtype)
        oc = jnp.einsum('bhgqk,bkhd->bqhgd', p[..., :C], vc)
        y_ctx = oc.reshape(B, C, Q_DIM) @ w_o
    return y_lat, y_ctx

def second_inputs(seed: int = 0) -> dict:
    key = jax.random.key(seed)
    ks = jax.random.split(key, 32)
    f32 = jnp.float32

    def nrm(k, shape, s):
        return jax.random.normal(k, shape, f32) * s

    D, F = D_MODEL, D_FF
    NC, NA = N_CONV_LAYERS, N_ATTN_LAYERS
    return {
        "x": nrm(ks[0], (BATCH, SEQ, D), 1.0),
        "c": nrm(ks[1], (BATCH, D), 1.0),
        "ctx": nrm(ks[2], (BATCH, CTX_LEN, D), 1.0),
        "c_ctx": nrm(ks[3], (D,), 1.0),
        "norm_g": 1.0 + nrm(ks[4], (DEPTH, 3, D), 0.05),
        "ada_w": nrm(ks[5], (DEPTH, D, N_MOD * D), D ** -0.5),
        "ada_b": nrm(ks[6], (DEPTH, N_MOD * D), 0.02),
        "ffn1_wi": nrm(ks[7], (DEPTH, D, 2 * F), D ** -0.5),
        "ffn1_wo": nrm(ks[8], (DEPTH, F, D), F ** -0.5),
        "ffn2_wi": nrm(ks[9], (DEPTH, D, 2 * F), D ** -0.5),
        "ffn2_wo": nrm(ks[10], (DEPTH, F, D), F ** -0.5),
        "conv_pw1_w": nrm(ks[11], (NC, D, 2 * D), D ** -0.5),
        "conv_pw1_b": nrm(ks[12], (NC, 2 * D), 0.02),
        "conv_dw_w": nrm(ks[13], (NC, CONV_WIDTH, D), CONV_WIDTH ** -0.5),
        "conv_dw_b": nrm(ks[14], (NC, D), 0.02),
        "conv_ln_g": 1.0 + nrm(ks[15], (NC, D), 0.05),
        "conv_ln_b": nrm(ks[16], (NC, D), 0.02),
        "conv_pw2_w": nrm(ks[17], (NC, D, D), D ** -0.5),
        "conv_pw2_b": nrm(ks[18], (NC, D), 0.02),
        "attn_w_qkv": nrm(ks[19], (NA, D, Q_DIM + 2 * KV_DIM), D ** -0.5),
        "attn_w_o": nrm(ks[20], (NA, Q_DIM, D), Q_DIM ** -0.5),
        "attn_sink": nrm(ks[21], (NA, N_Q_HEADS), 1.0),
        "final_g": 1.0 + nrm(ks[22], (D,), 0.05),
    }

def second_block(x, c, ctx, c_ctx, norm_g, ada_w, ada_b, ffn1_wi, ffn1_wo, ffn2_wi, ffn2_wo,
              conv_pw1_w, conv_pw1_b, conv_dw_w, conv_dw_b, conv_ln_g, conv_ln_b,
              conv_pw2_w, conv_pw2_b, attn_w_qkv, attn_w_o, attn_sink, final_g):
    for i in range(DEPTH):
        last = i == DEPTH - 1
        m_lat = (jax.nn.silu(c) @ ada_w[i] + ada_b[i])[:, None, :]
        m_ctx = (jax.nn.silu(c_ctx) @ ada_w[i] + ada_b[i])[None, None, :]
        sh1, sc1, gt1, sh2, sc2, gt2, sh3, sc3, gt3 = jnp.split(m_lat, N_MOD, axis=-1)
        ch1, cs1, cg1, ch2, cs2, cg2, ch3, cs3, cg3 = jnp.split(m_ctx, N_MOD, axis=-1)
        g1, g2, g3 = norm_g[i, 0], norm_g[i, 1], norm_g[i, 2]

        x = x + 0.5 * gt1 * swiglu(modulate(x, g1, sh1, sc1), ffn1_wi[i], ffn1_wo[i])
        ctx = ctx + 0.5 * cg1 * swiglu(modulate(ctx, g1, ch1, cs1), ffn1_wi[i], ffn1_wo[i])

        hx = modulate(x, g2, sh2, sc2)
        hc = modulate(ctx, g2, ch2, cs2)
        j = i // 2
        if i % 2 == 0:
            conv_args = (conv_pw1_w[j], conv_pw1_b[j], conv_dw_w[j], conv_dw_b[j],
                         conv_ln_g[j], conv_ln_b[j], conv_pw2_w[j], conv_pw2_b[j])
            y_lat = conformer_conv(hx, *conv_args)
            y_ctx = None if last else conformer_conv(hc, *conv_args)
        else:
            y_lat, y_ctx = windowed_gqa_sink(hx, hc, attn_w_qkv[j], attn_w_o[j],
                                             attn_sink[j], not last)
        x = x + gt2 * y_lat

        x = x + 0.5 * gt3 * swiglu(modulate(x, g3, sh3, sc3), ffn2_wi[i], ffn2_wo[i])
        if not last:
            ctx = ctx + cg2 * y_ctx
            ctx = ctx + 0.5 * cg3 * swiglu(modulate(ctx, g3, ch3, cs3), ffn2_wi[i], ffn2_wo[i])
    return rmsnorm(x, final_g)


def setup_inputs(seed=0):
    out = dict(first_inputs(seed))
    for name, value in second_inputs(seed + 1).items():
        if name != "x":
            out[name + "_2"] = value
    return out


def reference(
    x, p, ffn1_norm, ffn1_w_in, ffn1_w_out, mix_norm, w_in, merge_b, conv_w, conv_b, rg_wa,
    rg_ba, rg_wx, rg_bx, rg_lambda, f_b, q_norm, k_norm, w_rnn_out, w_attn_out, w_o, ffn2_norm,
    ffn2_w_in, ffn2_w_out, ple_norm, ple_w_gate, ple_b_gate, ple_w_proj, final_norm, c_2, ctx_2,
    c_ctx_2, norm_g_2, ada_w_2, ada_b_2, ffn1_wi_2, ffn1_wo_2, ffn2_wi_2, ffn2_wo_2,
    conv_pw1_w_2, conv_pw1_b_2, conv_dw_w_2, conv_dw_b_2, conv_ln_g_2, conv_ln_b_2,
    conv_pw2_w_2, conv_pw2_b_2, attn_w_qkv_2, attn_w_o_2, attn_sink_2, final_g_2,
):
    x = first_block(
        x, p, ffn1_norm, ffn1_w_in, ffn1_w_out, mix_norm, w_in, merge_b, conv_w, conv_b, rg_wa,
        rg_ba, rg_wx, rg_bx, rg_lambda, f_b, q_norm, k_norm, w_rnn_out, w_attn_out, w_o,
        ffn2_norm, ffn2_w_in, ffn2_w_out, ple_norm, ple_w_gate, ple_b_gate, ple_w_proj,
        final_norm,
    )
    return second_block(
        x, c_2, ctx_2, c_ctx_2, norm_g_2, ada_w_2, ada_b_2, ffn1_wi_2, ffn1_wo_2, ffn2_wi_2,
        ffn2_wo_2, conv_pw1_w_2, conv_pw1_b_2, conv_dw_w_2, conv_dw_b_2, conv_ln_g_2,
        conv_ln_b_2, conv_pw2_w_2, conv_pw2_b_2, attn_w_qkv_2, attn_w_o_2, attn_sink_2,
        final_g_2,
    )


_drawn_inputs = setup_inputs


def setup_inputs(seed=0):
    import zlib

    import numpy as np

    out = dict(_drawn_inputs(seed))
    spreads = {}
    factors = {'merge_b': 8.0,
     'rg_ba': 24.613,
     'rg_bx': 8.0,
     'q_norm': 5.802,
     'k_norm': 6.455,
     'ple_norm': 4.62,
     'ple_b_gate': 8.0,
     'conv_pw1_b_2': 8.0,
     'conv_dw_b_2': 5.441,
     'conv_ln_g_2': 2.688,
     'conv_ln_b_2': 7.131,
     'conv_pw2_b_2': 4.57,
     'attn_sink_2': 8.0}
    for name, (base, spread) in spreads.items():
        noise = np.random.default_rng([zlib.crc32(name.encode()), seed]).standard_normal(out[name].shape)
        drawn = base * np.exp(spread * noise) if base else spread * noise
        out[name] = __import__('jax').numpy.asarray(drawn.astype(out[name].dtype))
    for name, factor in factors.items():
        out[name] = (out[name] * factor).astype(out[name].dtype)
    return out
```

```python
import numpy as np

import concourse.bass as bass
from concourse import mybir

F32 = mybir.dt.float32
F32R = mybir.dt.float32r
ALU = mybir.AluOpType
ACT = mybir.ActivationFunctionType
AX_X = mybir.AxisListType.X

P = 128
T = 256
D = 1024
C = D // P
DEPTH = 2
F = 2816
FC = F // P
GROUPS = (8, 8, 6)
HEADS = 8
PLE = 256
RNN_BW = 64
N_MOD = 9
QH, KVH, HD = 16, 4, 64
TAPS = 31
PAD = (TAPS - 1) // 2
EPS = 1e-6
NEG = -3.0e38
GELU_C = 0.7978845608028654
GELU_A = 0.044715

ADA_UNITS = N_MOD * D // 256
GROUP_ADA = 4
FFN_A = 52
FFN_B = 34
K_MIX, K_FFN2, K_PLE, K_LAYER = FFN_A, FFN_A + 40, 2 * FFN_A + 40, 2 * FFN_A + 48
assert ADA_UNITS == 2 * (2 * GROUP_ADA + 10) and K_LAYER % 4 == 0
Q_LAYER = K_LAYER // 4
Q_SECOND = DEPTH * Q_LAYER
K2_CONV, K2_PW2, K2_FFN2, K2_L1 = FFN_B, FFN_B + 8, FFN_B + 12, 2 * FFN_B + 12
K2_Q, K2_KV, K2_WO, K2_FFN4 = K2_L1 + FFN_B, K2_L1 + FFN_B + 4, K2_L1 + FFN_B + 6, K2_L1 + FFN_B + 10
K2_END = K2_FFN4 + FFN_B


class Unit:

    def __init__(self, q, k):
        self.q, self.k = q, k
        self.slot = k % 4
        self.par = k % 2

    def later(self, by):
        return Unit(self.q, self.k + by)

    def last(self):
        return isinstance(self.q, int) and 4 * self.q + self.k >= 4 * Q_SECOND + K2_END

    def raw_full(self):
        return (self.q + (self.k // 4 + 1)) * 32

    def raw_free(self):
        return self.q * 8 + (2 * self.k + 2)

    def split_free(self, t):
        return self.q * 8 + (2 * self.k + t + 1)

    def hi_done(self, t):
        return self.q * 8 + (2 * self.k + t + 1)

    def lo_done(self, t):
        return self.q * 8 + (2 * self.k + t + 9)

    def mm_done(self, t):
        return self.q * 8 + (2 * self.k + t + 5)

    def banks_free(self):
        return self.q * 2 + (self.k // 2 + 1)

    def read_out(self):
        return self.q * 2 + (self.k // 2 + 2)


FULL_GROUP = [("G", 0), ("G", 1), ("A", 0), ("G", 2), ("G", 3), ("A", 1), ("G", 4), ("G", 5), ("A", 2),
              ("G", 6), ("G", 7), ("A", 3), ("O", 0), ("O", 1), ("O", 2), ("O", 3)]
LAST_GROUP = [x for i in range(10) for x in ((("G", i) if i < 6 else ("O", i - 6)), ("A", i))]
PLAIN_FULL = [x for x in FULL_GROUP if x[0] != "A"]
PLAIN_LAST = [x for x in LAST_GROUP if x[0] != "A"]

R_FFN1, R_MIX, R_MERGE, R_CONV, R_CONVB, R_BA, R_BX, R_LAM, R_FFN2, R_PLE, R_PLEB, R_QN, R_KN = (
    0, 8, 16, 32, 64, 72, 80, 88, 96, 104, 112, 120, 121)
R_LAYER = 122
R_FINAL, R_NORM, R_PW1B, R_DWB, R_LNG, R_LNB, R_PW2B, R_FING, R_C, R_CCTX = (
    0, 8, 56, 72, 80, 88, 96, 104, 112, 120)
PAR_TILES = 7
PAR_ROWS = (R_LAYER, R_LAYER, 128, 128, (TAPS - 16) * 8, 72, 72)
PAR_LOADS = 2 * 13 + 10 + 2 + 2

CO_IDENT, CO_LOW, CO_UP, CO_PICK, CO_N = 0, 128, 256, 384, 384 + 32
RO_COS, RO_SIN, RO_ROT, RO_DUP, RO_N = 0, 256, 512, 640, 896


def shape_constants():
    co = np.zeros((P, CO_N), np.float32)
    i = np.arange(P)
    co[:, CO_IDENT:CO_IDENT + P] = np.eye(P)
    co[:, CO_LOW:CO_LOW + P] = np.where(i[None, :] <= i[:, None], 0.0, NEG)
    co[:, CO_UP:CO_UP + P] = np.where(i[None, :] >= i[:, None], 0.0, NEG)
    co[:, CO_PICK + 15] = 1.0
    ro = np.zeros((P, RO_N), np.float32)
    n_freq = HD // 4
    inv = (np.float32(10000.0) ** (-np.arange(n_freq, dtype=np.float32) / np.float32(n_freq))).astype(np.float32)
    tok = np.arange(T)
    d = i % HD
    place = np.where((d // 32)[:, None] == 0, (tok // 64)[None, :], (tok % 64)[None, :]).astype(np.float32)
    angle = (place * inv[d % n_freq][:, None]).astype(np.float32)
    ro[:, RO_COS:RO_COS + T] = np.cos(angle)
    ro[:, RO_SIN:RO_SIN + T] = np.sin(angle)
    for m in range(P):
        if m % 32 < 16:
            ro[m + 16, RO_ROT + m] = -1.0
        else:
            ro[m - 16, RO_ROT + m] = 1.0
        for e in range(2):
            ro[64 * e + m % 64, RO_DUP + 128 * e + m] = 1.0
    return co, ro


def build(nc, A, out):
    off = [(nc.sbuf_base + 31) // 32 * 32]

    def sb(name, shape, dt=F32, at=None):
        size = 4 * int(np.prod(shape[1:]))
        where = off[0] if at is None else at
        if at is None:
            off[0] += (size + 31) // 32 * 32
        return nc.alloc_sbuf_tensor_at(name, shape, dt, offset=where)

    from contextlib import ExitStack
    ctx = ExitStack()
    with ctx:
        Xx = sb("Xx", [P, C, T])
        Xc = sb("Xc", [P, C, T])
        Hh = sb("Hh", [P, 2, C, T], F32R)
        hh_ctx_at = off[0] - 4 * C * T
        Hl = sb("Hl", [P, 2, C, T], F32R)
        fh_at = off[0]
        Fh = sb("Fh", [P, 2, C, T], F32R)
        fl_at = off[0]
        Fl = sb("Fl", [P, 2, C, T], F32R)
        decay = sb("decay", [P, C, T], at=fh_at)
        keep = sb("keep", [P, C, T], at=fl_at)
        gateA = sb("gateA", [P, C, T], at=hh_ctx_at)
        raw = sb("raw", [P, 4, C, 256])
        wh = sb("wh", [P, 2, C, 256], F32R)
        wl = sb("wl", [P, 2, C, 256], F32R)
        Gb = sb("Gb", [P, C, T])
        Qb = sb("Qb", [P, C, T])
        Kb = sb("Kb", [P, C, T])
        Vb = sb("Vb", [P, 2, D])
        Tt = sb("Tt", [P, 2, 512])
        Pp = sb("Pp", [P, 2, 512])
        Ss = sb("Ss", [P, 512])
        Rr = sb("Rr", [P, 512])
        par = sb("par", [P, PAR_TILES, P])
        cur = sb("cur", [P, R_LAYER])
        half = sb("half", [P, R_LAYER])
        co = sb("co", [P, CO_N])
        gate_at = off[0]
        wgate = sb("wgate", [P, 2, C, P])
        ro = sb("ro", [P, RO_N], at=gate_at)
        wf = sb("wf", [P, C, HEADS])
        ones = sb("ones", [P, P])
        MOD = sb("MOD", [P, DEPTH, N_MOD * C, 2])
        cs = sb("cs", [P, C, 4], F32R)
        tiny = sb("tiny", [P, 64])
        S1 = sb("S1", [P, 3, C, 2])
        G1 = sb("G1", [P, 3, C, 2])
        eps = sb("eps", [P, 2])
        dneg = sb("dneg", [HEADS, T])
        dmask = sb("dmask", [HEADS, T])
        rqk = sb("rqk", [2 * HEADS, T])
        fb = sb("fb", [HEADS, DEPTH])
        assert off[0] <= nc.sbuf_usable_end, (off[0], nc.sbuf_usable_end)
        ident, low, up = (co[:, a:a + P] for a in (CO_IDENT, CO_LOW, CO_UP))
        prow = Gb[:].rearrange("p c t -> p (c t)")[:, 0:PAR_TILES * P].rearrange("p (n f) -> p n f", f=P)
        xtok = Qb[:].rearrange("p c t -> p (c t)").rearrange("p (n d) -> p n d", n=2)
        ctok = Kb[:].rearrange("p c t -> p (c t)").rearrange("p (n d) -> p n d", n=2)
        ptok = Vb[:, :, 0:PLE]
        otok = Gb[:].rearrange("p c t -> p (c t)").rearrange("p (n d) -> p n d", n=2)
        upad = Vb[:].rearrange("p n d -> p (n d)")[:, 0:4 * (T + 2 * PAD)].rearrange(
            "p (b s t) -> p b s t", b=2, s=2)
        kraw = Gb[:].rearrange("p c t -> p (c t)")[:, 0:1024].rearrange("p (n t) -> p n t", n=2)
        kdup = Kb[:].rearrange("p c t -> p (c t)").rearrange("p (n t) -> p n t", n=KVH)
        v2 = Vb[:].rearrange("p n d -> p (n d)")[:, 0:4 * 256].rearrange("p (n d) -> p n d", n=4)
        rmask = Rr[0:2 * HEADS, :]
        scores = Tt[:, 0, 0:384]
        probsT = Tt[:, 1, 0:384]

        ps = ctx.enter_context(nc.psum_tensor("ps", [P, 8, 512], F32))

        def sem(name):
            return ctx.enter_context(nc.semaphore(name))

        raw_full = [sem(f"raw_full{i}") for i in range(4)]
        hi_done, lo_done, mm_done = sem("hi_done"), sem("lo_done"), sem("mm_done")
        banks_free = [sem(f"banks_free{i}") for i in range(2)]
        par_in, tok_in, small_in = sem("par_in"), sem("tok_in"), sem("small_in")
        zeroed, ones_there, turned, turned_out, x_there = sem("zeroed"), sem("ones_there"), sem("turned"), sem("turned_out"), sem("x_there")
        par_there, eps_there, lam_exp, c_tanh, c_prod, c_hi, c_there = (
            sem(n) for n in ("par_there", "eps_there", "lam_exp", "c_tanh", "c_prod", "c_hi", "c_there"))
        sq_done, ss_done, std_done, hp_done, hh_done, h_done = (
            sem(n) for n in ("sq_done", "ss_done", "std_done", "hp_done", "hh_done", "h_done"))
        x_normed, final_done = sem("x_normed"), sem("final_done")
        tanh_done, fh_done, f_done = sem("tanh_done"), sem("fh_done"), sem("f_done")
        cur_there, wgate_in, wf_in, rg_mm, rg_tanh, la_done, rg_exp, keep_done, root_done = (
            sem(n) for n in ("cur_there", "wgate_in", "wf_in", "rg_mm", "rg_tanh", "la_done", "rg_exp",
                             "keep_done", "root_done"))
        gelu_sq, gelu_arg, gelu_tanh = sem("gelu_sq"), sem("gelu_arg"), sem("gelu_tanh")
        qk_sq, qk_ss, qk_std = sem("qk_sq"), sem("qk_ss"), sem("qk_std")
        f_mm, f_in, f_abs, dneg_done = sem("f_mm"), sem("f_in"), sem("f_abs"), sem("dneg_done")
        y_done, yh_done, ya_done = sem("y_done"), sem("yh_done"), sem("ya_done")
        rm_done, bc_done, qkn_done, s_done, nmax_done, exp_done, pn_done, tr_done, pt_done, pv_done, oh_done, \
            o_done = (sem(n) for n in ("rm_done", "bc_done", "qkn_done", "s_done", "nmax_done", "exp_done",
                                       "pn_done", "tr_done", "pt_done", "pv_done", "oh_done", "o_done"))
        gb_tanh, mp_done, mh_done, m_done = sem("gb_tanh"), sem("mp_done"), sem("mh_done"), sem("m_done")
        p_in, p_turned, pth_done, p_there, pg_tanh = (
            sem(n) for n in ("p_in", "p_turned", "pth_done", "p_there", "pg_tanh"))
        mod_there, ro_in = sem("mod_there"), sem("ro_in")
        cv_tanh, cv_done, mu_mm, cen_done, csq_done, var_mm, cstd_done, z_done, zt_done, zp_done, zh_done, z_there = (
            sem(n) for n in ("cv_tanh", "cv_done", "mu_mm", "cen_done", "csq_done", "var_mm", "cstd_done",
                             "z_done", "zt_done", "zp_done", "zh_done", "z_there"))
        rot_mm, rot_done, dup_mm, dup_done, sink_mm, sink_done = (
            sem(n) for n in ("rot_mm", "rot_done", "dup_mm", "dup_done", "sink_mm", "sink_done"))
        s2_done, nm2_done, e2_done, pn2_done, tr2_done, pt2_done, pv2_done, oh2_done, o2_done = (
            sem(n) for n in ("s2_done", "nm2_done", "e2_done", "pn2_done", "tr2_done", "pt2_done", "pv2_done",
                             "oh2_done", "o2_done"))
        out_mm, out_copied, stored = sem("out_mm"), sem("out_copied"), sem("stored")

        def bank(u, t, n=512):
            return ps[:, 2 * u.par + t, 0:n]

        def pair(u):
            return ps[:, 2 * u.par:2 * u.par + 2, 0:T]

        def two(ap):
            return ap.rearrange("p (s n) -> p s n", s=2)

        def groups_of(eng, q, k, order, last):
            with eng.Fori(0, 2) as g:
                yield g, [(kind, i, Unit(q + g * (len(order) // 4), k + j)) for j, (kind, i) in enumerate(order)]
            yield 2, [(kind, i, Unit(q, k + 2 * len(order) + j)) for j, (kind, i) in enumerate(last)]

        def ada_index(s, g, i):
            return g * GROUP_ADA + (s * (ADA_UNITS // 2) + i)

        block = ctx.enter_context(nc.Block())

        @block.sync
        def _(sp):
            sp.dma_start(co[:], A["co"]).then_inc(small_in, 16)

            def row(tile, r, src):
                n = src.shape[0]
                sp.dma_start(prow[r:r + n, tile, :], src).then_inc(par_in, 16)

            for l in range(DEPTH):
                for r, name in ((R_FFN1, "ffn1_norm"), (R_MIX, "mix_norm"), (R_MERGE, "merge_b"), (R_CONVB, "conv_b"),
                                (R_BA, "rg_ba"), (R_BX, "rg_bx"), (R_LAM, "rg_lambda"), (R_FFN2, "ffn2_norm"),
                                (R_PLE, "ple_norm"), (R_PLEB, "ple_b_gate"), (R_QN, "q_norm"), (R_KN, "k_norm")):
                    row(l, r, A[name][l].rearrange("(c p) -> c p", p=P))
                row(l, R_CONV, A["conv_w"][l].rearrange("k (c p) -> (k c) p", p=P))
            for r, src in ((R_FINAL, A["final_norm"]), (R_PW1B, A["conv_pw1_b_2"][0]), (R_DWB, A["conv_dw_b_2"][0]),
                           (R_LNG, A["conv_ln_g_2"][0]), (R_LNB, A["conv_ln_b_2"][0]), (R_PW2B, A["conv_pw2_b_2"][0]),
                           (R_FING, A["final_g_2"]), (R_C, A["c_2"][0]), (R_CCTX, A["c_ctx_2"])):
                row(2, r, src.rearrange("(c p) -> c p", p=P))
            row(2, R_NORM, A["norm_g_2"].rearrange("l n (c p) -> (l n c) p", p=P))
            row(3, 0, A["conv_dw_w_2"][0, 0:16].rearrange("k (c p) -> (k c) p", p=P))
            row(4, 0, A["conv_dw_w_2"][0, 16:TAPS].rearrange("k (c p) -> (k c) p", p=P))
            for l in range(DEPTH):
                row(5 + l, 0, A["ada_b_2"][l].rearrange("(c p) -> c p", p=P))
            sp.dma_start(xtok, A["x"][0].rearrange("(n p) d -> p n d", p=P)).then_inc(tok_in, 16)
            with nc.allow_non_contiguous_dma(reason="sixteen values"):
                sp.dma_start(fb[:], A["f_b"].rearrange("l h -> h l")).then_inc(small_in, 16)
            sp.dma_start(tiny[0:1, 48:64], A["attn_sink_2"]).then_inc(small_in, 16)

            def load_pair(u, halves):
                sp.wait_ge(lo_done, u.raw_free())
                for h in range(2):
                    sp.dma_start(raw[:, u.slot, :, P * h:P * h + P], halves[:, :, h, :]) \
                        .then_inc(raw_full[u.slot], 16)

            def load_cols(u, w, col, kc=C, k0=0):
                rows = w.rearrange("(c p) n -> p c n", p=P)
                cols = bass.ds(col, 256) if not isinstance(col, int) else slice(col, col + 256)
                sp.wait_ge(lo_done, u.raw_free())
                for h in (1, 0):
                    a, n = h * (kc // 2), kc // 2
                    chunks = slice(k0 + a, k0 + a + n) if isinstance(k0, int) else bass.ds(k0 + a, n)
                    sp.dma_start(raw[:, u.slot, a:a + n, :], rows[:, chunks, cols]).then_inc(raw_full[u.slot], 16)

            def load_ffn(q, k, w_in, w_out, order, last, ada=None):
                gu = w_in.rearrange("(c p) (h n) -> p c h n", p=P, h=2)
                for g, units in groups_of(sp, q, k, order, last):
                    for kind, i, u in units:
                        if kind == "G":
                            f = g * (8 * P) + i * P
                            cols = slice(f, f + P) if isinstance(f, int) else bass.ds(f, P)
                            load_pair(u, gu[:, :, :, cols])
                        elif kind == "O":
                            load_cols(u, w_out, 256 * i, GROUPS[2] if isinstance(g, int) else 8, g * 8)
                        else:
                            l, s = ada
                            load_cols(u, A["ada_w_2"][l], ada_index(s, g, i) * 256)

            with sp.Fori(0, DEPTH) as l:
                q = l * Q_LAYER
                sp.wait_ge(zeroed, 1)
                sp.wait_ge(rg_mm, l * C + 1)
                for g, name in enumerate(("rg_wa", "rg_wx")):
                    blocks = A[name][l].rearrange("(j e) c d -> e c j d", e=2)
                    for e in range(2):
                        sl = slice(RNN_BW * e, RNN_BW * (e + 1))
                        sp.dma_start(wgate[sl, g, :, sl], blocks[e]).then_inc(wgate_in, 16)
                sp.wait_ge(f_mm, l + 1)
                with nc.allow_non_contiguous_dma(reason="eight columns"):
                    sp.dma_start(wf[:], A["w_in"][l].rearrange("(c p) n -> p c n", p=P)[:, :, 5 * D:5 * D + HEADS]) \
                        .then_inc(wf_in, 16)
                load_ffn(q, 0, A["ffn1_w_in"][l], A["ffn1_w_out"][l], FULL_GROUP, LAST_GROUP, (l, 0))
                w_in = A["w_in"][l]
                k = K_MIX
                for j in range(8):
                    load_cols(Unit(q, k + j), w_in, 256 * j)
                for i in range(12):
                    load_cols(Unit(q, k + 8 + i), w_in, 2 * D + (i % 3) * D + 256 * (i // 3))
                for j in range(4):
                    load_cols(Unit(q, k + 20 + j), w_in, 5 * D + HEADS + 256 * j)
                for j in range(4):
                    load_cols(Unit(q, k + 24 + j), A["w_rnn_out"][l], 256 * j)
                for j in range(4):
                    load_cols(Unit(q, k + 28 + 2 * j), w_in, 6 * D + HEADS + 256 * j)
                    load_cols(Unit(q, k + 29 + 2 * j), A["w_attn_out"][l], 256 * j)
                for j in range(4):
                    load_cols(Unit(q, k + 36 + j), A["w_o"][l], 256 * j)
                sp.wait_ge(pv_done, l * HEADS + HEADS)
                sp.dma_start(ptok, A["p"][l, 0].rearrange("(n p) d -> p n d", p=P)).then_inc(p_in, 16)
                load_ffn(q, K_FFN2, A["ffn2_w_in"][l], A["ffn2_w_out"][l], FULL_GROUP, LAST_GROUP, (l, 1))
                for j in range(4):
                    load_cols(Unit(q, K_PLE + 2 * j), A["ple_w_gate"][l], 256 * j)
                    load_cols(Unit(q, K_PLE + 2 * j + 1), A["ple_w_proj"][l], 256 * j, PLE // P)

            q = Q_SECOND
            sp.wait_ge(rg_mm, DEPTH * C + 1)
            sp.dma_start(ro[:], A["ro"]).then_inc(ro_in, 16)
            sp.wait_ge(s_done, DEPTH * HEADS)
            sp.dma_start(ctok, A["ctx_2"][0].rearrange("(n p) d -> p n d", p=P)).then_inc(tok_in, 16)
            load_ffn(q, 0, A["ffn1_wi_2"][0], A["ffn1_wo_2"][0], PLAIN_FULL, PLAIN_LAST)
            pw1 = A["conv_pw1_w_2"][0].rearrange("(c p) (h n) -> p c h n", p=P, h=2)
            for j in range(C):
                load_pair(Unit(q, K2_CONV + j), pw1[:, :, :, P * j:P * j + P])
            for j in range(4):
                load_cols(Unit(q, K2_PW2 + j), A["conv_pw2_w_2"][0], 256 * j)
            load_ffn(q, K2_FFN2, A["ffn2_wi_2"][0], A["ffn2_wo_2"][0], PLAIN_FULL, PLAIN_LAST)
            load_ffn(q, K2_L1, A["ffn1_wi_2"][1], A["ffn1_wo_2"][1], PLAIN_FULL, PLAIN_LAST)
            for j in range(6):
                load_cols(Unit(q, K2_Q + j), A["attn_w_qkv_2"][0], 256 * j)
            for j in range(4):
                load_cols(Unit(q, K2_WO + j), A["attn_w_o_2"][0], 256 * j)
            load_ffn(q, K2_FFN4, A["ffn2_wi_2"][1], A["ffn2_wo_2"][1], PLAIN_FULL, PLAIN_LAST)
            for n in range(2):
                sp.wait_ge(out_copied, 2 * (n + 1))
                sp.dma_start(out[0, n * P:(n + 1) * P, :], otok[:, n, :]).then_inc(stored, 16)
            sp.wait_ge(stored, 32)

        @block.gpsimd
        def _(pool):
            nc.gpsimd.memset(wgate[:], 0.0).then_inc(zeroed, 1)

        @block.tensor
        def _(pe):
            pe.sem_inc(mm_done, 4)
            pe.sem_inc(rg_mm, 1)
            pe.sem_inc(f_mm, 1)

            def out_of(u, t, n):
                return bank(u, t, n) if n == T else two(bank(u, t))

            def linear(u, xh, xl, n, kc_n=C, ready=None, tiles=(0, 1)):
                for t in tiles:
                    pe.wait_ge(lo_done, u.lo_done(t))
                    if t == 0:
                        pe.wait_ge(banks_free[u.par], u.banks_free())
                    for kc in range(kc_n):
                        if ready is not None and t == 0:
                            ready(kc)
                        w = slice(P * t, P * t + P)
                        o = out_of(u, t, n)
                        nc.tensor.matmul(o, wh[:, u.par, kc, w], xh(kc), start=(kc == 0), stop=False)
                        nc.tensor.matmul(o, wh[:, u.par, kc, w], xl(kc), start=False, stop=False)
                        mm = nc.tensor.matmul(o, wl[:, u.par, kc, w], xh(kc), start=False, stop=(kc == kc_n - 1))
                    mm.then_inc(mm_done, 1)

            def part(buf, n, s=0):
                if n == T:
                    return lambda kc: buf[:, s, kc, :]
                return lambda kc: buf[:, 0:2, kc, :]

            def h_ready(norm):
                return lambda kc: pe.wait_ge(h_done, norm * C + (kc + 1))

            def norm_sums(norm, n):
                for kc in range(C):
                    pe.wait_ge(sq_done, norm * C + (kc + 1))
                    nc.tensor.matmul(ps[:, 4, 0:n], ones[:], Tt[:, kc % 2, 0:n], start=(kc == 0),
                                     stop=(kc == C - 1)).then_inc(ss_done, 1)

            def modulation(u):
                for t in range(2):
                    pe.wait_ge(lo_done, u.lo_done(t))
                    if t == 0:
                        pe.wait_ge(banks_free[u.par], u.banks_free())
                    for kc in range(C):
                        w = slice(P * t, P * t + P)
                        nc.tensor.matmul(bank(u, t, 4), wh[:, u.par, kc, w], cs[:, kc, :], start=(kc == 0), stop=False)
                        mm = nc.tensor.matmul(bank(u, t, 4), wl[:, u.par, kc, w], cs[:, kc, :], start=False,
                                              stop=(kc == C - 1))
                    mm.then_inc(mm_done, 1)

            def ffn(q, k, fi, hn, n, order, last):
                for g, units in groups_of(pe, q, k, order, last):
                    held = 8 if not isinstance(g, int) else GROUPS[2]
                    for kind, i, u in units:
                        if kind == "G":
                            linear(u, part(Hh, n), part(Hl, n), n, ready=h_ready(hn) if i == 0 else None)
                        elif kind == "O":
                            done = fi * FC + g * 8

                            def ready(kc, done=done):
                                pe.wait_ge(f_done, done + (kc + 1))
                            linear(u, part(Fh, n), part(Fl, n), n, held, ready if i == 0 else None)
                        else:
                            modulation(u)

            pe.wait_ge(small_in, 48)
            pe.wait_ge(ones_there, 1)
            pe.wait_ge(par_in, 16 * PAR_LOADS)
            for i, n in enumerate(PAR_ROWS):
                mm = nc.tensor.transpose(ps[:, i // 4, (i % 4) * P:(i % 4) * P + n], prow[0:n, i, :],
                                         ident[0:n, 0:n])
            mm.then_inc(turned, 1)
            nc.tensor.matmul(ps[:, 7, 0:QH], ones[0:1, :], tiny[0:1, 48:64], start=True, stop=True) \
                .then_inc(sink_mm, 1)
            def turn_tokens(src, bank0):
                for b in range(4):
                    for i in range(4):
                        mm = nc.tensor.transpose(ps[:, bank0 + b, i * P:(i + 1) * P],
                                                 src[:, i % 2, (2 * b + i // 2) * P:(2 * b + i // 2 + 1) * P], ident)
                    mm.then_inc(turned, 1)

            pe.wait_ge(tok_in, 16)
            turn_tokens(xtok, 2)
            pe.wait_ge(c_there, 1)

            with pe.Fori(0, DEPTH) as l:
                q = l * Q_LAYER
                norm_sums(l * 4, T)
                ffn(q, 0, l * 2, l * 4, T, FULL_GROUP, LAST_GROUP)

                k = K_MIX
                norm_sums(l * 4 + 1, T)
                for j in range(8):
                    linear(Unit(q, k + j), part(Hh, T), part(Hl, T), T, ready=h_ready(l * 4 + 1) if j == 0 else None)
                pe.wait_ge(wf_in, l * 16 + 16)
                for kc in range(C):
                    nc.tensor.matmul(ps[0:HEADS, 4, 0:T], wf[:, kc, :], Hh[:, 0, kc, :].bitcast(F32),
                                     start=(kc == 0), stop=False)
                    mm = nc.tensor.matmul(ps[0:HEADS, 4, 0:T], wf[:, kc, :], Hl[:, 0, kc, :].bitcast(F32),
                                          start=False, stop=(kc == C - 1))
                mm.then_inc(f_mm, 1)

                def qk_sums(idx):
                    pe.wait_ge(qk_sq, l * 8 + (idx + 1))
                    for t in range(2):
                        r = (idx % 2) * HEADS + 2 * (idx // 2) + t
                        mm = nc.tensor.matmul(ps[0:2 * HEADS, 5, 0:T], co[:, CO_PICK + 15 - r:CO_PICK + 31 - r],
                                              Tt[:, idx % 2, t * T:(t + 1) * T], start=(idx == 0 and t == 0),
                                              stop=(idx == 7 and t == 1), skip_group_check=True)
                    mm.then_inc(qk_ss, 1)

                def gates(j):
                    rx = Unit(q, k + j // 2)
                    pe.wait_ge(banks_free[rx.par], rx.read_out())
                    if j == 0:
                        pe.wait_ge(wgate_in, l * 64 + 64)
                    if j >= 2:
                        pe.wait_ge(rg_tanh, l * 8 + (j - 1))
                    for g in range(2):
                        mm = nc.tensor.matmul(ps[:, 6 + j % 2, g * T:(g + 1) * T], wgate[:, g, j, :], Xc[:, j, :],
                                              start=True, stop=True)
                    mm.then_inc(rg_mm, 1)

                for i in range(12):
                    u = Unit(q, k + 8 + i)
                    hp, what = i // 3, i % 3
                    if what < 2:
                        gates(2 * hp + what)
                        linear(u, part(Hh, T), part(Hl, T), T)
                        if what == 1:
                            qk_sums(2 * hp)
                    else:
                        for t in range(2):
                            pe.wait_ge(lo_done, u.lo_done(1))
                            if t == 0:
                                pe.wait_ge(banks_free[u.par], u.banks_free())
                            tok = slice(t * P, t * P + P)
                            for kc in range(C):
                                o = bank(u, t, T)
                                nc.tensor.matmul(o, Hh[:, 0, kc, tok], wh[:, u.par, kc, :], start=(kc == 0), stop=False)
                                nc.tensor.matmul(o, Hl[:, 0, kc, tok], wh[:, u.par, kc, :], start=False, stop=False)
                                mm = nc.tensor.matmul(o, Hh[:, 0, kc, tok], wl[:, u.par, kc, :], start=False,
                                                      stop=(kc == C - 1))
                        mm.then_inc(mm_done, 2)
                        qk_sums(2 * hp + 1)

                def turn_probs(h):
                    pe.wait_ge(pn_done, l * HEADS + (h + 1))
                    for b in range(3):
                        mm = nc.tensor.transpose(ps[:, 6, b * P:(b + 1) * P], scores[:, b * P:(b + 1) * P], ident)
                    mm.then_inc(tr_done, 1)

                def spread(h):
                    pe.wait_ge(rm_done, l * HEADS + (h + 1))
                    nc.tensor.matmul(ps[:, 4, :], ones[0:2 * HEADS, :], rmask, start=True, stop=True) \
                        .then_inc(bc_done, 1)

                def head_scores(h):
                    pe.wait_ge(qkn_done, l * HEADS + (h + 1))
                    for b in range(2):
                        o = ps[:, 5, b * P:b * P + (b + 1) * P]
                        nc.tensor.matmul(o, Qb[:, h, b * P:(b + 1) * P], Kb[:, h, 0:(b + 1) * P], start=True, stop=False)
                        mm = nc.tensor.matmul(o, ones[0:HEADS, :], dmask[:, 0:(b + 1) * P], start=False, stop=True)
                    mm.then_inc(s_done, 1)

                def head_values(h):
                    pe.wait_ge(pt_done, l * HEADS + (h + 1))
                    if h >= 1:
                        pe.wait_ge(o_done, l * HEADS + h)
                    v = slice(h * P, h * P + P)
                    nc.tensor.matmul(ps[:, 7, 0:T], Vb[:, 0, v], probsT[:, 0:T], start=True, stop=False)
                    nc.tensor.matmul(ps[:, 7, P:T], Vb[:, 1, v], probsT[:, T:T + P], start=False, stop=True) \
                        .then_inc(pv_done, 1)

                def ya_ready(kc):
                    pe.wait_ge(ya_done, l * C + (kc + 1))

                for st in range(HEADS):
                    u = Unit(q, k + 20 + st)
                    src = (part(Hh, T), part(Hl, T)) if st < 4 else (part(Fh, T), part(Fl, T))
                    if st >= 1:
                        turn_probs(st - 1)
                    spread(st)
                    linear(u, *src, T, ready=ya_ready if st == 4 else None, tiles=(0,))
                    if st >= 1:
                        head_values(st - 1)
                    head_scores(st)
                    linear(u, *src, T, tiles=(1,))

                def o_ready(kc):
                    pe.wait_ge(o_done, l * HEADS + (kc + 1))

                for j in range(4):
                    u = Unit(q, k + 28 + 2 * j)
                    if j == 0:
                        turn_probs(HEADS - 1)
                    linear(u, part(Hh, T), part(Hl, T), T, tiles=(0,))
                    if j == 0:
                        head_values(HEADS - 1)
                    linear(u, part(Hh, T), part(Hl, T), T, tiles=(1,))
                    linear(u.later(1), part(Fh, T, 1), part(Fl, T, 1), T, ready=o_ready if j == 0 else None)

                def m_ready(kc):
                    pe.wait_ge(m_done, l * 4 + (kc // 2 + 1))

                for j in range(4):
                    linear(Unit(q, k + 36 + j), part(Hh, T, 1), part(Hl, T, 1), T, ready=m_ready if j == 0 else None)

                norm_sums(l * 4 + 2, T)
                ffn(q, K_FFN2, l * 2 + 1, l * 4 + 2, T, FULL_GROUP, LAST_GROUP)

                pe.wait_ge(p_in, l * 16 + 16)
                for i in range(4):
                    mm = nc.tensor.transpose(ps[:, 7, i * P:(i + 1) * P], ptok[:, i % 2, (i // 2) * P:(i // 2 + 1) * P],
                                             ident)
                mm.then_inc(p_turned, 1)
                norm_sums(l * 4 + 3, T)
                for j in range(4):
                    u = Unit(q, K_PLE + 2 * j)
                    linear(u, part(Hh, T), part(Hl, T), T, ready=h_ready(l * 4 + 3) if j == 0 else None)
                    if j == 0:
                        pe.wait_ge(p_there, l + 1)
                    linear(u.later(1), part(Fh, T, 1), part(Fl, T, 1), T, PLE // P)

            q = Q_SECOND
            norm_sums(8, T)
            pe.wait_ge(std_done, 9)
            pe.wait_ge(tok_in, 32)
            turn_tokens(ctok, 4)
            pe.wait_ge(turned_out, 8)
            norm_sums(9, 512)
            ffn(q, 0, 4, 8, 512, PLAIN_FULL, PLAIN_LAST)
            norm_sums(10, 512)
            for j in range(C):
                linear(Unit(q, K2_CONV + j), part(Hh, 512), part(Hl, 512), 512, ready=h_ready(9) if j == 0 else None)
            conv_x, conv_c = Qb, Kb
            for kc in range(C):
                pe.wait_ge(cv_done, kc + 1)
                nc.tensor.matmul(ps[:, 4, 0:T], ones[:], conv_x[:, kc, :], start=(kc == 0), stop=(kc == C - 1),
                                 skip_group_check=True)
                mm = nc.tensor.matmul(ps[:, 5, 0:T], ones[:], conv_c[:, kc, :], start=(kc == 0), stop=(kc == C - 1),
                                      skip_group_check=True)
            mm.then_inc(mu_mm, 1)
            for kc in range(C):
                pe.wait_ge(csq_done, kc + 1)
                nc.tensor.matmul(ps[:, 6, :], ones[:], Tt[:, kc % 2, :], start=(kc == 0), stop=(kc == C - 1)) \
                    .then_inc(var_mm, 1)

            def z_ready(kc):
                pe.wait_ge(z_there, kc + 1)

            for j in range(4):
                linear(Unit(q, K2_PW2 + j), part(Fh, 512), part(Fl, 512), 512, ready=z_ready if j == 0 else None)
            norm_sums(11, 512)
            ffn(q, K2_FFN2, 5, 10, 512, PLAIN_FULL, PLAIN_LAST)
            norm_sums(12, 512)
            ffn(q, K2_L1, 6, 11, 512, PLAIN_FULL, PLAIN_LAST)
            norm_sums(13, 512)
            pe.wait_ge(ro_in, 16)

            def rotate(i, src):
                ue = Unit(q, K2_Q + i)
                pe.wait_ge(banks_free[ue.par], ue.read_out())
                if i >= 2:
                    pe.wait_ge(rot_done, i - 1)
                nc.tensor.matmul(two(ps[:, 4 + i % 2, :]), ro[:, RO_ROT:RO_ROT + P], src, start=True, stop=True) \
                    .then_inc(rot_mm, 1)

            def q_tiles(i):
                return Qb[:, 2 * i:2 * i + 2, :]

            for j in range(4):
                linear(Unit(q, K2_Q + j), part(Hh, T), part(Hl, T), T, ready=h_ready(12) if j == 0 else None)
                if j >= 1:
                    rotate(j - 1, q_tiles(j - 1))
            u = Unit(q, K2_KV)
            linear(u, part(Hh, 512), part(Hl, 512), 512)
            rotate(3, q_tiles(3))
            u = u.later(1)
            pe.wait_ge(lo_done, u.lo_done(1))
            pe.wait_ge(banks_free[u.par], u.banks_free())
            for t in range(4):
                tok = slice((t % 2) * P, (t % 2) * P + P)
                o = ps[:, 2 * u.par + t // 2, (t % 2) * T:(t % 2 + 1) * T]
                for kc in range(C):
                    nc.tensor.matmul(o, Hh[:, t // 2, kc, tok], wh[:, u.par, kc, :], start=(kc == 0), stop=False)
                    nc.tensor.matmul(o, Hl[:, t // 2, kc, tok], wh[:, u.par, kc, :], start=False, stop=False)
                    mm = nc.tensor.matmul(o, Hh[:, t // 2, kc, tok], wl[:, u.par, kc, :], start=False,
                                          stop=(kc == C - 1))
            mm.then_inc(mm_done, 2)
            rotate(4, kraw[:, :, 0:T])
            pe.wait_ge(rot_done, 5)
            for kv in range(KVH):
                if kv >= 2:
                    pe.wait_ge(dup_done, kv - 1)
                nc.tensor.matmul(ps[:, 6 + kv % 2, :], ro[:, RO_DUP + P * (kv % 2):RO_DUP + P * (kv % 2 + 1)],
                                 kraw[:, kv // 2, :], start=True, stop=True).then_inc(dup_mm, 1)
            pe.wait_ge(dup_done, KVH)

            def scores2(h):
                half_p = slice(HD * (h % 2), HD * (h % 2) + HD)
                if h >= 2:
                    pe.wait_ge(e2_done, 2 * (h - 1))
                for b in range(2):
                    nc.tensor.matmul(ps[:, 2 * (h % 2) + b, :], Qb[half_p, h // 2, b * P:(b + 1) * P],
                                     kdup[half_p, h // 4, :], start=True, stop=True).then_inc(s2_done, 1)

            for back in (1, 2):
                ue = Unit(q, K2_WO - back)
                pe.wait_ge(banks_free[ue.par], ue.read_out())
            scores2(0)
            for h in range(QH):
                if h + 1 < QH:
                    scores2(h + 1)
                pe.wait_ge(pn2_done, 2 * h + 2)
                if h >= 1:
                    pe.wait_ge(pt2_done, 2 * h)
                for b in range(2):
                    for kb in range(4):
                        mm = nc.tensor.transpose(ps[:, 4 + kb // 2, (kb % 2) * T + b * P:(kb % 2) * T + (b + 1) * P],
                                                 Pp[:, b, kb * P:(kb + 1) * P], ident)
                mm.then_inc(tr2_done, 1)
                pe.wait_ge(pt2_done, 2 * h + 2)
                if h % 2 == 0 and h >= 4:
                    pe.wait_ge(o2_done, h // 2 - 1)
                for kb in range(4):
                    o = ps[HD * (h % 2):HD * (h % 2) + HD, 6 + (h // 2) % 2, 0:T]
                    mm = nc.tensor.matmul(o, v2[:, kb, HD * (h // 4):HD * (h // 4) + HD],
                                          two(Tt[:, kb // 2, :])[:, kb % 2, :], start=(kb == 0), stop=(kb == 3))
                mm.then_inc(pv2_done, 1)

            def o2_ready(kc):
                pe.wait_ge(o2_done, kc + 1)

            for j in range(4):
                linear(Unit(q, K2_WO + j), part(Fh, T), part(Fl, T), T, ready=o2_ready if j == 0 else None)
            norm_sums(14, T)
            ffn(q, K2_FFN4, 7, 13, T, PLAIN_FULL, PLAIN_LAST)
            norm_sums(15, T)
            for n in range(2):
                for b in range(2):
                    for i in range(4):
                        kc = 4 * b + i
                        pe.wait_ge(final_done, kc + 1)
                        mm = nc.tensor.transpose(ps[:, 4 + 2 * n + b, i * P:(i + 1) * P],
                                                 Xx[:, kc, n * P:(n + 1) * P], ident)
                    mm.then_inc(out_mm, 1)

        @block.scalar
        def _(act):
            def hi(u, t):
                if u.last():
                    return
                if t == 0:
                    act.wait_ge(raw_full[u.slot], u.raw_full())
                act.wait_ge(mm_done, u.split_free(t))
                w = slice(P * t, P * t + P)
                nc.scalar.activation(wh[:, u.par, :, w], raw[:, u.slot, :, w], ACT.Copy).then_inc(hi_done, 1)

            def tanh_table():
                nc.scalar.activation(eps[:, 1:2], eps[:, 0:1], ACT.Tanh)

            def stream(u):
                hi(u.later(2), 0)
                hi(u.later(2), 1)

            def norm(norm_i, n, u, with_h=None, shift=None):
                if u is not None:
                    act.wait_ge(banks_free[u.par], u.read_out())
                for kc in range(C):
                    if kc >= 2:
                        act.wait_ge(ss_done, norm_i * C + (kc - 1))
                    ins = nc.scalar.activation(Tt[:, kc % 2, 0:T], Xx[:, kc, :], ACT.Square)
                    if n > T:
                        ins = nc.scalar.activation(Tt[:, kc % 2, T:n], Xc[:, kc, :], ACT.Square)
                    ins.then_inc(sq_done, 1)
                act.wait_ge(ss_done, norm_i * C + C)
                nc.scalar.activation(Rr[:, 0:n], ps[:, 4, 0:n], ACT.Sqrt, bias=eps[:, 0:1], scale=1.0 / D) \
                    .then_inc(std_done, 1)
                tanh_table()
                if with_h is None:
                    return
                for kc in range(C):
                    act.wait_ge(hp_done, with_h * C + (kc + 1))
                    for s in range(n // T):
                        src = Pp[:, kc % 2, s * T:(s + 1) * T]
                        if shift is None:
                            ins = nc.scalar.activation(Hh[:, s, kc, :], src, ACT.Copy)
                        else:
                            ins = nc.scalar.activation(Hh[:, s, kc, :], src, ACT.Identity, bias=shift(kc, s))
                    ins.then_inc(hh_done, 1)

            def ffn(q, k, fi, n, order, last):
                for g, units in groups_of(act, q, k, order, last):
                    for kind, i, u in units:
                        hi(u.later(2), 0)
                        if kind == "G":
                            act.wait_ge(mm_done, u.mm_done(0))
                            nc.scalar.activation(Tt[:, u.par, 0:n], bank(u, 0, n), ACT.Tanh, scale=0.5) \
                                .then_inc(tanh_done, 1)
                        hi(u.later(2), 1)
                        if kind == "G":
                            act.wait_ge(banks_free[u.par], u.read_out())
                            dst = Fh[:, 0, i, :] if n == T else Fh[:, 0:2, i, :]
                            src = Pp[:, u.par, 0:n] if n == T else two(Pp[:, u.par, :])
                            nc.scalar.activation(dst, src, ACT.Copy).then_inc(fh_done, 1)

            act.wait_ge(eps_there, 1)
            act.wait_ge(par_there, 1)
            nc.scalar.activation(tiny[:, 0:16], tiny[:, 16:32], ACT.Exp, scale=-1.0).then_inc(lam_exp, 1)
            nc.scalar.activation(tiny[:, 32:48], par[:, 2, R_C:R_C + 16], ACT.Tanh, scale=0.5).then_inc(c_tanh, 1)
            act.wait_ge(c_prod, 1)
            nc.scalar.activation(cs[:, :, 0:2], Ss[:, 0:16].rearrange("p (s c) -> p c s", s=2), ACT.Copy) \
                .then_inc(c_hi, 1)
            for n in range(2):
                for t in range(2):
                    hi(Unit(0, n), t)
            act.wait_ge(x_there, 1)

            with act.Fori(0, DEPTH) as l:
                q = l * Q_LAYER
                act.wait_ge(cur_there, l + 1)
                norm(l * 4, T, Unit(q, -1), l * 4)
                ffn(q, 0, l * 2, T, FULL_GROUP, LAST_GROUP)

                k = K_MIX
                norm(l * 4 + 1, T, Unit(q, k - 1 - 1), l * 4 + 1)
                for j in range(4):
                    stream(Unit(q, k + j))
                for j in range(4):
                    u = Unit(q, k + 4 + j)
                    hi(u.later(2), 0)
                    act.wait_ge(mm_done, u.mm_done(1))
                    nc.scalar.activation(two(Tt[:, u.par, :]), pair(u), ACT.Square).then_inc(gelu_sq, 1)
                    hi(u.later(2), 1)
                    act.wait_ge(gelu_arg, l * 4 + (j + 1))
                    nc.scalar.activation(Tt[:, u.par, :], Pp[:, u.par, :], ACT.Tanh, scale=GELU_C) \
                        .then_inc(gelu_tanh, 1)
                for i in range(12):
                    u = Unit(q, k + 8 + i)
                    hp, what = i // 3, i % 3
                    if what < 2:
                        j = 2 * hp + what
                        act.wait_ge(rg_mm, l * C + (j + 2))
                        if j >= 1:
                            act.wait_ge(la_done, l * C + j)
                        nc.scalar.activation(Rr[:, 0:T], ps[:, 6 + j % 2, 0:T], ACT.Tanh, scale=0.5,
                                             bias=half[:, R_BA + j:R_BA + j + 1])
                        nc.scalar.activation(Rr[:, T:2 * T], ps[:, 6 + j % 2, T:2 * T], ACT.Tanh, scale=0.5,
                                             bias=half[:, R_BX + j:R_BX + j + 1]).then_inc(rg_tanh, 1)
                        hi(u.later(2), 0)
                        act.wait_ge(la_done, l * C + (j + 1))
                        nc.scalar.activation(decay[:, j, :], Ss[:, 0:T], ACT.Exp)
                        nc.scalar.activation(Pp[:, j % 2, 0:T], Ss[:, 0:T], ACT.Tanh).then_inc(rg_exp, 1)
                        act.wait_ge(mm_done, u.mm_done(1))
                        if j >= 2:
                            act.wait_ge(qk_ss, l * 8 + (j - 1))
                        nc.scalar.activation(two(Tt[:, j % 2, :]), pair(u), ACT.Square).then_inc(qk_sq, 1)
                        hi(u.later(2), 1)
                    else:
                        hi(u.later(2), 0)
                        if hp == 0:
                            act.wait_ge(f_in, l + 1)
                            nc.scalar.activation(Ss[0:HEADS, T:2 * T], Ss[0:HEADS, 0:T], ACT.Abs).then_inc(f_abs, 1)
                            act.wait_ge(f_abs, l * 2 + 1)
                            nc.scalar.activation(Ss[0:HEADS, T:2 * T], Ss[0:HEADS, T:2 * T], ACT.Exp, scale=-1.0) \
                                .then_inc(f_abs, 1)
                        hi(u.later(2), 1)
                act.wait_ge(qk_ss, l * 8 + 8)
                nc.scalar.activation(rqk[:], ps[0:2 * HEADS, 5, 0:T], ACT.Sqrt, bias=eps[0:2 * HEADS, 0:1],
                                     scale=1.0 / P).then_inc(qk_std, 1)
                act.wait_ge(keep_done, l * C + C)
                nc.scalar.activation(keep[:], keep[:], ACT.Sqrt, scale=-1.0).then_inc(root_done, 1)
                tanh_table()

                def copy_probs(h):
                    act.wait_ge(tr_done, l * HEADS + (h + 1))
                    nc.scalar.activation(probsT, ps[:, 6, 0:384], ACT.Copy).then_inc(pt_done, 1)

                def head_out(h):
                    act.wait_ge(pv_done, l * HEADS + (h + 1))
                    nc.scalar.activation(Fh[:, 1, h, :], ps[:, 7, 0:T], ACT.Copy).then_inc(oh_done, 1)

                def head_exp(h):
                    act.wait_ge(nmax_done, l * HEADS + (h + 1))
                    for b, sl in enumerate((slice(0, P), slice(P, 3 * P))):
                        ins = nc.scalar.activation(scores[:, sl], scores[:, sl], ACT.Exp, bias=tiny[:, b:b + 1],
                                                   accum_out=tiny[:, 2 + b:3 + b])
                    ins.then_inc(exp_done, 1)

                for st in range(HEADS):
                    u = Unit(q, k + 20 + st)
                    if st >= 1:
                        copy_probs(st - 1)
                    hi(u.later(2), 0)
                    if st >= 1:
                        head_out(st - 1)
                    head_exp(st)
                    if st < 4:
                        for j in (2 * st, 2 * st + 1):
                            act.wait_ge(y_done, l * C + (j + 1))
                            nc.scalar.activation(Fh[:, 0, j, :], Pp[:, j % 2, T:2 * T], ACT.Copy).then_inc(yh_done, 1)
                    hi(u.later(2), 1)
                    if st < 4:
                        act.wait_ge(mm_done, u.mm_done(1))
                        for t in range(2):
                            r = R_MERGE + 2 * st + t
                            ins = nc.scalar.activation(gateA[:, 2 * st + t, :], bank(u, t, T), ACT.Tanh, scale=0.5,
                                                       bias=half[:, r:r + 1])
                        ins.then_inc(banks_free[u.par], 1)
                for j in range(4):
                    u = Unit(q, k + 28 + 2 * j)
                    if j == 0:
                        copy_probs(HEADS - 1)
                    hi(u.later(2), 0)
                    if j == 0:
                        head_out(HEADS - 1)
                    hi(u.later(2), 1)
                    act.wait_ge(mm_done, u.mm_done(1))
                    for t in range(2):
                        r = R_MERGE + C + 2 * j + t
                        ins = nc.scalar.activation(Tt[:, j % 2, t * T:(t + 1) * T], bank(u, t, T), ACT.Tanh, scale=0.5,
                                                   bias=half[:, r:r + 1])
                    ins.then_inc(banks_free[u.par], 1)
                    u = u.later(1)
                    hi(u.later(2), 0)
                    hi(u.later(2), 1)
                    act.wait_ge(mp_done, l * 4 + (j + 1))
                    nc.scalar.activation(Hh[:, 1, 2 * j:2 * j + 2, :], two(Pp[:, j % 2, :]), ACT.Copy) \
                        .then_inc(mh_done, 1)
                for j in range(4):
                    stream(Unit(q, k + 36 + j))

                norm(l * 4 + 2, T, Unit(q, K_FFN2 - 1), l * 4 + 2)
                ffn(q, K_FFN2, l * 2 + 1, T, FULL_GROUP, LAST_GROUP)
                act.wait_ge(p_turned, l + 1)
                nc.scalar.activation(Fh[:, 1, 0:2, :], two(ps[:, 7, :]), ACT.Copy).then_inc(pth_done, 1)
                norm(l * 4 + 3, T, Unit(q, K_PLE - 2), l * 4 + 3)
                for j in range(4):
                    u = Unit(q, K_PLE + 2 * j)
                    hi(u.later(2), 0)
                    hi(u.later(2), 1)
                    act.wait_ge(mm_done, u.mm_done(1))
                    for t in range(2):
                        r = R_PLEB + 2 * j + t
                        ins = nc.scalar.activation(Tt[:, j % 2, t * T:(t + 1) * T], bank(u, t, T), ACT.Tanh, scale=0.5,
                                                   bias=half[:, r:r + 1])
                    ins.then_inc(banks_free[u.par], 1)
                    stream(u.later(1))

            q = Q_SECOND

            def shift(l, i):
                return lambda kc, s: MOD[:, l, (3 * i) * C + kc, s:s + 1]

            norm(8, T, Unit(q, -1))
            act.wait_ge(x_normed, 1)
            act.wait_ge(mod_there, 1)
            norm(9, 512, None, 8, shift(0, 0))
            ffn(q, 0, 4, 512, PLAIN_FULL, PLAIN_LAST)
            norm(10, 512, Unit(q, K2_CONV - 1), 9, shift(0, 1))
            for j in range(C):
                u = Unit(q, K2_CONV + j)
                hi(u.later(2), 0)
                act.wait_ge(mm_done, u.mm_done(1))
                nc.scalar.activation(Tt[:, u.par, :], bank(u, 1), ACT.Tanh, scale=0.5, bias=tiny[:, 40 + j:41 + j]) \
                    .then_inc(cv_tanh, 1)
                hi(u.later(2), 1)
            for kc in range(C):
                act.wait_ge(cen_done, kc + 1)
                if kc >= 2:
                    act.wait_ge(var_mm, kc - 1)
                nc.scalar.activation(Tt[:, kc % 2, 0:T], Qb[:, kc, :], ACT.Square)
                nc.scalar.activation(Tt[:, kc % 2, T:512], Kb[:, kc, :], ACT.Square).then_inc(csq_done, 1)
            act.wait_ge(var_mm, C)
            nc.scalar.activation(Rr[:], ps[:, 6, :], ACT.Sqrt, bias=eps[:, 0:1], scale=1.0 / D).then_inc(cstd_done, 1)
            tanh_table()
            for kc in range(C):
                act.wait_ge(z_done, kc + 1)
                if kc >= 2:
                    act.wait_ge(zp_done, kc - 1)
                nc.scalar.activation(Tt[:, kc % 2, 0:T], Qb[:, kc, :], ACT.Tanh, scale=tiny[:, kc:kc + 1],
                                     bias=tiny[:, 8 + kc:9 + kc])
                nc.scalar.activation(Tt[:, kc % 2, T:512], Kb[:, kc, :], ACT.Tanh, scale=tiny[:, kc:kc + 1],
                                     bias=tiny[:, 8 + kc:9 + kc]).then_inc(zt_done, 1)
                act.wait_ge(zp_done, kc + 1)
                nc.scalar.activation(Fh[:, 0:2, kc, :], two(Pp[:, kc % 2, :]), ACT.Copy).then_inc(zh_done, 1)
            for j in range(4):
                stream(Unit(q, K2_PW2 + j))
            norm(11, 512, Unit(q, K2_FFN2 - 1), 10, shift(0, 2))
            ffn(q, K2_FFN2, 5, 512, PLAIN_FULL, PLAIN_LAST)
            act.wait_ge(mod_there, 2)
            norm(12, 512, Unit(q, K2_L1 - 1), 11, shift(1, 0))
            ffn(q, K2_L1, 6, 512, PLAIN_FULL, PLAIN_LAST)
            norm(13, 512, Unit(q, K2_Q - 1), 12, shift(1, 1))
            for j in range(6):
                stream(Unit(q, K2_Q + j))
            for kv in range(KVH):
                act.wait_ge(dup_mm, kv + 1)
                nc.scalar.activation(kdup[:, kv, :], ps[:, 6 + kv % 2, :], ACT.Copy).then_inc(dup_done, 1)

            def head2_out(tile):
                act.wait_ge(pv2_done, 2 * tile + 2)
                nc.scalar.activation(Fh[:, 0, tile, :], ps[:, 6 + tile % 2, 0:T], ACT.Copy).then_inc(oh2_done, 1)

            for h in range(QH):
                for b in range(2):
                    act.wait_ge(nm2_done, 2 * h + b + 1)
                    if h >= 1 and b == 0:
                        act.wait_ge(tr2_done, h)
                    nc.scalar.activation(tiny[:, 4 + b:5 + b], tiny[:, 16 + h:17 + h], ACT.Exp,
                                         bias=tiny[:, b:b + 1])
                    nc.scalar.activation(Pp[:, b, :], ps[:, 2 * (h % 2) + b, :], ACT.Exp, bias=tiny[:, b:b + 1],
                                         accum_out=tiny[:, 2 + b:3 + b]).then_inc(e2_done, 1)
                act.wait_ge(tr2_done, h + 1)
                for i in range(2):
                    if h >= 1:
                        act.wait_ge(pv2_done, h)
                    nc.scalar.activation(Tt[:, i, :], ps[:, 4 + i, :], ACT.Copy).then_inc(pt2_done, 1)
                if h % 2 == 0 and h >= 2:
                    head2_out(h // 2 - 1)
            head2_out(QH // 2 - 1)
            for j in range(4):
                stream(Unit(q, K2_WO + j))
            norm(14, T, Unit(q, K2_FFN4 - 1), 13, shift(1, 2))
            ffn(q, K2_FFN4, 7, T, PLAIN_FULL, PLAIN_LAST)
            norm(15, T, Unit(q, K2_END - 1))
            for n in range(2):
                for b in range(2):
                    act.wait_ge(out_mm, 2 * n + b + 1)
                    nc.scalar.activation(otok[:, n, 512 * b:512 * (b + 1)], ps[:, 4 + 2 * n + b, :], ACT.Copy) \
                        .then_inc(out_copied, 1)

        @block.vector
        def _(dve):
            dve.sem_inc(lo_done, 8)
            dve.sem_inc(banks_free[0], 1)
            dve.sem_inc(banks_free[1], 1)
            V = nc.vector

            def stt(o, in0, scalar, in1, op0, op1):
                return V.scalar_tensor_tensor(out=o, in0=in0, scalar=scalar, in1=in1, op0=op0, op1=op1)

            def lo(u, t):
                if u.last():
                    return
                dve.wait_ge(hi_done, u.hi_done(t))
                w = slice(P * t, P * t + P)
                V.tensor_tensor(wl[:, u.par, :, w], raw[:, u.slot, :, w], wh[:, u.par, :, w].bitcast(F32),
                                ALU.subtract).then_inc(lo_done, 1)

            def stream(u):
                lo(u.later(2), 0)
                lo(u.later(2), 1)

            def rms(norm_i, n):
                dve.wait_ge(std_done, norm_i + 1)
                V.reciprocal(Rr[:, 0:n], Rr[:, 0:n])
                dve.drain()

            def norm(norm_i, n, hn, gain, shift=None):
                rms(norm_i, n)

                def product(kc):
                    for s in range(n // T):
                        x = (Xx, Xc)[s]
                        ins = stt(Pp[:, kc % 2, s * T:(s + 1) * T], x[:, kc, :], gain(kc, s), Rr[:, s * T:(s + 1) * T],
                                  ALU.mult, ALU.mult)
                    ins.then_inc(hp_done, 1)

                product(0)
                product(1)
                for kc in range(C):
                    dve.wait_ge(hh_done, hn * C + (kc + 1))
                    for s in range(n // T):
                        p, h = Pp[:, kc % 2, s * T:(s + 1) * T], Hh[:, s, kc, :].bitcast(F32)
                        if shift is None:
                            ins = V.tensor_tensor(Hl[:, s, kc, :], p, h, ALU.subtract)
                        else:
                            ins = stt(Hl[:, s, kc, :], p, shift(kc, s), h, ALU.add, ALU.subtract)
                    ins.then_inc(h_done, 1)
                    if kc + 2 < C:
                        dve.drain()
                        product(kc + 2)

            def modulation(u, l, idx, turn):
                lo(u.later(2), 0)
                dve.wait_ge(mm_done, u.mm_done(1))
                t2 = ps[:, 2 * u.par:2 * u.par + 2, :]
                tmp = tiny[:, 48 + 4 * turn:52 + 4 * turn].rearrange("p (t s) -> p t s", t=2)
                V.tensor_copy(tmp, t2[:, :, 0:2])
                dve.drain()
                V.tensor_tensor(MOD[:, bass.ds(l, 1), bass.ds(idx * 2, 2), :].rearrange("p l t s -> p (l t) s"),
                                t2[:, :, 2:4], tmp, ALU.add).then_inc(banks_free[u.par], 1)
                lo(u.later(2), 1)

            def ffn(q, k, fi, n, order, last, gate=None, ada=None):
                for g, units in groups_of(dve, q, k, order, last):
                    for kind, i, u in units:
                        if kind == "A":
                            modulation(u, ada[0], ada_index(ada[1], g, i), i % 2)
                            continue
                        lo(u.later(2), 0)
                        if kind == "G":
                            done = fi * FC + g * 8
                            dve.wait_ge(tanh_done, done + (i + 1))
                            stt(Ss[:, 0:n], Tt[:, u.par, 0:n], 1.0, bank(u, 0, n), ALU.add, ALU.mult)
                            dve.drain()
                            dve.wait_ge(mm_done, u.mm_done(1))
                            V.tensor_tensor(Pp[:, u.par, 0:n], Ss[:, 0:n], bank(u, 1, n), ALU.mult) \
                                .then_inc(banks_free[u.par], 1)
                        elif gate is None:
                            dve.wait_ge(mm_done, u.mm_done(1))
                            x = Xx[:, 2 * i:2 * i + 2, :]
                            stt(x, pair(u), 0.25, x, ALU.mult, ALU.add).then_inc(banks_free[u.par], 1)
                        else:
                            dve.wait_ge(mm_done, u.mm_done(1))
                            add_gated(u, i, n, gate)
                        lo(u.later(2), 1)
                        if kind == "G":
                            dve.wait_ge(fh_done, done + (i + 1))
                            if n == T:
                                o, p, h = Fl[:, 0, i, :], Pp[:, u.par, 0:n], Fh[:, 0, i, :]
                            else:
                                o, p, h = Fl[:, 0:2, i, :], two(Pp[:, u.par, :]), Fh[:, 0:2, i, :]
                            V.tensor_tensor(o, p, h.bitcast(F32), ALU.subtract).then_inc(f_done, 1)

            def add_gated(u, i, n, gate):
                for t in range(2):
                    kc = 2 * i + t
                    for s in range(n // T):
                        x = (Xx, Xc)[s][:, kc, :]
                        ins = stt(x, ps[:, 2 * u.par + t, s * T:(s + 1) * T], gate(kc, s), x, ALU.mult, ALU.add)
                ins.then_inc(banks_free[u.par], 1)

            def log1p(o, e, z2, acc):
                V.tensor_scalar(acc, e, 2.0, None, ALU.add)
                dve.drain()
                V.reciprocal(acc, acc)
                dve.drain()
                V.tensor_tensor(o, e, acc, ALU.mult)
                dve.drain()
                V.tensor_tensor(z2, o, o, ALU.mult)
                dve.drain()
                V.tensor_scalar(acc, z2, 2.0 / 17, None, ALU.mult)
                dve.drain()
                for j in (15, 13, 11, 9, 7, 5, 3):
                    stt(acc, acc, 2.0 / j, z2, ALU.add, ALU.mult)
                    dve.drain()
                stt(o, acc, 2.0, o, ALU.add, ALU.mult)
                dve.drain()

            V.memset(ones[:], 1.0)
            V.memset(eps[:], EPS).then_inc(eps_there, 1)
            dve.drain().then_inc(ones_there, 1)
            dve.wait_ge(turned, 1)
            for i, n in enumerate(PAR_ROWS):
                V.tensor_copy(par[:, i, 0:n], ps[:, i // 4, (i % 4) * P:(i % 4) * P + n])
            dve.wait_ge(sink_mm, 1)
            dve.drain()
            lam = par[:, 0:2, R_LAM:R_LAM + C]
            two8 = [x.rearrange("p (l c) -> p l c", l=2) for x in
                    (tiny[:, 0:16], tiny[:, 16:32], Ss[:, 16:32], Ss[:, 32:48], Ss[:, 48:64])]
            V.tensor_scalar(two8[2], lam, -1.0, None, ALU.mult)
            dve.drain()
            V.tensor_tensor(two8[1], lam, two8[2], ALU.max).then_inc(par_there, 1)
            dve.wait_ge(lam_exp, 1)
            log1p(two8[4], two8[0], two8[3], two8[1])
            stt(two8[4], two8[2], 0.0, two8[4], ALU.max, ALU.add)
            dve.drain()
            V.tensor_scalar(lam, two8[4], -4.0, None, ALU.mult)
            V.tensor_scalar(par[:, 0:2, R_QN:R_QN + 1], par[:, 0:2, R_QN:R_QN + 1], float(P) ** -0.5, None, ALU.mult)
            dve.wait_ge(c_tanh, 1)
            stt(Ss[:, 0:16], tiny[:, 32:48], 1.0, par[:, 2, R_C:R_C + 16], ALU.add, ALU.mult)
            dve.drain()
            V.tensor_scalar(Ss[:, 0:16], Ss[:, 0:16], 0.5, None, ALU.mult).then_inc(c_prod, 1)
            dve.wait_ge(c_hi, 1)
            V.tensor_tensor(cs[:, :, 2:4], Ss[:, 0:16].rearrange("p (s c) -> p c s", s=2), cs[:, :, 0:2].bitcast(F32),
                            ALU.subtract).then_inc(c_there, 1)
            V.tensor_copy(tiny[:, 16:32], ps[:, 7, 0:QH])
            for b in range(4):
                dve.wait_ge(turned, b + 2)
                V.tensor_copy(Xx[:, 2 * b:2 * b + 2, :], two(ps[:, 2 + b, :])).then_inc(turned_out, 1)
            dve.drain().then_inc(x_there, 1)
            for n in range(2):
                for t in range(2):
                    lo(Unit(0, n), t)

            def layer_gain(r):
                return lambda kc, s: cur[:, r + kc:r + kc + 1]

            with dve.Fori(0, DEPTH) as l:
                q = l * Q_LAYER
                V.tensor_copy(cur[:], par[:, bass.ds(l, 1), 0:R_LAYER].rearrange("p l f -> p (l f)"))
                V.tensor_copy(tiny[0:HEADS, 12:13], fb[:, bass.ds(l, 1)])
                dve.drain()
                V.tensor_scalar(half[:], cur[:], 0.5, None, ALU.mult).then_inc(cur_there, 1)
                norm(l * 4, T, l * 4, layer_gain(R_FFN1))
                ffn(q, 0, l * 2, T, FULL_GROUP, LAST_GROUP, ada=(l, 0))

                k = K_MIX
                norm(l * 4 + 1, T, l * 4 + 1, layer_gain(R_MIX))
                for j in range(4):
                    u = Unit(q, k + j)
                    lo(u.later(2), 0)
                    dve.wait_ge(mm_done, u.mm_done(1))
                    for s in range(4):
                        for t in range(2):
                            kc = 2 * j + t
                            tap = cur[:, R_CONV + 8 * (3 - s) + kc:R_CONV + 8 * (3 - s) + kc + 1]
                            if s == 0:
                                ins = V.tensor_scalar(Xc[:, kc, :], bank(u, t, T), tap,
                                                      cur[:, R_CONVB + kc:R_CONVB + kc + 1], ALU.mult, ALU.add)
                            else:
                                ins = stt(Xc[:, kc, s:T], bank(u, t, T - s), tap, Xc[:, kc, s:T], ALU.mult, ALU.add)
                        if s < 3:
                            dve.drain()
                    ins.then_inc(banks_free[u.par], 1)
                    lo(u.later(2), 1)
                for j in range(4):
                    u = Unit(q, k + 4 + j)
                    lo(u.later(2), 0)
                    dve.wait_ge(gelu_sq, l * 4 + (j + 1))
                    V.tensor_scalar(Ss[:], Tt[:, u.par, :], GELU_A, 1.0, ALU.mult, ALU.add)
                    dve.drain()
                    V.tensor_tensor(two(Pp[:, u.par, :]), two(Ss[:]), pair(u), ALU.mult).then_inc(gelu_arg, 1)
                    lo(u.later(2), 1)
                    dve.wait_ge(gelu_tanh, l * 4 + (j + 1))
                    stt(Gb[:, 2 * j:2 * j + 2, :], two(Tt[:, u.par, :]), 1.0, pair(u), ALU.add, ALU.mult) \
                        .then_inc(banks_free[u.par], 1)
                for i in range(12):
                    u = Unit(q, k + 8 + i)
                    hp, what = i // 3, i % 3
                    if what < 2:
                        j = 2 * hp + what
                        dve.wait_ge(rg_tanh, l * C + (j + 1))
                        stt(Xc[:, j, :], Rr[:, T:2 * T], 1.0, Xc[:, j, :], ALU.add, ALU.mult)
                        V.tensor_scalar(Ss[:, 0:T], Rr[:, 0:T], 1.0, cur[:, R_LAM + j:R_LAM + j + 1], ALU.add, ALU.mult) \
                            .then_inc(la_done, 1)
                        lo(u.later(2), 0)
                        dve.wait_ge(rg_exp, l * C + (j + 1))
                        V.tensor_tensor(Ss[:, T:2 * T], decay[:, j, :], decay[:, j, :], ALU.mult)
                        dve.drain()
                        stt(keep[:, j, :], Ss[:, T:2 * T], 1.0, Pp[:, j % 2, 0:T], ALU.add, ALU.mult) \
                            .then_inc(keep_done, 1)
                        dve.wait_ge(qk_sq, l * 8 + (j + 1))
                        dst = (Qb, Kb)[what][:, 2 * hp:2 * hp + 2, :]
                        V.tensor_scalar(dst, pair(u), cur[:, R_QN + what:R_QN + what + 1], None, ALU.mult) \
                            .then_inc(banks_free[u.par], 1)
                        lo(u.later(2), 1)
                    else:
                        lo(u.later(2), 0)
                        if hp == 0:
                            z, e = Ss[0:HEADS, 0:T], Ss[0:HEADS, T:2 * T]
                            a, b = Pp[0:HEADS, 0, T:2 * T], Pp[0:HEADS, 1, T:2 * T]
                            dve.wait_ge(f_mm, l + 2)
                            V.tensor_scalar(z, ps[0:HEADS, 4, 0:T], tiny[0:HEADS, 12:13], None, ALU.add).then_inc(f_in, 1)
                            dve.wait_ge(f_abs, l * 2 + 2)
                            log1p(a, e, b, dmask[:])
                            stt(a, z, 0.0, a, ALU.min, ALU.subtract)
                            V.memset(e, 1.0)
                            dve.drain()
                            V.tensor_tensor_scan(z, e, a, 0.0, ALU.mult, ALU.add)
                            dve.drain()
                            V.tensor_scalar(dneg[:], z, -1.0, None, ALU.mult)
                            dve.drain()
                        dve.wait_ge(mm_done, u.mm_done(1))
                        V.tensor_copy(Vb[:, :, T * hp:T * (hp + 1)], pair(u)).then_inc(banks_free[u.par], 1)
                        lo(u.later(2), 1)
                dve.wait_ge(qk_std, l + 1)
                V.reciprocal(rqk[:], rqk[:])
                dve.drain()

                def masks(h):
                    V.tensor_scalar(rmask[:, 0:T], rqk[:], ident[0:2 * HEADS, h:h + 1], None, ALU.mult)
                    V.tensor_scalar(rmask[:, T:2 * T], rqk[:], ident[0:2 * HEADS, HEADS + h:HEADS + h + 1], None,
                                    ALU.mult)
                    V.tensor_scalar(dmask[:], dneg[:], ident[0:HEADS, h:h + 1], None, ALU.mult).then_inc(rm_done, 1)

                def low_out(h):
                    dve.wait_ge(oh_done, l * HEADS + (h + 1))
                    V.tensor_tensor(Fl[:, 1, h, :], ps[:, 7, 0:T], Fh[:, 1, h, :].bitcast(F32), ALU.subtract) \
                        .then_inc(o_done, 1)

                masks(0)
                for st in range(HEADS):
                    u = Unit(q, k + 20 + st)
                    dve.wait_ge(bc_done, l * HEADS + (st + 1))
                    V.tensor_tensor(Qb[:, st, :], Qb[:, st, :], ps[:, 4, 0:T], ALU.mult)
                    V.tensor_tensor(Kb[:, st, :], Kb[:, st, :], ps[:, 4, T:2 * T], ALU.mult).then_inc(qkn_done, 1)
                    lo(u.later(2), 0)
                    dve.wait_ge(s_done, l * HEADS + (st + 1))
                    V.tensor_tensor(scores[:, 0:P], ps[:, 5, 0:P], low, ALU.add)
                    V.tensor_copy(scores[:, P:2 * P], ps[:, 5, P:2 * P])
                    V.tensor_tensor(scores[:, 2 * P:3 * P], ps[:, 5, 2 * P:3 * P], low, ALU.add)
                    dve.drain()
                    V.tensor_reduce(tiny[:, 6:7], scores[:, 0:P], AX_X, ALU.max)
                    V.tensor_reduce(tiny[:, 7:8], scores[:, P:3 * P], AX_X, ALU.max)
                    dve.drain()
                    V.tensor_scalar(tiny[:, 0:2], tiny[:, 6:8], -1.0, None, ALU.mult).then_inc(nmax_done, 1)
                    if st >= 1:
                        low_out(st - 1)
                    if st < 4:
                        if st == 0:
                            dve.wait_ge(root_done, l + 1)
                        two_chunks = (2 * st, 2 * st + 1)
                        for j in two_chunks:
                            stt(Xc[:, j, :], Xc[:, j, :], 0.5, keep[:, j, :], ALU.mult, ALU.mult)
                        dve.drain()
                        for j in two_chunks:
                            V.tensor_tensor_scan(Pp[:, j % 2, 0:T], decay[:, j, :], Xc[:, j, :], 0.0, ALU.mult, ALU.add)
                        dve.drain()
                        for j in two_chunks:
                            V.tensor_tensor(Pp[:, j % 2, T:2 * T], Pp[:, j % 2, 0:T], Gb[:, j, :], ALU.mult) \
                                .then_inc(y_done, 1)
                    dve.wait_ge(exp_done, l * HEADS + (st + 1))
                    V.reciprocal(tiny[:, 4:6], tiny[:, 2:4])
                    dve.drain()
                    V.tensor_scalar(scores[:, 0:P], scores[:, 0:P], tiny[:, 4:5], None, ALU.mult)
                    V.tensor_scalar(scores[:, P:3 * P], scores[:, P:3 * P], tiny[:, 5:6], None, ALU.mult) \
                        .then_inc(pn_done, 1)
                    if st < 4:
                        for j in two_chunks:
                            dve.wait_ge(yh_done, l * C + (j + 1))
                            V.tensor_tensor(Fl[:, 0, j, :], Pp[:, j % 2, T:2 * T], Fh[:, 0, j, :].bitcast(F32),
                                            ALU.subtract).then_inc(ya_done, 1)
                    if st + 1 < HEADS:
                        masks(st + 1)
                    lo(u.later(2), 1)
                    if st >= 4:
                        dve.wait_ge(mm_done, u.mm_done(1))
                        ga = gateA[:, 2 * (st - 4):2 * (st - 4) + 2, :]
                        stt(ga, ga, 1.0, pair(u), ALU.add, ALU.mult).then_inc(banks_free[u.par], 1)
                for j in range(4):
                    u = Unit(q, k + 28 + 2 * j)
                    lo(u.later(2), 0)
                    if j == 0:
                        low_out(HEADS - 1)
                    lo(u.later(2), 1)
                    u = u.later(1)
                    lo(u.later(2), 0)
                    dve.wait_ge(mm_done, u.mm_done(1))
                    ue = u.later(-1)
                    dve.wait_ge(banks_free[ue.par], ue.read_out())
                    stt(two(Ss[:]), two(Tt[:, j % 2, :]), 1.0, pair(u), ALU.add, ALU.mult) \
                        .then_inc(banks_free[u.par], 1)
                    dve.drain()
                    stt(two(Pp[:, j % 2, :]), two(Ss[:]), 2.0, gateA[:, 2 * j:2 * j + 2, :], ALU.mult, ALU.add) \
                        .then_inc(mp_done, 1)
                    lo(u.later(2), 1)
                    dve.wait_ge(mh_done, l * 4 + (j + 1))
                    V.tensor_tensor(Hl[:, 1, 2 * j:2 * j + 2, :], two(Pp[:, j % 2, :]),
                                    Hh[:, 1, 2 * j:2 * j + 2, :].bitcast(F32), ALU.subtract).then_inc(m_done, 1)
                for j in range(4):
                    u = Unit(q, k + 36 + j)
                    lo(u.later(2), 0)
                    dve.wait_ge(mm_done, u.mm_done(1))
                    x = Xx[:, 2 * j:2 * j + 2, :]
                    stt(x, pair(u), 0.25, x, ALU.mult, ALU.add).then_inc(banks_free[u.par], 1)
                    lo(u.later(2), 1)

                norm(l * 4 + 2, T, l * 4 + 2, layer_gain(R_FFN2))
                ffn(q, K_FFN2, l * 2 + 1, T, FULL_GROUP, LAST_GROUP, ada=(l, 1))
                dve.wait_ge(pth_done, l + 1)
                V.tensor_tensor(Fl[:, 1, 0:2, :], two(ps[:, 7, :]), Fh[:, 1, 0:2, :].bitcast(F32), ALU.subtract) \
                    .then_inc(p_there, 1)
                norm(l * 4 + 3, T, l * 4 + 3, layer_gain(R_PLE))
                for j in range(4):
                    u = Unit(q, K_PLE + 2 * j)
                    stream(u)
                    ue, u = u, u.later(1)
                    lo(u.later(2), 0)
                    dve.wait_ge(banks_free[ue.par], ue.read_out())
                    dve.wait_ge(mm_done, u.mm_done(1))
                    stt(two(Ss[:]), two(Tt[:, j % 2, :]), 1.0, pair(u), ALU.add, ALU.mult)
                    dve.drain()
                    x = Xx[:, 2 * j:2 * j + 2, :]
                    stt(x, two(Ss[:]), 0.5, x, ALU.mult, ALU.add).then_inc(banks_free[u.par], 1)
                    lo(u.later(2), 1)

            q = Q_SECOND
            rms(8, T)
            for kc in range(C):
                stt(Xx[:, kc, :], Xx[:, kc, :], par[:, 2, R_FINAL + kc:R_FINAL + kc + 1], Rr[:, 0:T], ALU.mult, ALU.mult)
            for b in range(4):
                dve.wait_ge(turned, b + 6)
                V.tensor_copy(Xc[:, 2 * b:2 * b + 2, :], two(ps[:, 4 + b, :])).then_inc(turned_out, 1)
            dve.drain().then_inc(x_normed, 1)

            def layer_consts(l):
                for s in range(2):
                    V.tensor_tensor(MOD[:, l, :, s], MOD[:, l, :, s], par[:, 5 + l, 0:N_MOD * C], ALU.add)
                dve.drain()
                for i in range(3):
                    r = R_NORM + (3 * l + i) * C
                    for s in range(2):
                        stt(S1[:, i, :, s], MOD[:, l, (3 * i + 1) * C:(3 * i + 2) * C, s], 1.0, par[:, 2, r:r + C],
                            ALU.add, ALU.mult)
                    factor = 0.25 if i != 1 else (0.5 if l == 0 else 1.0)
                    V.tensor_scalar(G1[:, i], MOD[:, l, (3 * i + 2) * C:(3 * i + 3) * C, :], factor, None, ALU.mult)
                dve.drain().then_inc(mod_there, 1)

            def gain(i):
                return lambda kc, s: S1[:, i, kc, s:s + 1]

            def gate(i):
                return lambda kc, s: G1[:, i, kc, s:s + 1]

            def shift(l, i):
                return lambda kc, s: MOD[:, l, (3 * i) * C + kc, s:s + 1]

            layer_consts(0)
            V.tensor_scalar(tiny[:, 40:48], par[:, 2, R_PW1B + C:R_PW1B + 2 * C], 0.5, None, ALU.mult)
            V.tensor_scalar(tiny[:, 0:16], par[:, 2, R_LNG:R_LNG + 16], 0.5, None, ALU.mult)
            V.tensor_scalar(par[:, 3, :], par[:, 3, :], 0.5, None, ALU.mult)
            V.tensor_scalar(par[:, 4, 0:PAR_ROWS[4]], par[:, 4, 0:PAR_ROWS[4]], 0.5, None, ALU.mult)
            V.memset(upad[:], 0.0)
            dve.drain()
            norm(9, 512, 8, gain(0), shift(0, 0))
            ffn(q, 0, 4, 512, PLAIN_FULL, PLAIN_LAST, gate(0))
            norm(10, 512, 9, gain(1), shift(0, 1))
            conv = (Qb, Kb)
            for j in range(C):
                u = Unit(q, K2_CONV + j)
                lo(u.later(2), 0)
                dve.wait_ge(cv_tanh, j + 1)
                V.tensor_scalar(Ss[:], Tt[:, u.par, :], 1.0, None, ALU.add)
                dve.drain()
                pb = upad[:, u.par]
                stt(pb[:, :, PAD:PAD + T], two(bank(u, 0)), par[:, 2, R_PW1B + j:R_PW1B + j + 1], two(Ss[:]), ALU.add,
                    ALU.mult).then_inc(banks_free[u.par], 1)
                dve.drain()
                lo(u.later(2), 1)
                for tap in range(TAPS):
                    w = par[:, 3 + tap // 16, (tap % 16) * 8 + j:(tap % 16) * 8 + j + 1]
                    acc, src = two(Pp[:, tap % 2, :]), pb[:, :, tap:tap + T]
                    if tap == 0:
                        V.tensor_scalar(acc, src, w, par[:, 2, R_DWB + j:R_DWB + j + 1], ALU.mult, ALU.add)
                    elif tap == 1:
                        V.tensor_scalar(acc, src, w, None, ALU.mult)
                    else:
                        stt(acc, src, w, acc, ALU.mult, ALU.add)
                    if tap % 2:
                        dve.drain()
                dve.drain()
                for s in range(2):
                    ins = V.tensor_tensor(conv[s][:, j, :], Pp[:, 0, s * T:(s + 1) * T], Pp[:, 1, s * T:(s + 1) * T],
                                          ALU.add)
                ins.then_inc(cv_done, 1)
            dve.wait_ge(mu_mm, 1)
            for s in range(2):
                V.tensor_scalar(Ss[:, s * T:(s + 1) * T], ps[:, 4 + s, 0:T], -1.0 / D, None, ALU.mult)
            dve.drain()
            for kc in range(C):
                for s in range(2):
                    ins = V.tensor_tensor(conv[s][:, kc, :], conv[s][:, kc, :], Ss[:, s * T:(s + 1) * T], ALU.add)
                ins.then_inc(cen_done, 1)
            dve.wait_ge(cstd_done, 1)
            V.reciprocal(Rr[:], Rr[:])
            dve.drain()
            for kc in range(C):
                for s in range(2):
                    ins = V.tensor_tensor(conv[s][:, kc, :], conv[s][:, kc, :], Rr[:, s * T:(s + 1) * T], ALU.mult)
                ins.then_inc(z_done, 1)
            for kc in range(C):
                dve.drain()
                for s in range(2):
                    V.tensor_scalar(Ss[:, s * T:(s + 1) * T], conv[s][:, kc, :], par[:, 2, R_LNG + kc:R_LNG + kc + 1],
                                    par[:, 2, R_LNB + kc:R_LNB + kc + 1], ALU.mult, ALU.add)
                dve.wait_ge(zt_done, kc + 1)
                dve.drain()
                stt(Pp[:, kc % 2, :], Tt[:, kc % 2, :], 1.0, Ss[:], ALU.add, ALU.mult).then_inc(zp_done, 1)
                dve.wait_ge(zh_done, kc + 1)
                V.tensor_tensor(Fl[:, 0:2, kc, :], two(Pp[:, kc % 2, :]), Fh[:, 0:2, kc, :].bitcast(F32), ALU.subtract) \
                    .then_inc(z_there, 1)
            for s in range(2):
                V.tensor_tensor(Ss[:, s * C:(s + 1) * C], MOD[:, 0, 5 * C:6 * C, s], par[:, 2, R_PW2B:R_PW2B + C], ALU.mult)
            dve.drain()
            for kc in range(C):
                for s in range(2):
                    x = (Xx, Xc)[s][:, kc, :]
                    V.tensor_scalar(x, x, Ss[:, s * C + kc:s * C + kc + 1], None, ALU.add)
            dve.drain()
            for j in range(4):
                u = Unit(q, K2_PW2 + j)
                lo(u.later(2), 0)
                dve.wait_ge(mm_done, u.mm_done(1))
                add_gated(u, j, 512, gate(1))
                lo(u.later(2), 1)
            norm(11, 512, 10, gain(2), shift(0, 2))
            ffn(q, K2_FFN2, 5, 512, PLAIN_FULL, PLAIN_LAST, gate(2))
            dve.drain()
            layer_consts(1)
            norm(12, 512, 11, gain(0), shift(1, 0))
            ffn(q, K2_L1, 6, 512, PLAIN_FULL, PLAIN_LAST, gate(0))
            norm(13, 512, 12, gain(1), shift(1, 1))
            cos, sin = ro[:, RO_COS:RO_COS + T], ro[:, RO_SIN:RO_SIN + T]

            def rotated(i, tiles):
                dve.wait_ge(rot_mm, i + 1)
                dve.drain()
                for t in range(2):
                    V.tensor_tensor(Ss[:, t * T:(t + 1) * T], ps[:, 4 + i % 2, t * T:(t + 1) * T], sin, ALU.mult)
                    V.tensor_tensor(Pp[:, 0, t * T:(t + 1) * T], tiles(t), cos, ALU.mult)
                dve.drain()
                for t in range(2):
                    ins = V.tensor_tensor(tiles(t), Pp[:, 0, t * T:(t + 1) * T], Ss[:, t * T:(t + 1) * T], ALU.add)
                ins.then_inc(rot_done, 1)

            for j in range(4):
                u = Unit(q, K2_Q + j)
                lo(u.later(2), 0)
                dve.wait_ge(mm_done, u.mm_done(1))
                V.tensor_scalar(Qb[:, 2 * j:2 * j + 2, :], pair(u), HD ** -0.5, None, ALU.mult) \
                    .then_inc(banks_free[u.par], 1)
                lo(u.later(2), 1)
                if j >= 1:
                    rotated(j - 1, lambda t, j=j: Qb[:, 2 * (j - 1) + t, :])
            u = Unit(q, K2_KV)
            lo(u.later(2), 0)
            dve.wait_ge(mm_done, u.mm_done(1))
            V.tensor_copy(kraw, ps[:, 2 * u.par:2 * u.par + 2, :]).then_inc(banks_free[u.par], 1)
            lo(u.later(2), 1)
            rotated(3, lambda t: Qb[:, 6 + t, :])
            u = u.later(1)
            lo(u.later(2), 0)
            dve.wait_ge(mm_done, u.mm_done(1))
            V.tensor_copy(v2, ps[:, 2 * u.par:2 * u.par + 2, :].rearrange("p b (t d) -> p (b t) d", t=2)) \
                .then_inc(banks_free[u.par], 1)
            lo(u.later(2), 1)
            rotated(4, lambda t: kraw[:, t, 0:T])

            def low2_out(tile):
                dve.wait_ge(oh2_done, tile + 1)
                V.tensor_tensor(Fl[:, 0, tile, :], ps[:, 6 + tile % 2, 0:T], Fh[:, 0, tile, :].bitcast(F32),
                                ALU.subtract).then_inc(o2_done, 1)

            for h in range(QH):
                for b in range(2):
                    s = ps[:, 2 * (h % 2) + b, :]
                    dve.wait_ge(s2_done, 2 * h + b + 1)
                    masked, m = (s[:, P:2 * P], low) if b == 0 else (s[:, 0:P], up)
                    V.tensor_tensor(masked, masked, m, ALU.add)
                    dve.drain()
                    V.tensor_reduce(tiny[:, 6 + b:7 + b], s, AX_X, ALU.max)
                    dve.drain()
                    if h >= 1:
                        dve.wait_ge(e2_done, 2 * (h - 1) + b + 1)
                    V.tensor_scalar(tiny[:, b:b + 1], tiny[:, 6 + b:7 + b], tiny[:, 16 + h:17 + h], -1.0, ALU.max,
                                    ALU.mult).then_inc(nm2_done, 1)
                for b in range(2):
                    dve.wait_ge(e2_done, 2 * h + b + 1)
                    V.tensor_tensor(tiny[:, 8 + b:9 + b], tiny[:, 2 + b:3 + b], tiny[:, 4 + b:5 + b], ALU.add)
                    dve.drain()
                    V.reciprocal(tiny[:, 10 + b:11 + b], tiny[:, 8 + b:9 + b])
                    dve.drain()
                    V.tensor_scalar(Pp[:, b, :], Pp[:, b, :], tiny[:, 10 + b:11 + b], None, ALU.mult) \
                        .then_inc(pn2_done, 1)
                if h % 2 == 0 and h >= 2:
                    low2_out(h // 2 - 1)
            low2_out(QH // 2 - 1)
            for j in range(4):
                u = Unit(q, K2_WO + j)
                lo(u.later(2), 0)
                dve.wait_ge(mm_done, u.mm_done(1))
                add_gated(u, j, T, gate(1))
                lo(u.later(2), 1)
            norm(14, T, 13, gain(2), shift(1, 2))
            ffn(q, K2_FFN4, 7, T, PLAIN_FULL, PLAIN_LAST, gate(2))
            rms(15, T)
            for kc in range(C):
                stt(Xx[:, kc, :], Xx[:, kc, :], par[:, 2, R_FING + kc:R_FING + kc + 1], Rr[:, 0:T], ALU.mult, ALU.mult) \
                    .then_inc(final_done, 1)


_INS = ["x", "p", "ffn1_norm", "ffn1_w_in", "ffn1_w_out", "mix_norm", "w_in", "merge_b", "conv_w", "conv_b", "rg_wa",
        "rg_ba", "rg_wx", "rg_bx", "rg_lambda", "f_b", "q_norm", "k_norm", "w_rnn_out", "w_attn_out", "w_o",
        "ffn2_norm", "ffn2_w_in", "ffn2_w_out", "ple_norm", "ple_w_gate", "ple_b_gate", "ple_w_proj", "final_norm",
        "c_2", "ctx_2", "c_ctx_2", "norm_g_2", "ada_w_2", "ada_b_2", "ffn1_wi_2", "ffn1_wo_2", "ffn2_wi_2",
        "ffn2_wo_2", "conv_pw1_w_2", "conv_pw1_b_2", "conv_dw_w_2", "conv_dw_b_2", "conv_ln_g_2", "conv_ln_b_2",
        "conv_pw2_w_2", "conv_pw2_b_2", "attn_w_qkv_2", "attn_w_o_2", "attn_sink_2", "final_g_2"]


def kernel(**inputs):
    import concourse.bacc as bacc
    from concourse.bass_utils import run_bass_kernel_spmd

    nc = bacc.Bacc("TRN2", target_bir_lowering=False, num_devices=1)
    arrays = {f"in_{n}": np.ascontiguousarray(inputs[n]) for n in _INS}
    arrays["in_co"], arrays["in_ro"] = shape_constants()
    aps = {n[3:]: nc.dram_tensor(n, a.shape, F32, kind="ExternalInput").ap() for n, a in arrays.items()}
    out = nc.dram_tensor("out", (1, T, D), F32, kind="ExternalOutput").ap()
    build(nc, aps, out)
    r = run_bass_kernel_spmd(nc, [arrays], core_ids=[0])
    return r.results[0]["out"]
```

```python
import numpy as np

import concourse.bass as bass
from concourse import mybir

F32 = mybir.dt.float32
F32R = mybir.dt.float32r
ALU = mybir.AluOpType
ACT = mybir.ActivationFunctionType
AX_X = mybir.AxisListType.X

P = 128
T = 256
D = 1024
C = D // P
DEPTH = 2
F = 2816
FC = F // P
GROUPS = (8, 8, 6)
HEADS = 8
PLE = 256
RNN_BW = 64
N_MOD = 9
QH, KVH, HD = 16, 4, 64
TAPS = 31
PAD = (TAPS - 1) // 2
PE_TAPS = (8,) * (C - 1) + (14,)
DIAGS = D // P * T // P
EPS = 1e-6
NEG = -3.0e38
GELU_C = 0.7978845608028654
GELU_A = 0.044715

ADA_UNITS = N_MOD * D // 256
GROUP_ADA = 8
FFN_A = 52
FFN_B = 34
K_MIX, K_FFN2, K_PLE, K_LAYER = FFN_A, FFN_A + 40, 2 * FFN_A + 40, 2 * FFN_A + 48
assert ADA_UNITS == 2 * (2 * GROUP_ADA + 2) and K_LAYER % 4 == 0
Q_LAYER = K_LAYER // 4
Q_SECOND = DEPTH * Q_LAYER
K2_CONV, K2_PW2, K2_FFN2, K2_L1 = FFN_B, FFN_B + 8, FFN_B + 12, 2 * FFN_B + 12
K2_Q, K2_KV, K2_WO, K2_FFN4 = K2_L1 + FFN_B, K2_L1 + FFN_B + 4, K2_L1 + FFN_B + 6, K2_L1 + FFN_B + 10
K2_END = K2_FFN4 + FFN_B


class Unit:

    def __init__(self, q, k):
        self.q, self.k = q, k
        self.slot = k % 4
        self.par = k % 2

    def later(self, by):
        return Unit(self.q, self.k + by)

    def last(self):
        return isinstance(self.q, int) and 4 * self.q + self.k >= 4 * Q_SECOND + K2_END

    def raw_full(self):
        return (self.q + (self.k // 4 + 1)) * 32

    def raw_free(self):
        return self.q * 8 + (2 * self.k + 2)

    def split_free(self, t):
        return self.q * 8 + (2 * self.k + t + 1)

    def hi_done(self, t):
        return self.q * 8 + (2 * self.k + t + 1)

    def lo_done(self, t):
        return self.q * 8 + (2 * self.k + t + 9)

    def mm_done(self, t):
        return self.q * 8 + (2 * self.k + t + 5)

    def banks_free(self):
        return self.q * 2 + (self.k // 2 + 1)

    def read_out(self):
        return self.q * 2 + (self.k // 2 + 2)


FULL_GROUP = [("G", 0)] + [x for i in range(1, 8) for x in (("G", i), ("A", i - 1))] \
    + [("O", 0), ("A", 7), ("O", 1), ("O", 2), ("O", 3)]
LAST_GROUP = [("G", 0), ("G", 1), ("A", 0)] + [("G", i) for i in range(2, 6)] + [("O", i) for i in range(4)] + [("A", 1)]
PLAIN_FULL = [x for x in FULL_GROUP if x[0] != "A"]
PLAIN_LAST = [x for x in LAST_GROUP if x[0] != "A"]

R_FFN1, R_MIX, R_MERGE, R_CONV, R_CONVB, R_BA, R_BX, R_LAM, R_FFN2, R_PLE, R_PLEB, R_QN, R_KN = (
    0, 8, 16, 32, 64, 72, 80, 88, 96, 104, 112, 120, 121)
R_LAYER = 122
R_FINAL, R_NORM, R_PW1B, R_DWB, R_LNG, R_LNB, R_PW2B, R_FING, R_C, R_CCTX = (
    0, 8, 56, 72, 80, 88, 96, 104, 112, 120)
PAR_TILES = 7
PAR_ROWS = (R_LAYER, R_LAYER, 128, 128, (TAPS - 16) * 8, 72, 72)
PAR_LOADS = 2 * 13 + 10 + 2 + 2

CO_IDENT, CO_LOW, CO_UP, CO_PICK, CO_SUM, CO_N = 0, 128, 256, 384, 416, 418
RO_COS, RO_SIN, RO_ROT, RO_DUP, RO_N = 0, 256, 512, 640, 896


def shape_constants():
    co = np.zeros((P, CO_N), np.float32)
    i = np.arange(P)
    co[:, CO_IDENT:CO_IDENT + P] = np.eye(P)
    co[:, CO_LOW:CO_LOW + P] = np.where(i[None, :] <= i[:, None], 0.0, NEG)
    co[:, CO_UP:CO_UP + P] = np.where(i[None, :] >= i[:, None], 0.0, NEG)
    for r in range(4):
        co[r, CO_SUM + r % 2] = 1.0
    co[:, CO_PICK + 15] = 1.0
    ro = np.zeros((P, RO_N), np.float32)
    n_freq = HD // 4
    inv = (np.float32(10000.0) ** (-np.arange(n_freq, dtype=np.float32) / np.float32(n_freq))).astype(np.float32)
    tok = np.arange(T)
    d = i % HD
    place = np.where((d // 32)[:, None] == 0, (tok // 64)[None, :], (tok % 64)[None, :]).astype(np.float32)
    angle = (place * inv[d % n_freq][:, None]).astype(np.float32)
    ro[:, RO_COS:RO_COS + T] = np.cos(angle)
    ro[:, RO_SIN:RO_SIN + T] = np.sin(angle)
    for m in range(P):
        if m % 32 < 16:
            ro[m + 16, RO_ROT + m] = -1.0
        else:
            ro[m - 16, RO_ROT + m] = 1.0
        for e in range(2):
            ro[64 * e + m % 64, RO_DUP + 128 * e + m] = 1.0
    return co, ro


def build(nc, A, out):
    off = [(nc.sbuf_base + 31) // 32 * 32]

    def sb(name, shape, dt=F32, at=None):
        size = 4 * int(np.prod(shape[1:]))
        where = off[0] if at is None else at
        if at is None:
            off[0] += (size + 31) // 32 * 32
        return nc.alloc_sbuf_tensor_at(name, shape, dt, offset=where)

    from contextlib import ExitStack
    ctx = ExitStack()
    with ctx:
        Xx = sb("Xx", [P, C, T])
        Xc = sb("Xc", [P, C, T])
        Hh = sb("Hh", [P, 2, C, T], F32R)
        hh_ctx_at = off[0] - 4 * C * T
        Hl = sb("Hl", [P, 2, C, T], F32R)
        fh_at = off[0]
        Fh = sb("Fh", [P, 2, C, T], F32R)
        fl_at = off[0]
        Fl = sb("Fl", [P, 2, C, T], F32R)
        decay = sb("decay", [P, C, T], at=fh_at)
        keep = sb("keep", [P, C, T], at=fl_at)
        gateA = sb("gateA", [P, C, T], at=hh_ctx_at)
        raw = sb("raw", [P, 4, C, 256])
        wh = sb("wh", [P, 2, C, 256], F32R)
        wl = sb("wl", [P, 2, C, 256], F32R)
        Gb = sb("Gb", [P, C, T])
        QK = sb("QK", [P, 2, C, T])
        Qb, Kb = QK[:, 0], QK[:, 1]
        Vb = sb("Vb", [P, 2, D])
        Tt = sb("Tt", [P, 2, 512])
        Pp = sb("Pp", [P, 2, 512])
        Ss = sb("Ss", [P, 512])
        Rr = sb("Rr", [P, 512])
        par = sb("par", [P, PAR_TILES, P])
        cur = sb("cur", [P, R_LAYER])
        half = sb("half", [P, R_LAYER])
        co = sb("co", [P, CO_N])
        gate_at = off[0]
        wgate = sb("wgate", [P, 2, C, P])
        ro = sb("ro", [P, RO_N], at=gate_at)
        wf = sb("wf", [P, C, HEADS])
        ones = sb("ones", [P, P])
        MOD = sb("MOD", [P, DEPTH, N_MOD * C, 2])
        cs = sb("cs", [P, C, 4], F32R)
        tiny = sb("tiny", [P, 64])
        S1 = sb("S1", [P, 3, C, 2])
        G1 = sb("G1", [P, 3, C, 2])
        eps = sb("eps", [P, 2])
        dneg = sb("dneg", [HEADS, T])
        dmask = sb("dmask", [HEADS, T])
        rqk = sb("rqk", [2 * HEADS, T])
        fb = sb("fb", [HEADS, DEPTH])
        assert off[0] <= nc.sbuf_usable_end, (off[0], nc.sbuf_usable_end)
        ident, low, up = (co[:, a:a + P] for a in (CO_IDENT, CO_LOW, CO_UP))
        prow = Gb[:].rearrange("p c t -> p (c t)")[:, 0:PAR_TILES * P].rearrange("p (n f) -> p n f", f=P)
        xtok = Qb[:].rearrange("p c t -> p (c t)").rearrange("p (n d) -> p n d", n=2)
        ctok = Kb[:].rearrange("p c t -> p (c t)").rearrange("p (n d) -> p n d", n=2)
        ptok = Vb[:, :, 0:PLE]
        diag = Gb[:].rearrange("p c t -> p (c t)").rearrange("p (n f) -> p n f", f=P)
        scaled = Gb[:].rearrange("p c t -> p (c t)").rearrange("p (n f) -> p n f", f=2 * T)
        otok = Gb[:].rearrange("p c t -> p (c t)").rearrange("p (n d) -> p n d", n=2)
        upad = Vb[:].rearrange("p n d -> p (n d)")[:, 0:4 * (T + 2 * PAD)].rearrange(
            "p (b s t) -> p b s t", b=2, s=2)
        kraw = Gb[:].rearrange("p c t -> p (c t)")[:, 0:1024].rearrange("p (n t) -> p n t", n=2)
        kdup = Kb[:].rearrange("p c t -> p (c t)").rearrange("p (n t) -> p n t", n=KVH)
        v2 = Vb[:].rearrange("p n d -> p (n d)")[:, 0:4 * 256].rearrange("p (n d) -> p n d", n=4)
        probs2 = ((Pp[:, 0, :], Pp[:, 1, :]), (Ss[:], Rr[:]))
        probsT2 = (Tt[:], Gb[:].rearrange("p c t -> p (c t)")[:, 1024:2048].rearrange("p (n t) -> p n t", n=2))
        rmask = Rr[0:2 * HEADS, :]
        scores = Tt[:, 0, 0:384]
        probsT = Tt[:, 1, 0:384]

        ps = ctx.enter_context(nc.psum_tensor("ps", [P, 8, 512], F32))

        def sem(name):
            return ctx.enter_context(nc.semaphore(name))

        raw_full = [sem(f"raw_full{i}") for i in range(4)]
        hi_done, lo_done, mm_done = sem("hi_done"), sem("lo_done"), sem("mm_done")
        banks_free = [sem(f"banks_free{i}") for i in range(2)]
        par_in, tok_in, small_in = sem("par_in"), sem("tok_in"), sem("small_in")
        zeroed, ones_there, turned, turned_out, x_there = sem("zeroed"), sem("ones_there"), sem("turned"), sem("turned_out"), sem("x_there")
        par_there, eps_there, lam_exp, c_tanh, c_prod, c_hi, c_there = (
            sem(n) for n in ("par_there", "eps_there", "lam_exp", "c_tanh", "c_prod", "c_hi", "c_there"))
        sq_done, ss_done, std_done, hp_done, hh_done, h_done = (
            sem(n) for n in ("sq_done", "ss_done", "std_done", "hp_done", "hh_done", "h_done"))
        x_normed, final_done = sem("x_normed"), sem("final_done")
        tanh_done, fh_done, f_done = sem("tanh_done"), sem("fh_done"), sem("f_done")
        cur_there, wgate_in, wf_in, rg_mm, rg_tanh, la_done, rg_exp, keep_done, root_done = (
            sem(n) for n in ("cur_there", "wgate_in", "wf_in", "rg_mm", "rg_tanh", "la_done", "rg_exp",
                             "keep_done", "root_done"))
        gelu_sq, gelu_arg, gelu_tanh = sem("gelu_sq"), sem("gelu_arg"), sem("gelu_tanh")
        qk_sq, qk_ss, qk_std = sem("qk_sq"), sem("qk_ss"), sem("qk_std")
        f_mm, f_in, f_abs, dneg_done = sem("f_mm"), sem("f_in"), sem("f_abs"), sem("dneg_done")
        y_done, yh_done, ya_done = sem("y_done"), sem("yh_done"), sem("ya_done")
        rm_done, bc_done, qkn_done, s_done, nmax_done, exp_done, pn_done, tr_done, pt_done, pv_done, oh_done, \
            o_done = (sem(n) for n in ("rm_done", "bc_done", "qkn_done", "s_done", "nmax_done", "exp_done",
                                       "pn_done", "tr_done", "pt_done", "pv_done", "oh_done", "o_done"))
        gb_tanh, mp_done, mh_done, m_done = sem("gb_tanh"), sem("mp_done"), sem("mh_done"), sem("m_done")
        p_in, p_turned, pth_done, p_there, pg_tanh = (
            sem(n) for n in ("p_in", "p_turned", "pth_done", "p_there", "pg_tanh"))
        mod_turned, mod_there, ro_in = sem("mod_turned"), sem("mod_there"), sem("ro_in")
        u_done, diag_there, diag_used = sem("u_done"), sem("diag_there"), sem("diag_used")
        cv_done, mu_mm, cen_done, csq_done, var_mm, cstd_done, z_done, zt_done, zp_done, zh_done, z_there = (
            sem(n) for n in ("cv_done", "mu_mm", "cen_done", "csq_done", "var_mm", "cstd_done",
                             "z_done", "zt_done", "zp_done", "zh_done", "z_there"))
        rot_mm, rot_done, dup_mm, dup_done, sink_mm, sink_done = (
            sem(n) for n in ("rot_mm", "rot_done", "dup_mm", "dup_done", "sink_mm", "sink_done"))
        r2_done = sem("r2_done")
        s2_done, nm2_done, e2_done, pn2_done, tr2_done, pt2_done, pv2_done, oh2_done, o2_done = (
            sem(n) for n in ("s2_done", "nm2_done", "e2_done", "pn2_done", "tr2_done", "pt2_done", "pv2_done",
                             "oh2_done", "o2_done"))
        out_mm, out_copied, stored = sem("out_mm"), sem("out_copied"), sem("stored")

        def bank(u, t, n=512):
            return ps[:, 2 * u.par + t, 0:n]

        def pair(u):
            return ps[:, 2 * u.par:2 * u.par + 2, 0:T]

        def two(ap):
            return ap.rearrange("p (s n) -> p s n", s=2)

        def tile_of(w, t, mod):
            return w[:, 4 * t:4 * t + 4, :] if mod else w[:, :, P * t:P * t + P]

        def groups_of(eng, q, k, order, last):
            with eng.Fori(0, 2) as g:
                yield g, [(kind, i, Unit(q + g * (len(order) // 4), k + j)) for j, (kind, i) in enumerate(order)]
            yield 2, [(kind, i, Unit(q, k + 2 * len(order) + j)) for j, (kind, i) in enumerate(last)]

        def ada_index(s, g, i):
            return g * GROUP_ADA + (s * (ADA_UNITS // 2) + i)

        block = ctx.enter_context(nc.Block())

        @block.sync
        def _(sp):
            sp.dma_start(co[:], A["co"]).then_inc(small_in, 16)

            def row(tile, r, src):
                n = src.shape[0]
                sp.dma_start(prow[r:r + n, tile, :], src).then_inc(par_in, 16)

            for l in range(DEPTH):
                for r, name in ((R_FFN1, "ffn1_norm"), (R_MIX, "mix_norm"), (R_MERGE, "merge_b"), (R_CONVB, "conv_b"),
                                (R_BA, "rg_ba"), (R_BX, "rg_bx"), (R_LAM, "rg_lambda"), (R_FFN2, "ffn2_norm"),
                                (R_PLE, "ple_norm"), (R_PLEB, "ple_b_gate"), (R_QN, "q_norm"), (R_KN, "k_norm")):
                    row(l, r, A[name][l].rearrange("(c p) -> c p", p=P))
                row(l, R_CONV, A["conv_w"][l].rearrange("k (c p) -> (k c) p", p=P))
            for r, src in ((R_FINAL, A["final_norm"]), (R_PW1B, A["conv_pw1_b_2"][0]), (R_DWB, A["conv_dw_b_2"][0]),
                           (R_LNG, A["conv_ln_g_2"][0]), (R_LNB, A["conv_ln_b_2"][0]), (R_PW2B, A["conv_pw2_b_2"][0]),
                           (R_FING, A["final_g_2"]), (R_C, A["c_2"][0]), (R_CCTX, A["c_ctx_2"])):
                row(2, r, src.rearrange("(c p) -> c p", p=P))
            row(2, R_NORM, A["norm_g_2"].rearrange("l n (c p) -> (l n c) p", p=P))
            row(3, 0, A["conv_dw_w_2"][0, 0:16].rearrange("k (c p) -> (k c) p", p=P))
            row(4, 0, A["conv_dw_w_2"][0, 16:TAPS].rearrange("k (c p) -> (k c) p", p=P))
            for l in range(DEPTH):
                row(5 + l, 0, A["ada_b_2"][l].rearrange("(c p) -> c p", p=P))
            sp.dma_start(xtok, A["x"][0].rearrange("(n p) d -> p n d", p=P)).then_inc(tok_in, 16)
            with nc.allow_non_contiguous_dma(reason="sixteen values"):
                sp.dma_start(fb[:], A["f_b"].rearrange("l h -> h l")).then_inc(small_in, 16)
            sp.dma_start(tiny[0:1, 48:64], A["attn_sink_2"]).then_inc(small_in, 16)

            def load_pair(u, halves):
                sp.wait_ge(lo_done, u.raw_free())
                for h in range(2):
                    sp.dma_start(raw[:, u.slot, :, P * h:P * h + P], halves[:, :, h, :]) \
                        .then_inc(raw_full[u.slot], 16)

            def load_cols(u, w, col, kc=C, k0=0):
                rows = w.rearrange("(c p) n -> p c n", p=P)
                cols = bass.ds(col, 256) if not isinstance(col, int) else slice(col, col + 256)
                sp.wait_ge(lo_done, u.raw_free())
                for h in (1, 0):
                    a, n = h * (kc // 2), kc // 2
                    chunks = slice(k0 + a, k0 + a + n) if isinstance(k0, int) else bass.ds(k0 + a, n)
                    sp.dma_start(raw[:, u.slot, a:a + n, :], rows[:, chunks, cols]).then_inc(raw_full[u.slot], 16)

            def load_ffn(q, k, w_in, w_out, order, last, ada=None):
                gu = w_in.rearrange("(c p) (h n) -> p c h n", p=P, h=2)
                for g, units in groups_of(sp, q, k, order, last):
                    for kind, i, u in units:
                        if kind == "G":
                            f = g * (8 * P) + i * P
                            cols = slice(f, f + P) if isinstance(f, int) else bass.ds(f, P)
                            load_pair(u, gu[:, :, :, cols])
                        elif kind == "O":
                            load_cols(u, w_out, 256 * i, GROUPS[2] if isinstance(g, int) else 8, g * 8)
                        else:
                            l, s = ada
                            load_cols(u, A["ada_w_2"][l], ada_index(s, g, i) * 256)

            with sp.Fori(0, DEPTH) as l:
                q = l * Q_LAYER
                sp.wait_ge(zeroed, 1)
                sp.wait_ge(rg_mm, l * C + 1)
                for g, name in enumerate(("rg_wa", "rg_wx")):
                    blocks = A[name][l].rearrange("(j e) c d -> e c j d", e=2)
                    for e in range(2):
                        sl = slice(RNN_BW * e, RNN_BW * (e + 1))
                        sp.dma_start(wgate[sl, g, :, sl], blocks[e]).then_inc(wgate_in, 16)
                sp.wait_ge(f_mm, l + 1)
                with nc.allow_non_contiguous_dma(reason="eight columns"):
                    sp.dma_start(wf[:], A["w_in"][l].rearrange("(c p) n -> p c n", p=P)[:, :, 5 * D:5 * D + HEADS]) \
                        .then_inc(wf_in, 16)
                load_ffn(q, 0, A["ffn1_w_in"][l], A["ffn1_w_out"][l], FULL_GROUP, LAST_GROUP, (l, 0))
                w_in = A["w_in"][l]
                k = K_MIX
                for j in range(8):
                    load_cols(Unit(q, k + j), w_in, 256 * j)
                for i in range(12):
                    load_cols(Unit(q, k + 8 + i), w_in, 2 * D + (i % 3) * D + 256 * (i // 3))
                for j in range(4):
                    load_cols(Unit(q, k + 20 + j), w_in, 5 * D + HEADS + 256 * j)
                for j in range(4):
                    load_cols(Unit(q, k + 24 + j), A["w_rnn_out"][l], 256 * j)
                for j in range(4):
                    load_cols(Unit(q, k + 28 + 2 * j), w_in, 6 * D + HEADS + 256 * j)
                    load_cols(Unit(q, k + 29 + 2 * j), A["w_attn_out"][l], 256 * j)
                for j in range(4):
                    load_cols(Unit(q, k + 36 + j), A["w_o"][l], 256 * j)
                sp.wait_ge(pv_done, l * HEADS + HEADS)
                sp.dma_start(ptok, A["p"][l, 0].rearrange("(n p) d -> p n d", p=P)).then_inc(p_in, 16)
                load_ffn(q, K_FFN2, A["ffn2_w_in"][l], A["ffn2_w_out"][l], FULL_GROUP, LAST_GROUP, (l, 1))
                for j in range(4):
                    load_cols(Unit(q, K_PLE + 2 * j), A["ple_w_gate"][l], 256 * j)
                    load_cols(Unit(q, K_PLE + 2 * j + 1), A["ple_w_proj"][l], 256 * j, PLE // P)

            q = Q_SECOND
            sp.wait_ge(rg_mm, DEPTH * C + 1)
            sp.dma_start(ro[:], A["ro"]).then_inc(ro_in, 16)
            sp.wait_ge(s_done, DEPTH * HEADS)
            sp.dma_start(ctok, A["ctx_2"][0].rearrange("(n p) d -> p n d", p=P)).then_inc(tok_in, 16)
            load_ffn(q, 0, A["ffn1_wi_2"][0], A["ffn1_wo_2"][0], PLAIN_FULL, PLAIN_LAST)
            pw1 = A["conv_pw1_w_2"][0].rearrange("(c p) (h n) -> p c h n", p=P, h=2)
            for j in range(C):
                load_pair(Unit(q, K2_CONV + j), pw1[:, :, :, P * j:P * j + P])
            for j in range(4):
                load_cols(Unit(q, K2_PW2 + j), A["conv_pw2_w_2"][0], 256 * j)
            load_ffn(q, K2_FFN2, A["ffn2_wi_2"][0], A["ffn2_wo_2"][0], PLAIN_FULL, PLAIN_LAST)
            load_ffn(q, K2_L1, A["ffn1_wi_2"][1], A["ffn1_wo_2"][1], PLAIN_FULL, PLAIN_LAST)
            for j in range(6):
                load_cols(Unit(q, K2_Q + j), A["attn_w_qkv_2"][0], 256 * j)
            for j in range(4):
                load_cols(Unit(q, K2_WO + j), A["attn_w_o_2"][0], 256 * j)
            load_ffn(q, K2_FFN4, A["ffn2_wi_2"][1], A["ffn2_wo_2"][1], PLAIN_FULL, PLAIN_LAST)
            for n in range(2):
                sp.wait_ge(out_copied, 2 * (n + 1))
                sp.dma_start(out[0, n * P:(n + 1) * P, :], otok[:, n, :]).then_inc(stored, 16)
            sp.wait_ge(stored, 32)

        @block.gpsimd
        def _(pool):
            nc.gpsimd.memset(wgate[:], 0.0).then_inc(zeroed, 1)

        @block.tensor
        def _(pe):
            pe.sem_inc(mm_done, 4)
            pe.sem_inc(rg_mm, 1)
            pe.sem_inc(f_mm, 1)

            def out_of(u, t, n):
                return bank(u, t, n) if n == T else two(bank(u, t))

            def linear(u, xh, xl, n, kc_n=C, ready=None, tiles=(0, 1)):
                def products(kc, t):
                    w = slice(P * t, P * t + P)
                    o = out_of(u, t, n)
                    nc.tensor.matmul(o, wh[:, u.par, kc, w], xh(kc), start=(kc == 0), stop=False)
                    nc.tensor.matmul(o, wh[:, u.par, kc, w], xl(kc), start=False, stop=False)
                    return nc.tensor.matmul(o, wl[:, u.par, kc, w], xh(kc), start=False, stop=(kc == kc_n - 1))

                if ready is not None and len(tiles) == 2:
                    pe.wait_ge(lo_done, u.lo_done(1))
                    pe.wait_ge(banks_free[u.par], u.banks_free())
                    for kc in range(kc_n):
                        ready(kc)
                        for t in tiles:
                            mm = products(kc, t)
                            if kc == kc_n - 1:
                                mm.then_inc(mm_done, 1)
                    return
                for t in tiles:
                    pe.wait_ge(lo_done, u.lo_done(t))
                    if t == 0:
                        pe.wait_ge(banks_free[u.par], u.banks_free())
                    for kc in range(kc_n):
                        if ready is not None and t == 0:
                            ready(kc)
                        mm = products(kc, t)
                    mm.then_inc(mm_done, 1)

            def part(buf, n, s=0):
                if n == T:
                    return lambda kc: buf[:, s, kc, :]
                return lambda kc: buf[:, 0:2, kc, :]

            def h_ready(norm):
                return lambda kc: pe.wait_ge(h_done, norm * C + (kc + 1))

            def sums(norm, i, n):
                pe.wait_ge(sq_done, norm * 4 + (i + 1))
                for t in range(2):
                    o = ps[:, 4, 0:T] if n == T else two(ps[:, 4, :])
                    sq = Tt[:, i % 2, t * T:(t + 1) * T] if n == T else Tt[:, :, t * T:(t + 1) * T]
                    mm = nc.tensor.matmul(o, ones[:], sq, start=(i == 0 and t == 0), stop=(i == 3 and t == 1))
                mm.then_inc(ss_done, 1)

            def modulation(u):
                o = ps[0:4, 2 * u.par, 0:256]
                for t in range(2):
                    pe.wait_ge(lo_done, u.lo_done(t))
                    if t == 0:
                        pe.wait_ge(banks_free[u.par], u.banks_free())
                    for kc in range(4 * t, 4 * t + 4):
                        nc.tensor.matmul(o, cs[:, kc, :], wh[:, u.par, kc, :], start=(kc == 0), stop=False)
                        mm = nc.tensor.matmul(o, cs[:, kc, :], wl[:, u.par, kc, :], start=False, stop=(kc == C - 1))
                    mm.then_inc(mm_done, 1)

            def turn_modulation(u, i):
                pe.wait_ge(banks_free[u.par], u.read_out())
                for t in range(2):
                    mm = nc.tensor.matmul(ps[:, 5 + i % 2, 2 * t:2 * t + 2], Pp[0:4, u.par, T + P * t:T + P * (t + 1)],
                                          co[0:4, CO_SUM:CO_SUM + 2], start=True, stop=True)
                mm.then_inc(mod_turned, 1)

            def ffn(q, k, fi, hn, n, order, last, after):
                for g, units in groups_of(pe, q, k, order, last):
                    held = 8 if not isinstance(g, int) else GROUPS[2]
                    for j, (kind, i, u) in enumerate(units):
                        if kind == "G":
                            linear(u, part(Hh, n), part(Hl, n), n, ready=h_ready(hn) if i == 0 else None)
                        elif kind == "O":
                            done = fi * FC + g * 8

                            def ready(kc, done=done):
                                pe.wait_ge(f_done, done + (kc + 1))
                            linear(u, part(Fh, n), part(Fl, n), n, held, ready if i == 0 else None)
                        else:
                            modulation(u)
                        if j >= 1 and units[j - 1][0] == "A":
                            turn_modulation(units[j - 1][2], units[j - 1][1])
                        if isinstance(g, int) and j >= 1 and units[j - 1][0] == "O":
                            sums(after, units[j - 1][1], n)
                if units[-1][0] == "A":
                    turn_modulation(units[-1][2], units[-1][1])
                else:
                    sums(after, 3, n)

            pe.wait_ge(small_in, 48)
            pe.wait_ge(ones_there, 1)
            pe.wait_ge(par_in, 16 * PAR_LOADS)
            for i, n in enumerate(PAR_ROWS):
                mm = nc.tensor.transpose(ps[:, i // 4, (i % 4) * P:(i % 4) * P + n], prow[0:n, i, :],
                                         ident[0:n, 0:n])
            mm.then_inc(turned, 1)
            nc.tensor.matmul(ps[:, 7, 0:QH], ones[0:1, :], tiny[0:1, 48:64], start=True, stop=True) \
                .then_inc(sink_mm, 1)
            def turn_tokens(src, bank0):
                for b in range(4):
                    for i in range(4):
                        mm = nc.tensor.transpose(ps[:, bank0 + b, i * P:(i + 1) * P],
                                                 src[:, i % 2, (2 * b + i // 2) * P:(2 * b + i // 2 + 1) * P], ident)
                    mm.then_inc(turned, 1)

            pe.wait_ge(tok_in, 16)
            turn_tokens(xtok, 2)
            pe.wait_ge(c_there, 1)
            for i in range(4):
                sums(0, i, T)

            with pe.Fori(0, DEPTH) as l:
                q = l * Q_LAYER
                ffn(q, 0, l * 2, l * 4, T, FULL_GROUP, LAST_GROUP, l * 4 + 1)

                k = K_MIX
                for j in range(8):
                    linear(Unit(q, k + j), part(Hh, T), part(Hl, T), T, ready=h_ready(l * 4 + 1) if j == 0 else None)
                pe.wait_ge(wf_in, l * 16 + 16)
                for kc in range(C):
                    nc.tensor.matmul(ps[0:HEADS, 4, 0:T], wf[:, kc, :], Hh[:, 0, kc, :].bitcast(F32),
                                     start=(kc == 0), stop=False)
                    mm = nc.tensor.matmul(ps[0:HEADS, 4, 0:T], wf[:, kc, :], Hl[:, 0, kc, :].bitcast(F32),
                                          start=False, stop=(kc == C - 1))
                mm.then_inc(f_mm, 1)

                def qk_sums(idx):
                    pe.wait_ge(qk_sq, l * 8 + (idx + 1))
                    for t in range(2):
                        r = (idx % 2) * HEADS + 2 * (idx // 2) + t
                        mm = nc.tensor.matmul(ps[0:2 * HEADS, 5, 0:T], co[:, CO_PICK + 15 - r:CO_PICK + 31 - r],
                                              Tt[:, idx % 2, t * T:(t + 1) * T], start=(idx == 0 and t == 0),
                                              stop=(idx == 7 and t == 1), skip_group_check=True)
                    mm.then_inc(qk_ss, 1)

                def gates(j):
                    rx = Unit(q, k + j // 2)
                    pe.wait_ge(banks_free[rx.par], rx.read_out())
                    if j == 0:
                        pe.wait_ge(wgate_in, l * 64 + 64)
                    if j >= 2:
                        pe.wait_ge(rg_tanh, l * 8 + (j - 1))
                    for g in range(2):
                        mm = nc.tensor.matmul(ps[:, 6 + j % 2, g * T:(g + 1) * T], wgate[:, g, j, :], Xc[:, j, :],
                                              start=True, stop=True)
                    mm.then_inc(rg_mm, 1)

                for i in range(12):
                    u = Unit(q, k + 8 + i)
                    hp, what = i // 3, i % 3
                    if what < 2:
                        gates(2 * hp + what)
                        linear(u, part(Hh, T), part(Hl, T), T)
                        if what == 1:
                            qk_sums(2 * hp)
                    else:
                        for t in range(2):
                            pe.wait_ge(lo_done, u.lo_done(1))
                            if t == 0:
                                pe.wait_ge(banks_free[u.par], u.banks_free())
                            tok = slice(t * P, t * P + P)
                            for kc in range(C):
                                o = bank(u, t, T)
                                nc.tensor.matmul(o, Hh[:, 0, kc, tok], wh[:, u.par, kc, :], start=(kc == 0), stop=False)
                                nc.tensor.matmul(o, Hl[:, 0, kc, tok], wh[:, u.par, kc, :], start=False, stop=False)
                                mm = nc.tensor.matmul(o, Hh[:, 0, kc, tok], wl[:, u.par, kc, :], start=False,
                                                      stop=(kc == C - 1))
                        mm.then_inc(mm_done, 2)
                        qk_sums(2 * hp + 1)

                def turn_probs(h):
                    pe.wait_ge(pn_done, l * HEADS + (h + 1))
                    for b in range(3):
                        mm = nc.tensor.transpose(ps[:, 6, b * P:(b + 1) * P], scores[:, b * P:(b + 1) * P], ident)
                    mm.then_inc(tr_done, 1)

                def spread(h):
                    pe.wait_ge(rm_done, l * HEADS + (h + 1))
                    nc.tensor.matmul(ps[:, 4, :], ones[0:2 * HEADS, :], rmask, start=True, stop=True) \
                        .then_inc(bc_done, 1)

                def head_scores(h):
                    pe.wait_ge(qkn_done, l * HEADS + (h + 1))
                    for b in range(2):
                        o = ps[:, 5, b * P:b * P + (b + 1) * P]
                        nc.tensor.matmul(o, Qb[:, h, b * P:(b + 1) * P], Kb[:, h, 0:(b + 1) * P], start=True, stop=False)
                        mm = nc.tensor.matmul(o, ones[0:HEADS, :], dmask[:, 0:(b + 1) * P], start=False, stop=True)
                    mm.then_inc(s_done, 1)

                def head_values(h):
                    pe.wait_ge(pt_done, l * HEADS + (h + 1))
                    if h >= 1:
                        pe.wait_ge(o_done, l * HEADS + h)
                    v = slice(h * P, h * P + P)
                    nc.tensor.matmul(ps[:, 7, 0:T], Vb[:, 0, v], probsT[:, 0:T], start=True, stop=False)
                    nc.tensor.matmul(ps[:, 7, P:T], Vb[:, 1, v], probsT[:, T:T + P], start=False, stop=True) \
                        .then_inc(pv_done, 1)

                def ya_ready(kc):
                    pe.wait_ge(ya_done, l * C + (kc + 1))

                for st in range(HEADS):
                    u = Unit(q, k + 20 + st)
                    src = (part(Hh, T), part(Hl, T)) if st < 4 else (part(Fh, T), part(Fl, T))
                    if st >= 1:
                        turn_probs(st - 1)
                    spread(st)
                    linear(u, *src, T, ready=ya_ready if st == 4 else None, tiles=(0,))
                    if st >= 1:
                        head_values(st - 1)
                    head_scores(st)
                    linear(u, *src, T, tiles=(1,))

                def o_ready(kc):
                    pe.wait_ge(o_done, l * HEADS + (kc + 1))

                for j in range(4):
                    u = Unit(q, k + 28 + 2 * j)
                    if j == 0:
                        turn_probs(HEADS - 1)
                    linear(u, part(Hh, T), part(Hl, T), T, tiles=(0,))
                    if j == 0:
                        head_values(HEADS - 1)
                    linear(u, part(Hh, T), part(Hl, T), T, tiles=(1,))
                    linear(u.later(1), part(Fh, T, 1), part(Fl, T, 1), T, ready=o_ready if j == 0 else None)

                def m_ready(kc):
                    pe.wait_ge(m_done, l * 4 + (kc // 2 + 1))

                for j in range(4):
                    linear(Unit(q, k + 36 + j), part(Hh, T, 1), part(Hl, T, 1), T, ready=m_ready if j == 0 else None)
                    if j >= 1:
                        sums(l * 4 + 2, j - 1, T)
                sums(l * 4 + 2, 3, T)
                ffn(q, K_FFN2, l * 2 + 1, l * 4 + 2, T, FULL_GROUP, LAST_GROUP, l * 4 + 3)

                pe.wait_ge(p_in, l * 16 + 16)
                for i in range(4):
                    mm = nc.tensor.transpose(ps[:, 7, i * P:(i + 1) * P], ptok[:, i % 2, (i // 2) * P:(i // 2 + 1) * P],
                                             ident)
                mm.then_inc(p_turned, 1)
                for j in range(4):
                    u = Unit(q, K_PLE + 2 * j)
                    linear(u, part(Hh, T), part(Hl, T), T, ready=h_ready(l * 4 + 3) if j == 0 else None)
                    if j >= 1:
                        sums(l * 4 + 4, j - 1, T)
                    if j == 0:
                        pe.wait_ge(p_there, l + 1)
                    linear(u.later(1), part(Fh, T, 1), part(Fl, T, 1), T, PLE // P)
                sums(l * 4 + 4, 3, T)

            q = Q_SECOND
            pe.wait_ge(std_done, 9)
            pe.wait_ge(tok_in, 32)
            turn_tokens(ctok, 4)
            pe.wait_ge(turned_out, 8)
            for i in range(4):
                sums(9, i, 512)
            ffn(q, 0, 4, 8, 512, PLAIN_FULL, PLAIN_LAST, 10)
            def taps(j):
                pe.wait_ge(u_done, j + 1)
                if j >= 2:
                    pe.wait_ge(cv_done, j - 1)
                for i in range(PE_TAPS[j]):
                    n, tap = sum(PE_TAPS[:j]) + i, TAPS - PE_TAPS[j] + i
                    pe.wait_ge(diag_there, n + 1)
                    nc.tensor.matmul(two(ps[:, 4 + j % 2, :]), diag[:, n % DIAGS, :], upad[:, j % 2, :, tap:tap + T],
                                     start=(i == 0), stop=(i == PE_TAPS[j] - 1)).then_inc(diag_used, 1)

            def mean_sums(j):
                pe.wait_ge(cv_done, j + 1)
                return nc.tensor.matmul(two(ps[:, 6, :]), ones[:], QK[:, :, j, :], start=(j == 0), stop=(j == C - 1))

            for j in range(C):
                linear(Unit(q, K2_CONV + j), part(Hh, 512), part(Hl, 512), 512, ready=h_ready(9) if j == 0 else None)
                if j >= 1:
                    taps(j - 1)
                if j >= 2:
                    mean_sums(j - 2)
            taps(C - 1)
            mean_sums(C - 2)
            mean_sums(C - 1).then_inc(mu_mm, 1)
            for kc in range(C):
                pe.wait_ge(csq_done, kc + 1)
                nc.tensor.matmul(ps[:, 7, :], ones[:], Tt[:, kc % 2, :], start=(kc == 0), stop=(kc == C - 1)) \
                    .then_inc(var_mm, 1)

            def z_ready(kc):
                pe.wait_ge(z_there, kc + 1)

            for j in range(4):
                linear(Unit(q, K2_PW2 + j), part(Fh, 512), part(Fl, 512), 512, ready=z_ready if j == 0 else None)
                if j >= 1:
                    sums(11, j - 1, 512)
            sums(11, 3, 512)
            ffn(q, K2_FFN2, 5, 10, 512, PLAIN_FULL, PLAIN_LAST, 12)
            ffn(q, K2_L1, 6, 11, 512, PLAIN_FULL, PLAIN_LAST, 13)
            pe.wait_ge(ro_in, 16)

            def rotate(i, src):
                ue = Unit(q, K2_Q + i)
                pe.wait_ge(banks_free[ue.par], ue.read_out())
                if i >= 2:
                    pe.wait_ge(rot_done, i - 1)
                nc.tensor.matmul(two(ps[:, 4 + i % 2, :]), ro[:, RO_ROT:RO_ROT + P], src, start=True, stop=True) \
                    .then_inc(rot_mm, 1)

            def q_tiles(i):
                return Qb[:, 2 * i:2 * i + 2, :]

            for j in range(4):
                linear(Unit(q, K2_Q + j), part(Hh, T), part(Hl, T), T, ready=h_ready(12) if j == 0 else None)
                if j >= 1:
                    rotate(j - 1, q_tiles(j - 1))
            u = Unit(q, K2_KV)
            linear(u, part(Hh, 512), part(Hl, 512), 512)
            rotate(3, q_tiles(3))
            u = u.later(1)
            pe.wait_ge(lo_done, u.lo_done(1))
            pe.wait_ge(banks_free[u.par], u.banks_free())
            for t in range(4):
                tok = slice((t % 2) * P, (t % 2) * P + P)
                o = ps[:, 2 * u.par + t // 2, (t % 2) * T:(t % 2 + 1) * T]
                for kc in range(C):
                    nc.tensor.matmul(o, Hh[:, t // 2, kc, tok], wh[:, u.par, kc, :], start=(kc == 0), stop=False)
                    nc.tensor.matmul(o, Hl[:, t // 2, kc, tok], wh[:, u.par, kc, :], start=False, stop=False)
                    mm = nc.tensor.matmul(o, Hh[:, t // 2, kc, tok], wl[:, u.par, kc, :], start=False,
                                          stop=(kc == C - 1))
            mm.then_inc(mm_done, 2)
            rotate(4, kraw[:, :, 0:T])
            pe.wait_ge(rot_done, 5)
            for kv in range(KVH):
                if kv >= 2:
                    pe.wait_ge(dup_done, kv - 1)
                nc.tensor.matmul(ps[:, 6 + kv % 2, :], ro[:, RO_DUP + P * (kv % 2):RO_DUP + P * (kv % 2 + 1)],
                                 kraw[:, kv // 2, :], start=True, stop=True).then_inc(dup_mm, 1)
            pe.wait_ge(dup_done, KVH)

            def scores2(h):
                half_p = slice(HD * (h % 2), HD * (h % 2) + HD)
                if h >= 2:
                    pe.wait_ge(e2_done, h - 1)
                for b in range(2):
                    mm = nc.tensor.matmul(ps[:, 2 * (h % 2) + b, :], Qb[half_p, h // 2, b * P:(b + 1) * P],
                                          kdup[half_p, h // 4, :], start=True, stop=True)
                mm.then_inc(s2_done, 1)

            def turn_probs2(h):
                pe.wait_ge(pn2_done, h + 1)
                if h >= 1:
                    pe.wait_ge(pt2_done, h)
                for b in range(2):
                    for kb in range(4):
                        mm = nc.tensor.transpose(ps[:, 4 + kb // 2, (kb % 2) * T + b * P:(kb % 2) * T + (b + 1) * P],
                                                 probs2[h % 2][b][:, kb * P:(kb + 1) * P], ident)
                mm.then_inc(tr2_done, 1)

            def head_values2(h):
                pe.wait_ge(pt2_done, h + 1)
                if h % 2 == 0 and h >= 4:
                    pe.wait_ge(o2_done, h // 2 - 1)
                for kb in range(4):
                    o = ps[HD * (h % 2):HD * (h % 2) + HD, 6 + (h // 2) % 2, 0:T]
                    mm = nc.tensor.matmul(o, v2[:, kb, HD * (h // 4):HD * (h // 4) + HD],
                                          probsT2[h % 2][:, kb // 2, (kb % 2) * T:(kb % 2 + 1) * T], start=(kb == 0),
                                          stop=(kb == 3))
                mm.then_inc(pv2_done, 1)

            for back in (1, 2):
                ue = Unit(q, K2_WO - back)
                pe.wait_ge(banks_free[ue.par], ue.read_out())
            scores2(0)
            for i in range(QH + 2):
                if i + 1 < QH:
                    scores2(i + 1)
                if i >= 2:
                    head_values2(i - 2)
                if 1 <= i <= QH:
                    turn_probs2(i - 1)

            def o2_ready(kc):
                pe.wait_ge(o2_done, kc + 1)

            for j in range(4):
                linear(Unit(q, K2_WO + j), part(Fh, T), part(Fl, T), T, ready=o2_ready if j == 0 else None)
                if j >= 1:
                    sums(14, j - 1, T)
            sums(14, 3, T)
            ffn(q, K2_FFN4, 7, 13, T, PLAIN_FULL, PLAIN_LAST, 15)
            for n in range(2):
                for b in range(2):
                    for i in range(4):
                        kc = 4 * b + i
                        pe.wait_ge(final_done, kc + 1)
                        mm = nc.tensor.transpose(ps[:, 4 + 2 * n + b, i * P:(i + 1) * P],
                                                 Xx[:, kc, n * P:(n + 1) * P], ident)
                    mm.then_inc(out_mm, 1)

        @block.scalar
        def _(act):
            def hi(u, t, mod=False, other=False):
                if u.last():
                    return
                if t == 0:
                    act.wait_ge(raw_full[u.slot], u.raw_full())
                act.wait_ge(mm_done, u.split_free(1 if other else t))
                nc.scalar.activation(tile_of(wh[:, u.par], t, mod), tile_of(raw[:, u.slot], t, mod), ACT.Copy) \
                    .then_inc(hi_done, 1)

            def tanh_table():
                nc.scalar.activation(eps[:, 1:2], eps[:, 0:1], ACT.Tanh)

            def root_table():
                nc.scalar.activation(eps[:, 1:2], eps[:, 0:1], ACT.Sqrt)

            def stream(u):
                hi(u.later(2), 0)
                hi(u.later(2), 1)

            def squares(norm_i, i, n, u=None):
                if i == 3:
                    root_table()
                if u is not None:
                    act.wait_ge(banks_free[u.par], u.read_out())
                if n == T:
                    if i >= 2:
                        act.wait_ge(ss_done, norm_i * 4 + (i - 1))
                    ins = nc.scalar.activation(two(Tt[:, i % 2, :]), Xx[:, 2 * i:2 * i + 2, :], ACT.Square)
                else:
                    if i >= 1:
                        act.wait_ge(ss_done, norm_i * 4 + i)
                    nc.scalar.activation(two(Tt[:, 0, :]), Xx[:, 2 * i:2 * i + 2, :], ACT.Square)
                    ins = nc.scalar.activation(two(Tt[:, 1, :]), Xc[:, 2 * i:2 * i + 2, :], ACT.Square)
                ins.then_inc(sq_done, 1)

            def norm(norm_i, n, with_h=None, shift=None, late=None):
                act.wait_ge(ss_done, norm_i * 4 + 4)
                nc.scalar.activation(Rr[:, 0:n], ps[:, 4, 0:n], ACT.Sqrt, bias=eps[:, 0:1], scale=1.0 / D) \
                    .then_inc(std_done, 1)
                if with_h is None:
                    tanh_table()
                    return
                for kc in range(C):
                    act.wait_ge(hp_done, with_h * C + (kc + 1))
                    for s in range(n // T):
                        src = Pp[:, kc % 2, s * T:(s + 1) * T]
                        if shift is None:
                            ins = nc.scalar.activation(Hh[:, s, kc, :], src, ACT.Copy)
                        else:
                            ins = nc.scalar.activation(Hh[:, s, kc, :], src, ACT.Identity, bias=shift(kc, s))
                    ins.then_inc(hh_done, 1)
                tanh_table()
                hi(late, 1)

            def ffn(q, k, fi, n, order, last, after):
                for g, units in groups_of(act, q, k, order, last):
                    for j, (kind, i, u) in enumerate(units):
                        mod = j + 2 < len(units) and units[j + 2][0] == "A"
                        hi(u.later(2), 0, mod, mod or kind == "A")
                        if kind == "G":
                            act.wait_ge(mm_done, u.mm_done(0))
                            nc.scalar.activation(Tt[:, u.par, 0:n], bank(u, 0, n), ACT.Tanh, scale=0.5) \
                                .then_inc(tanh_done, 1)
                        if kind == "O" and isinstance(g, int):
                            squares(after, i, n, u)
                        if not isinstance(g, int) or j < len(units) - 1:
                            hi(u.later(2), 1, mod, mod or kind == "A")
                        if kind == "A":
                            act.wait_ge(mm_done, u.mm_done(1))
                            nc.scalar.activation(Pp[0:4, u.par, T:2 * T], ps[0:4, 2 * u.par, 0:256], ACT.Copy) \
                                .then_inc(banks_free[u.par], 1)
                        if kind == "G":
                            act.wait_ge(banks_free[u.par], u.read_out())
                            dst = Fh[:, 0, i, :] if n == T else Fh[:, 0:2, i, :]
                            src = Pp[:, u.par, 0:n] if n == T else two(Pp[:, u.par, :])
                            nc.scalar.activation(dst, src, ACT.Copy).then_inc(fh_done, 1)

            act.wait_ge(eps_there, 1)
            act.wait_ge(par_there, 1)
            nc.scalar.activation(tiny[:, 0:16], tiny[:, 16:32], ACT.Exp, scale=-1.0).then_inc(lam_exp, 1)
            nc.scalar.activation(tiny[:, 32:48], par[:, 2, R_C:R_C + 16], ACT.Tanh, scale=0.5).then_inc(c_tanh, 1)
            act.wait_ge(c_prod, 1)
            nc.scalar.activation(cs[:, :, 0:2], Ss[:, 0:16].rearrange("p (s c) -> p c s", s=2), ACT.Copy) \
                .then_inc(c_hi, 1)
            hi(Unit(0, 0), 0)
            hi(Unit(0, 0), 1)
            hi(Unit(0, 1), 0)
            act.wait_ge(x_there, 1)
            for i in range(4):
                squares(0, i, T)

            with act.Fori(0, DEPTH) as l:
                q = l * Q_LAYER
                act.wait_ge(cur_there, l + 1)
                norm(l * 4, T, l * 4, late=Unit(q, 1))
                ffn(q, 0, l * 2, T, FULL_GROUP, LAST_GROUP, l * 4 + 1)

                k = K_MIX
                norm(l * 4 + 1, T, l * 4 + 1, late=Unit(q, k + 1))
                for j in range(4):
                    stream(Unit(q, k + j))
                for j in range(4):
                    u = Unit(q, k + 4 + j)
                    hi(u.later(2), 0)
                    act.wait_ge(mm_done, u.mm_done(1))
                    nc.scalar.activation(two(Tt[:, u.par, :]), pair(u), ACT.Square).then_inc(gelu_sq, 1)
                    hi(u.later(2), 1)
                    act.wait_ge(gelu_arg, l * 4 + (j + 1))
                    nc.scalar.activation(Tt[:, u.par, :], Pp[:, u.par, :], ACT.Tanh, scale=GELU_C) \
                        .then_inc(gelu_tanh, 1)
                for i in range(12):
                    u = Unit(q, k + 8 + i)
                    hp, what = i // 3, i % 3
                    if what < 2:
                        j = 2 * hp + what
                        act.wait_ge(rg_mm, l * C + (j + 2))
                        if j >= 1:
                            act.wait_ge(la_done, l * C + j)
                        nc.scalar.activation(Rr[:, 0:T], ps[:, 6 + j % 2, 0:T], ACT.Tanh, scale=0.5,
                                             bias=half[:, R_BA + j:R_BA + j + 1])
                        nc.scalar.activation(Rr[:, T:2 * T], ps[:, 6 + j % 2, T:2 * T], ACT.Tanh, scale=0.5,
                                             bias=half[:, R_BX + j:R_BX + j + 1]).then_inc(rg_tanh, 1)
                        hi(u.later(2), 0)
                        act.wait_ge(la_done, l * C + (j + 1))
                        nc.scalar.activation(decay[:, j, :], Ss[:, 0:T], ACT.Exp)
                        nc.scalar.activation(Pp[:, j % 2, 0:T], Ss[:, 0:T], ACT.Tanh).then_inc(rg_exp, 1)
                        act.wait_ge(mm_done, u.mm_done(1))
                        if j >= 2:
                            act.wait_ge(qk_ss, l * 8 + (j - 1))
                        nc.scalar.activation(two(Tt[:, j % 2, :]), pair(u), ACT.Square).then_inc(qk_sq, 1)
                        hi(u.later(2), 1)
                    else:
                        hi(u.later(2), 0)
                        if hp == 0:
                            act.wait_ge(f_in, l + 1)
                            nc.scalar.activation(Ss[0:HEADS, T:2 * T], Ss[0:HEADS, 0:T], ACT.Abs).then_inc(f_abs, 1)
                            act.wait_ge(f_abs, l * 2 + 1)
                            nc.scalar.activation(Ss[0:HEADS, T:2 * T], Ss[0:HEADS, T:2 * T], ACT.Exp, scale=-1.0) \
                                .then_inc(f_abs, 1)
                        hi(u.later(2), 1)
                act.wait_ge(qk_ss, l * 8 + 8)
                nc.scalar.activation(rqk[:], ps[0:2 * HEADS, 5, 0:T], ACT.Sqrt, bias=eps[0:2 * HEADS, 0:1],
                                     scale=1.0 / P).then_inc(qk_std, 1)
                act.wait_ge(keep_done, l * C + C)
                nc.scalar.activation(keep[:], keep[:], ACT.Sqrt, scale=-1.0).then_inc(root_done, 1)
                tanh_table()

                def copy_probs(h):
                    act.wait_ge(tr_done, l * HEADS + (h + 1))
                    nc.scalar.activation(probsT, ps[:, 6, 0:384], ACT.Copy).then_inc(pt_done, 1)

                def head_out(h):
                    act.wait_ge(pv_done, l * HEADS + (h + 1))
                    nc.scalar.activation(Fh[:, 1, h, :], ps[:, 7, 0:T], ACT.Copy).then_inc(oh_done, 1)

                def head_exp(h):
                    act.wait_ge(nmax_done, l * HEADS + (h + 1))
                    for b, sl in enumerate((slice(0, P), slice(P, 3 * P))):
                        ins = nc.scalar.activation(scores[:, sl], scores[:, sl], ACT.Exp, bias=tiny[:, b:b + 1],
                                                   accum_out=tiny[:, 2 + b:3 + b])
                    ins.then_inc(exp_done, 1)

                for st in range(HEADS):
                    u = Unit(q, k + 20 + st)
                    if st >= 1:
                        copy_probs(st - 1)
                    hi(u.later(2), 0)
                    if st >= 1:
                        head_out(st - 1)
                    head_exp(st)
                    if st < 4:
                        for j in (2 * st, 2 * st + 1):
                            act.wait_ge(y_done, l * C + (j + 1))
                            nc.scalar.activation(Fh[:, 0, j, :], Pp[:, j % 2, T:2 * T], ACT.Copy).then_inc(yh_done, 1)
                    hi(u.later(2), 1)
                    if st < 4:
                        act.wait_ge(mm_done, u.mm_done(1))
                        for t in range(2):
                            r = R_MERGE + 2 * st + t
                            ins = nc.scalar.activation(gateA[:, 2 * st + t, :], bank(u, t, T), ACT.Tanh, scale=0.5,
                                                       bias=half[:, r:r + 1])
                        ins.then_inc(banks_free[u.par], 1)
                for j in range(4):
                    u = Unit(q, k + 28 + 2 * j)
                    if j == 0:
                        copy_probs(HEADS - 1)
                    hi(u.later(2), 0)
                    if j == 0:
                        head_out(HEADS - 1)
                    hi(u.later(2), 1)
                    act.wait_ge(mm_done, u.mm_done(1))
                    for t in range(2):
                        r = R_MERGE + C + 2 * j + t
                        ins = nc.scalar.activation(Tt[:, j % 2, t * T:(t + 1) * T], bank(u, t, T), ACT.Tanh, scale=0.5,
                                                   bias=half[:, r:r + 1])
                    ins.then_inc(banks_free[u.par], 1)
                    u = u.later(1)
                    hi(u.later(2), 0)
                    hi(u.later(2), 1)
                    act.wait_ge(mp_done, l * 4 + (j + 1))
                    nc.scalar.activation(Hh[:, 1, 2 * j:2 * j + 2, :], two(Pp[:, j % 2, :]), ACT.Copy) \
                        .then_inc(mh_done, 1)
                for j in range(4):
                    u = Unit(q, k + 36 + j)
                    hi(u.later(2), 0)
                    squares(l * 4 + 2, j, T, u)
                    if j < 3:
                        hi(u.later(2), 1)

                norm(l * 4 + 2, T, l * 4 + 2, late=Unit(q, K_FFN2 + 1))
                ffn(q, K_FFN2, l * 2 + 1, T, FULL_GROUP, LAST_GROUP, l * 4 + 3)
                norm(l * 4 + 3, T, l * 4 + 3, late=Unit(q, K_PLE + 1))
                act.wait_ge(p_turned, l + 1)
                nc.scalar.activation(Fh[:, 1, 0:2, :], two(ps[:, 7, :]), ACT.Copy).then_inc(pth_done, 1)
                for j in range(4):
                    u = Unit(q, K_PLE + 2 * j)
                    hi(u.later(2), 0)
                    hi(u.later(2), 1)
                    act.wait_ge(mm_done, u.mm_done(1))
                    if j >= 2:
                        act.wait_ge(ss_done, (l * 4 + 4) * 4 + (j - 1))
                    for t in range(2):
                        r = R_PLEB + 2 * j + t
                        ins = nc.scalar.activation(Tt[:, j % 2, t * T:(t + 1) * T], bank(u, t, T), ACT.Tanh, scale=0.5,
                                                   bias=half[:, r:r + 1])
                    ins.then_inc(banks_free[u.par], 1)
                    u = u.later(1)
                    hi(u.later(2), 0)
                    squares(l * 4 + 4, j, T, u)
                    if j < 3:
                        hi(u.later(2), 1)

            q = Q_SECOND

            def shift(l, i):
                return lambda kc, s: MOD[:, l, (3 * i) * C + kc, s:s + 1]

            norm(8, T)
            act.wait_ge(x_normed, 1)
            for i in range(4):
                squares(9, i, 512)
            act.wait_ge(mod_there, 1)
            norm(9, 512, 8, shift(0, 0), late=Unit(q, 1))
            ffn(q, 0, 4, 512, PLAIN_FULL, PLAIN_LAST, 10)
            norm(10, 512, 9, shift(0, 1), late=Unit(q, K2_CONV + 1))
            def tap_column(tap, j):
                return par[:, 3 + tap // 16, (tap % 16) * 8 + j:(tap % 16) * 8 + j + 1]

            for j in range(C):
                u = Unit(q, K2_CONV + j)
                hi(u.later(2), 0)
                act.wait_ge(mm_done, u.mm_done(1))
                if j >= 1:
                    act.wait_ge(u_done, j)
                nc.scalar.activation(Ss[:], bank(u, 0), ACT.Identity, bias=par[:, 2, R_PW1B + j:R_PW1B + j + 1])
                nc.scalar.activation(Tt[:, u.par, :], bank(u, 1), ACT.Tanh, scale=0.5, bias=tiny[:, 40 + j:41 + j]) \
                    .then_inc(banks_free[u.par], 1)
                hi(u.later(2), 1)
                for i in range(PE_TAPS[j]):
                    n, tap = sum(PE_TAPS[:j]) + i, TAPS - PE_TAPS[j] + i
                    if n >= DIAGS:
                        act.wait_ge(diag_used, n - DIAGS + 1)
                    nc.scalar.activation(diag[:, n % DIAGS, :], ident, ACT.Copy, scale=tap_column(tap, j)) \
                        .then_inc(diag_there, 1)
            for kc in range(C):
                act.wait_ge(cen_done, kc + 1)
                if kc == C - 1:
                    root_table()
                if kc >= 2:
                    act.wait_ge(var_mm, kc - 1)
                nc.scalar.activation(two(Tt[:, kc % 2, :]), QK[:, :, kc, :], ACT.Square).then_inc(csq_done, 1)
            act.wait_ge(var_mm, C)
            nc.scalar.activation(Rr[:], ps[:, 7, :], ACT.Sqrt, bias=eps[:, 0:1], scale=1.0 / D).then_inc(cstd_done, 1)
            tanh_table()

            def z_high(kc):
                act.wait_ge(zp_done, kc + 1)
                nc.scalar.activation(Fh[:, 0:2, kc, :], two(Pp[:, kc % 2, :]), ACT.Copy).then_inc(zh_done, 1)

            for kc in range(C):
                act.wait_ge(z_done, kc + 1)
                if kc >= 2:
                    act.wait_ge(zp_done, kc - 1)
                nc.scalar.activation(two(Tt[:, kc % 2, :]), QK[:, :, kc, :], ACT.Tanh, scale=tiny[:, kc:kc + 1],
                                     bias=tiny[:, 8 + kc:9 + kc])
                nc.scalar.activation(two(scaled[:, kc % 4, :]), QK[:, :, kc, :], ACT.Identity,
                                     scale=par[:, 2, R_LNG + kc:R_LNG + kc + 1],
                                     bias=par[:, 2, R_LNB + kc:R_LNB + kc + 1]).then_inc(zt_done, 1)
                if kc >= 1:
                    z_high(kc - 1)
            z_high(C - 1)

            def adding_units(k, n, after):
                for j in range(4):
                    u = Unit(q, k + j)
                    hi(u.later(2), 0)
                    squares(after, j, n, u)
                    if j < 3:
                        hi(u.later(2), 1)

            adding_units(K2_PW2, 512, 11)
            norm(11, 512, 10, shift(0, 2), late=Unit(q, K2_FFN2 + 1))
            ffn(q, K2_FFN2, 5, 512, PLAIN_FULL, PLAIN_LAST, 12)
            act.wait_ge(mod_there, 2)
            norm(12, 512, 11, shift(1, 0), late=Unit(q, K2_L1 + 1))
            ffn(q, K2_L1, 6, 512, PLAIN_FULL, PLAIN_LAST, 13)
            norm(13, 512, 12, shift(1, 1), late=Unit(q, K2_Q + 1))
            for j in range(6):
                stream(Unit(q, K2_Q + j))
            for kv in range(KVH):
                act.wait_ge(dup_mm, kv + 1)
                nc.scalar.activation(kdup[:, kv, :], ps[:, 6 + kv % 2, :], ACT.Copy).then_inc(dup_done, 1)

            def head2_out(tile):
                act.wait_ge(pv2_done, 2 * tile + 2)
                nc.scalar.activation(Fh[:, 0, tile, :], ps[:, 6 + tile % 2, 0:T], ACT.Copy).then_inc(oh2_done, 1)

            def exp2(h):
                act.wait_ge(nm2_done, h + 1)
                c = 8 * (h % 2)
                nc.scalar.activation(tiny[:, c + 4:c + 6], tiny[:, c + 4:c + 6], ACT.Exp)
                for b in range(2):
                    ins = nc.scalar.activation(probs2[h % 2][b], ps[:, 2 * (h % 2) + b, :], ACT.Exp,
                                               bias=tiny[:, c + b:c + b + 1], accum_out=tiny[:, c + 2 + b:c + 3 + b])
                ins.then_inc(e2_done, 1)

            def normalise2(h):
                act.wait_ge(r2_done, h + 1)
                c = 8 * (h % 2)
                for b in range(2):
                    p = probs2[h % 2][b]
                    ins = nc.scalar.activation(p, p, ACT.Copy, scale=tiny[:, c + 6 + b:c + 7 + b])
                ins.then_inc(pn2_done, 1)

            def copy_probs2(h):
                act.wait_ge(tr2_done, h + 1)
                for i in range(2):
                    ins = nc.scalar.activation(probsT2[h % 2][:, i, :], ps[:, 4 + i, :], ACT.Copy)
                ins.then_inc(pt2_done, 1)

            for i in range(QH + 2):
                if i >= 2:
                    copy_probs2(i - 2)
                if 1 <= i <= QH:
                    normalise2(i - 1)
                if i < QH:
                    exp2(i)
                if i % 2 == 0 and i >= 4:
                    head2_out(i // 2 - 2)
            head2_out(QH // 2 - 1)
            adding_units(K2_WO, T, 14)
            norm(14, T, 13, shift(1, 2), late=Unit(q, K2_FFN4 + 1))
            ffn(q, K2_FFN4, 7, T, PLAIN_FULL, PLAIN_LAST, 15)
            norm(15, T)
            for n in range(2):
                for b in range(2):
                    act.wait_ge(out_mm, 2 * n + b + 1)
                    nc.scalar.activation(otok[:, n, 512 * b:512 * (b + 1)], ps[:, 4 + 2 * n + b, :], ACT.Copy) \
                        .then_inc(out_copied, 1)

        @block.vector
        def _(dve):
            dve.sem_inc(lo_done, 8)
            dve.sem_inc(banks_free[0], 1)
            dve.sem_inc(banks_free[1], 1)
            V = nc.vector

            def stt(o, in0, scalar, in1, op0, op1):
                return V.scalar_tensor_tensor(out=o, in0=in0, scalar=scalar, in1=in1, op0=op0, op1=op1)

            def lo(u, t, mod=False):
                if u.last():
                    return
                dve.wait_ge(hi_done, u.hi_done(t))
                V.tensor_tensor(tile_of(wl[:, u.par], t, mod), tile_of(raw[:, u.slot], t, mod),
                                tile_of(wh[:, u.par], t, mod).bitcast(F32), ALU.subtract).then_inc(lo_done, 1)

            def stream(u):
                lo(u.later(2), 0)
                lo(u.later(2), 1)

            def rms(norm_i, n):
                dve.wait_ge(std_done, norm_i + 1)
                V.reciprocal(Rr[:, 0:n], Rr[:, 0:n])
                dve.drain()

            def norm(norm_i, n, hn, gain, shift=None, late=None):
                rms(norm_i, n)

                def product(kc):
                    for s in range(n // T):
                        x = (Xx, Xc)[s]
                        ins = stt(Pp[:, kc % 2, s * T:(s + 1) * T], x[:, kc, :], gain(kc, s), Rr[:, s * T:(s + 1) * T],
                                  ALU.mult, ALU.mult)
                    ins.then_inc(hp_done, 1)

                product(0)
                product(1)
                for kc in range(C):
                    dve.wait_ge(hh_done, hn * C + (kc + 1))
                    for s in range(n // T):
                        p, h = Pp[:, kc % 2, s * T:(s + 1) * T], Hh[:, s, kc, :].bitcast(F32)
                        if shift is None:
                            ins = V.tensor_tensor(Hl[:, s, kc, :], p, h, ALU.subtract)
                        else:
                            ins = stt(Hl[:, s, kc, :], p, shift(kc, s), h, ALU.add, ALU.subtract)
                    ins.then_inc(h_done, 1)
                    if kc + 2 < C:
                        dve.drain()
                        product(kc + 2)
                lo(late, 1)

            def keep_modulation(l, idx, i):
                dve.wait_ge(mod_turned, l * ADA_UNITS + (idx + 1))
                V.tensor_scalar(MOD[:, bass.ds(l, 1), bass.ds(idx * 2, 2), :].rearrange("p l t s -> p (l t) s"),
                                ps[:, 5 + i % 2, 0:4].rearrange("p (t s) -> p t s", t=2), 1.0, None,
                                ALU.mult)

            def ffn(q, k, fi, n, order, last, gate=None, ada=None):
                for g, units in groups_of(dve, q, k, order, last):
                    for j, (kind, i, u) in enumerate(units):
                        mod = j + 2 < len(units) and units[j + 2][0] == "A"
                        lo(u.later(2), 0, mod)
                        if j >= 2 and units[j - 2][0] == "A":
                            keep_modulation(ada[0], ada_index(ada[1], g, units[j - 2][1]), units[j - 2][1])
                        if kind == "A":
                            pass
                        elif kind == "G":
                            done = fi * FC + g * 8
                            dve.wait_ge(tanh_done, done + (i + 1))
                            stt(Ss[:, 0:n], Tt[:, u.par, 0:n], 1.0, bank(u, 0, n), ALU.add, ALU.mult)
                            dve.drain()
                            dve.wait_ge(mm_done, u.mm_done(1))
                            V.tensor_tensor(Pp[:, u.par, 0:n], Ss[:, 0:n], bank(u, 1, n), ALU.mult) \
                                .then_inc(banks_free[u.par], 1)
                        elif gate is None:
                            dve.wait_ge(mm_done, u.mm_done(1))
                            x = Xx[:, 2 * i:2 * i + 2, :]
                            stt(x, pair(u), 0.25, x, ALU.mult, ALU.add).then_inc(banks_free[u.par], 1)
                        else:
                            dve.wait_ge(mm_done, u.mm_done(1))
                            add_gated(u, i, n, gate)
                        if not isinstance(g, int) or j < len(units) - 1:
                            lo(u.later(2), 1, mod)
                        if kind == "G":
                            dve.wait_ge(fh_done, done + (i + 1))
                            if n == T:
                                o, p, h = Fl[:, 0, i, :], Pp[:, u.par, 0:n], Fh[:, 0, i, :]
                            else:
                                o, p, h = Fl[:, 0:2, i, :], two(Pp[:, u.par, :]), Fh[:, 0:2, i, :]
                            V.tensor_tensor(o, p, h.bitcast(F32), ALU.subtract).then_inc(f_done, 1)

            def add_gated(u, i, n, gate):
                for t in range(2):
                    kc = 2 * i + t
                    for s in range(n // T):
                        x = (Xx, Xc)[s][:, kc, :]
                        ins = stt(x, ps[:, 2 * u.par + t, s * T:(s + 1) * T], gate(kc, s), x, ALU.mult, ALU.add)
                ins.then_inc(banks_free[u.par], 1)

            def log1p(o, e, z2, acc):
                V.tensor_scalar(acc, e, 2.0, None, ALU.add)
                dve.drain()
                V.reciprocal(acc, acc)
                dve.drain()
                V.tensor_tensor(o, e, acc, ALU.mult)
                dve.drain()
                V.tensor_tensor(z2, o, o, ALU.mult)
                dve.drain()
                V.tensor_scalar(acc, z2, 2.0 / 17, None, ALU.mult)
                dve.drain()
                for j in (15, 13, 11, 9, 7, 5, 3):
                    stt(acc, acc, 2.0 / j, z2, ALU.add, ALU.mult)
                    dve.drain()
                stt(o, acc, 2.0, o, ALU.add, ALU.mult)
                dve.drain()

            V.memset(ones[:], 1.0)
            V.memset(eps[:], EPS).then_inc(eps_there, 1)
            dve.drain().then_inc(ones_there, 1)
            dve.wait_ge(turned, 1)
            for i, n in enumerate(PAR_ROWS):
                V.tensor_copy(par[:, i, 0:n], ps[:, i // 4, (i % 4) * P:(i % 4) * P + n])
            dve.wait_ge(sink_mm, 1)
            dve.drain()
            lam = par[:, 0:2, R_LAM:R_LAM + C]
            two8 = [x.rearrange("p (l c) -> p l c", l=2) for x in
                    (tiny[:, 0:16], tiny[:, 16:32], Ss[:, 16:32], Ss[:, 32:48], Ss[:, 48:64])]
            V.tensor_scalar(two8[2], lam, -1.0, None, ALU.mult)
            dve.drain()
            V.tensor_tensor(two8[1], lam, two8[2], ALU.max).then_inc(par_there, 1)
            dve.wait_ge(lam_exp, 1)
            log1p(two8[4], two8[0], two8[3], two8[1])
            stt(two8[4], two8[2], 0.0, two8[4], ALU.max, ALU.add)
            dve.drain()
            V.tensor_scalar(lam, two8[4], -4.0, None, ALU.mult)
            V.tensor_scalar(par[:, 0:2, R_QN:R_QN + 1], par[:, 0:2, R_QN:R_QN + 1], float(P) ** -0.5, None, ALU.mult)
            dve.wait_ge(c_tanh, 1)
            stt(Ss[:, 0:16], tiny[:, 32:48], 1.0, par[:, 2, R_C:R_C + 16], ALU.add, ALU.mult)
            dve.drain()
            V.tensor_scalar(Ss[:, 0:16], Ss[:, 0:16], 0.5, None, ALU.mult).then_inc(c_prod, 1)
            dve.wait_ge(c_hi, 1)
            V.tensor_tensor(cs[:, :, 2:4], Ss[:, 0:16].rearrange("p (s c) -> p c s", s=2), cs[:, :, 0:2].bitcast(F32),
                            ALU.subtract).then_inc(c_there, 1)
            V.tensor_copy(tiny[:, 16:32], ps[:, 7, 0:QH])
            for b in range(4):
                dve.wait_ge(turned, b + 2)
                V.tensor_copy(Xx[:, 2 * b:2 * b + 2, :], two(ps[:, 2 + b, :])).then_inc(turned_out, 1)
            dve.drain().then_inc(x_there, 1)
            lo(Unit(0, 0), 0)
            lo(Unit(0, 0), 1)
            lo(Unit(0, 1), 0)

            def layer_gain(r):
                return lambda kc, s: cur[:, r + kc:r + kc + 1]

            with dve.Fori(0, DEPTH) as l:
                q = l * Q_LAYER
                V.tensor_copy(cur[:], par[:, bass.ds(l, 1), 0:R_LAYER].rearrange("p l f -> p (l f)"))
                V.tensor_copy(tiny[0:HEADS, 12:13], fb[:, bass.ds(l, 1)])
                dve.drain()
                V.tensor_scalar(half[:], cur[:], 0.5, None, ALU.mult).then_inc(cur_there, 1)
                norm(l * 4, T, l * 4, layer_gain(R_FFN1), late=Unit(q, 1))
                ffn(q, 0, l * 2, T, FULL_GROUP, LAST_GROUP, ada=(l, 0))

                k = K_MIX
                norm(l * 4 + 1, T, l * 4 + 1, layer_gain(R_MIX), late=Unit(q, k + 1))
                keep_modulation(l, ada_index(0, 2, 1), 1)
                for j in range(4):
                    u = Unit(q, k + j)
                    lo(u.later(2), 0)
                    dve.wait_ge(mm_done, u.mm_done(1))
                    for s in range(4):
                        for t in range(2):
                            kc = 2 * j + t
                            tap = cur[:, R_CONV + 8 * (3 - s) + kc:R_CONV + 8 * (3 - s) + kc + 1]
                            if s == 0:
                                ins = V.tensor_scalar(Xc[:, kc, :], bank(u, t, T), tap,
                                                      cur[:, R_CONVB + kc:R_CONVB + kc + 1], ALU.mult, ALU.add)
                            else:
                                ins = stt(Xc[:, kc, s:T], bank(u, t, T - s), tap, Xc[:, kc, s:T], ALU.mult, ALU.add)
                        if s < 3:
                            dve.drain()
                    ins.then_inc(banks_free[u.par], 1)
                    lo(u.later(2), 1)
                for j in range(4):
                    u = Unit(q, k + 4 + j)
                    lo(u.later(2), 0)
                    dve.wait_ge(gelu_sq, l * 4 + (j + 1))
                    V.tensor_scalar(Ss[:], Tt[:, u.par, :], GELU_A, 1.0, ALU.mult, ALU.add)
                    dve.drain()
                    V.tensor_tensor(two(Pp[:, u.par, :]), two(Ss[:]), pair(u), ALU.mult).then_inc(gelu_arg, 1)
                    lo(u.later(2), 1)
                    dve.wait_ge(gelu_tanh, l * 4 + (j + 1))
                    stt(Gb[:, 2 * j:2 * j + 2, :], two(Tt[:, u.par, :]), 1.0, pair(u), ALU.add, ALU.mult) \
                        .then_inc(banks_free[u.par], 1)
                for i in range(12):
                    u = Unit(q, k + 8 + i)
                    hp, what = i // 3, i % 3
                    if what < 2:
                        j = 2 * hp + what
                        dve.wait_ge(rg_tanh, l * C + (j + 1))
                        stt(Xc[:, j, :], Rr[:, T:2 * T], 1.0, Xc[:, j, :], ALU.add, ALU.mult)
                        V.tensor_scalar(Ss[:, 0:T], Rr[:, 0:T], 1.0, cur[:, R_LAM + j:R_LAM + j + 1], ALU.add, ALU.mult) \
                            .then_inc(la_done, 1)
                        lo(u.later(2), 0)
                        dve.wait_ge(rg_exp, l * C + (j + 1))
                        V.tensor_tensor(Ss[:, T:2 * T], decay[:, j, :], decay[:, j, :], ALU.mult)
                        dve.drain()
                        stt(keep[:, j, :], Ss[:, T:2 * T], 1.0, Pp[:, j % 2, 0:T], ALU.add, ALU.mult) \
                            .then_inc(keep_done, 1)
                        dve.wait_ge(qk_sq, l * 8 + (j + 1))
                        dst = (Qb, Kb)[what][:, 2 * hp:2 * hp + 2, :]
                        V.tensor_scalar(dst, pair(u), cur[:, R_QN + what:R_QN + what + 1], None, ALU.mult) \
                            .then_inc(banks_free[u.par], 1)
                        lo(u.later(2), 1)
                    else:
                        lo(u.later(2), 0)
                        if hp == 0:
                            z, e = Ss[0:HEADS, 0:T], Ss[0:HEADS, T:2 * T]
                            a, b = Pp[0:HEADS, 0, T:2 * T], Pp[0:HEADS, 1, T:2 * T]
                            dve.wait_ge(f_mm, l + 2)
                            V.tensor_scalar(z, ps[0:HEADS, 4, 0:T], tiny[0:HEADS, 12:13], None, ALU.add).then_inc(f_in, 1)
                            dve.wait_ge(f_abs, l * 2 + 2)
                            log1p(a, e, b, dmask[:])
                            stt(a, z, 0.0, a, ALU.min, ALU.subtract)
                            V.memset(e, 1.0)
                            dve.drain()
                            V.tensor_tensor_scan(z, e, a, 0.0, ALU.mult, ALU.add)
                            dve.drain()
                            V.tensor_scalar(dneg[:], z, -1.0, None, ALU.mult)
                            dve.drain()
                        dve.wait_ge(mm_done, u.mm_done(1))
                        V.tensor_copy(Vb[:, :, T * hp:T * (hp + 1)], pair(u)).then_inc(banks_free[u.par], 1)
                        lo(u.later(2), 1)
                dve.wait_ge(qk_std, l + 1)
                V.reciprocal(rqk[:], rqk[:])
                dve.drain()

                def masks(h):
                    V.tensor_scalar(rmask[:, 0:T], rqk[:], ident[0:2 * HEADS, h:h + 1], None, ALU.mult)
                    V.tensor_scalar(rmask[:, T:2 * T], rqk[:], ident[0:2 * HEADS, HEADS + h:HEADS + h + 1], None,
                                    ALU.mult)
                    V.tensor_scalar(dmask[:], dneg[:], ident[0:HEADS, h:h + 1], None, ALU.mult).then_inc(rm_done, 1)

                def low_out(h):
                    dve.wait_ge(oh_done, l * HEADS + (h + 1))
                    V.tensor_tensor(Fl[:, 1, h, :], ps[:, 7, 0:T], Fh[:, 1, h, :].bitcast(F32), ALU.subtract) \
                        .then_inc(o_done, 1)

                masks(0)
                for st in range(HEADS):
                    u = Unit(q, k + 20 + st)
                    dve.wait_ge(bc_done, l * HEADS + (st + 1))
                    V.tensor_tensor(Qb[:, st, :], Qb[:, st, :], ps[:, 4, 0:T], ALU.mult)
                    V.tensor_tensor(Kb[:, st, :], Kb[:, st, :], ps[:, 4, T:2 * T], ALU.mult).then_inc(qkn_done, 1)
                    lo(u.later(2), 0)
                    dve.wait_ge(s_done, l * HEADS + (st + 1))
                    V.tensor_tensor(scores[:, 0:P], ps[:, 5, 0:P], low, ALU.add)
                    V.tensor_copy(scores[:, P:2 * P], ps[:, 5, P:2 * P])
                    V.tensor_tensor(scores[:, 2 * P:3 * P], ps[:, 5, 2 * P:3 * P], low, ALU.add)
                    dve.drain()
                    V.tensor_reduce(tiny[:, 6:7], scores[:, 0:P], AX_X, ALU.max)
                    V.tensor_reduce(tiny[:, 7:8], scores[:, P:3 * P], AX_X, ALU.max)
                    dve.drain()
                    V.tensor_scalar(tiny[:, 0:2], tiny[:, 6:8], -1.0, None, ALU.mult).then_inc(nmax_done, 1)
                    if st >= 1:
                        low_out(st - 1)
                    if st < 4:
                        if st == 0:
                            dve.wait_ge(root_done, l + 1)
                        two_chunks = (2 * st, 2 * st + 1)
                        for j in two_chunks:
                            stt(Xc[:, j, :], Xc[:, j, :], 0.5, keep[:, j, :], ALU.mult, ALU.mult)
                        dve.drain()
                        for j in two_chunks:
                            V.tensor_tensor_scan(Pp[:, j % 2, 0:T], decay[:, j, :], Xc[:, j, :], 0.0, ALU.mult, ALU.add)
                        dve.drain()
                        for j in two_chunks:
                            V.tensor_tensor(Pp[:, j % 2, T:2 * T], Pp[:, j % 2, 0:T], Gb[:, j, :], ALU.mult) \
                                .then_inc(y_done, 1)
                    dve.wait_ge(exp_done, l * HEADS + (st + 1))
                    V.reciprocal(tiny[:, 4:6], tiny[:, 2:4])
                    dve.drain()
                    V.tensor_scalar(scores[:, 0:P], scores[:, 0:P], tiny[:, 4:5], None, ALU.mult)
                    V.tensor_scalar(scores[:, P:3 * P], scores[:, P:3 * P], tiny[:, 5:6], None, ALU.mult) \
                        .then_inc(pn_done, 1)
                    if st < 4:
                        for j in two_chunks:
                            dve.wait_ge(yh_done, l * C + (j + 1))
                            V.tensor_tensor(Fl[:, 0, j, :], Pp[:, j % 2, T:2 * T], Fh[:, 0, j, :].bitcast(F32),
                                            ALU.subtract).then_inc(ya_done, 1)
                    if st + 1 < HEADS:
                        masks(st + 1)
                    lo(u.later(2), 1)
                    if st >= 4:
                        dve.wait_ge(mm_done, u.mm_done(1))
                        ga = gateA[:, 2 * (st - 4):2 * (st - 4) + 2, :]
                        stt(ga, ga, 1.0, pair(u), ALU.add, ALU.mult).then_inc(banks_free[u.par], 1)
                for j in range(4):
                    u = Unit(q, k + 28 + 2 * j)
                    lo(u.later(2), 0)
                    if j == 0:
                        low_out(HEADS - 1)
                    lo(u.later(2), 1)
                    u = u.later(1)
                    lo(u.later(2), 0)
                    dve.wait_ge(mm_done, u.mm_done(1))
                    ue = u.later(-1)
                    dve.wait_ge(banks_free[ue.par], ue.read_out())
                    stt(two(Ss[:]), two(Tt[:, j % 2, :]), 1.0, pair(u), ALU.add, ALU.mult) \
                        .then_inc(banks_free[u.par], 1)
                    dve.drain()
                    stt(two(Pp[:, j % 2, :]), two(Ss[:]), 2.0, gateA[:, 2 * j:2 * j + 2, :], ALU.mult, ALU.add) \
                        .then_inc(mp_done, 1)
                    lo(u.later(2), 1)
                    dve.wait_ge(mh_done, l * 4 + (j + 1))
                    V.tensor_tensor(Hl[:, 1, 2 * j:2 * j + 2, :], two(Pp[:, j % 2, :]),
                                    Hh[:, 1, 2 * j:2 * j + 2, :].bitcast(F32), ALU.subtract).then_inc(m_done, 1)
                for j in range(4):
                    u = Unit(q, k + 36 + j)
                    lo(u.later(2), 0)
                    dve.wait_ge(mm_done, u.mm_done(1))
                    x = Xx[:, 2 * j:2 * j + 2, :]
                    stt(x, pair(u), 0.25, x, ALU.mult, ALU.add).then_inc(banks_free[u.par], 1)
                    if j < 3:
                        lo(u.later(2), 1)

                norm(l * 4 + 2, T, l * 4 + 2, layer_gain(R_FFN2), late=Unit(q, K_FFN2 + 1))
                ffn(q, K_FFN2, l * 2 + 1, T, FULL_GROUP, LAST_GROUP, ada=(l, 1))
                norm(l * 4 + 3, T, l * 4 + 3, layer_gain(R_PLE), late=Unit(q, K_PLE + 1))
                keep_modulation(l, ada_index(1, 2, 1), 1)
                dve.wait_ge(pth_done, l + 1)
                V.tensor_tensor(Fl[:, 1, 0:2, :], two(ps[:, 7, :]), Fh[:, 1, 0:2, :].bitcast(F32), ALU.subtract) \
                    .then_inc(p_there, 1)
                for j in range(4):
                    u = Unit(q, K_PLE + 2 * j)
                    stream(u)
                    ue, u = u, u.later(1)
                    lo(u.later(2), 0)
                    dve.wait_ge(banks_free[ue.par], ue.read_out())
                    dve.wait_ge(mm_done, u.mm_done(1))
                    stt(two(Ss[:]), two(Tt[:, j % 2, :]), 1.0, pair(u), ALU.add, ALU.mult)
                    dve.drain()
                    x = Xx[:, 2 * j:2 * j + 2, :]
                    stt(x, two(Ss[:]), 0.5, x, ALU.mult, ALU.add).then_inc(banks_free[u.par], 1)
                    if j < 3:
                        lo(u.later(2), 1)

            q = Q_SECOND
            rms(8, T)
            for kc in range(C):
                stt(Xx[:, kc, :], Xx[:, kc, :], par[:, 2, R_FINAL + kc:R_FINAL + kc + 1], Rr[:, 0:T], ALU.mult, ALU.mult)
            for b in range(4):
                dve.wait_ge(turned, b + 6)
                V.tensor_copy(Xc[:, 2 * b:2 * b + 2, :], two(ps[:, 4 + b, :])).then_inc(turned_out, 1)
            dve.drain().then_inc(x_normed, 1)

            def layer_consts(l):
                for s in range(2):
                    V.tensor_tensor(MOD[:, l, :, s], MOD[:, l, :, s], par[:, 5 + l, 0:N_MOD * C], ALU.add)
                dve.drain()
                for i in range(3):
                    r = R_NORM + (3 * l + i) * C
                    for s in range(2):
                        stt(S1[:, i, :, s], MOD[:, l, (3 * i + 1) * C:(3 * i + 2) * C, s], 1.0, par[:, 2, r:r + C],
                            ALU.add, ALU.mult)
                    factor = 0.25 if i != 1 else (0.5 if l == 0 else 1.0)
                    V.tensor_scalar(G1[:, i], MOD[:, l, (3 * i + 2) * C:(3 * i + 3) * C, :], factor, None, ALU.mult)
                dve.drain().then_inc(mod_there, 1)

            def gain(i):
                return lambda kc, s: S1[:, i, kc, s:s + 1]

            def gate(i):
                return lambda kc, s: G1[:, i, kc, s:s + 1]

            def shift(l, i):
                return lambda kc, s: MOD[:, l, (3 * i) * C + kc, s:s + 1]

            layer_consts(0)
            V.tensor_scalar(tiny[:, 40:48], par[:, 2, R_PW1B + C:R_PW1B + 2 * C], 0.5, None, ALU.mult)
            V.tensor_scalar(tiny[:, 0:16], par[:, 2, R_LNG:R_LNG + 16], 0.5, None, ALU.mult)
            V.tensor_scalar(par[:, 3, :], par[:, 3, :], 0.5, None, ALU.mult)
            V.tensor_scalar(par[:, 4, 0:PAR_ROWS[4]], par[:, 4, 0:PAR_ROWS[4]], 0.5, None, ALU.mult)
            V.memset(upad[:], 0.0)
            dve.drain()
            norm(9, 512, 8, gain(0), shift(0, 0), Unit(q, 1))
            ffn(q, 0, 4, 512, PLAIN_FULL, PLAIN_LAST, gate(0))
            norm(10, 512, 9, gain(1), shift(0, 1), Unit(q, K2_CONV + 1))
            def add_tap_sums(j):
                dve.wait_ge(diag_used, sum(PE_TAPS[:j + 1]))
                V.tensor_tensor(QK[:, :, j, :], QK[:, :, j, :], two(ps[:, 4 + j % 2, :]), ALU.add).then_inc(cv_done, 1)

            for j in range(C):
                u = Unit(q, K2_CONV + j)
                lo(u.later(2), 0)
                dve.wait_ge(banks_free[u.par], u.read_out())
                pb = upad[:, u.par]
                stt(pb[:, :, PAD:PAD + T], two(Tt[:, u.par, :]), 1.0, two(Ss[:]), ALU.add, ALU.mult).then_inc(u_done, 1)
                lo(u.later(2), 1)
                dve.drain()
                for tap in range(TAPS - PE_TAPS[j]):
                    w = par[:, 3 + tap // 16, (tap % 16) * 8 + j:(tap % 16) * 8 + j + 1]
                    acc, src = two(Pp[:, tap % 2, :]), pb[:, :, tap:tap + T]
                    if tap == 0:
                        V.tensor_scalar(acc, src, w, par[:, 2, R_DWB + j:R_DWB + j + 1], ALU.mult, ALU.add)
                    elif tap == 1:
                        V.tensor_scalar(acc, src, w, None, ALU.mult)
                    else:
                        stt(acc, src, w, acc, ALU.mult, ALU.add)
                    if tap % 2:
                        dve.drain()
                dve.drain()
                V.tensor_tensor(QK[:, :, j, :], two(Pp[:, 0, :]), two(Pp[:, 1, :]), ALU.add)
                if j >= 1:
                    add_tap_sums(j - 1)
            dve.drain()
            add_tap_sums(C - 1)
            dve.wait_ge(mu_mm, 1)
            V.tensor_scalar(Ss[:], ps[:, 6, :], -1.0 / D, None, ALU.mult)
            dve.drain()
            for kc in range(C):
                V.tensor_tensor(QK[:, :, kc, :], QK[:, :, kc, :], two(Ss[:]), ALU.add).then_inc(cen_done, 1)
            dve.wait_ge(cstd_done, 1)
            V.reciprocal(Rr[:], Rr[:])
            dve.drain()
            for kc in range(C):
                V.tensor_tensor(QK[:, :, kc, :], QK[:, :, kc, :], two(Rr[:]), ALU.mult).then_inc(z_done, 1)

            def z_low(kc):
                dve.wait_ge(zh_done, kc + 1)
                V.tensor_tensor(Fl[:, 0:2, kc, :], two(Pp[:, kc % 2, :]), Fh[:, 0:2, kc, :].bitcast(F32), ALU.subtract) \
                    .then_inc(z_there, 1)

            for kc in range(C):
                dve.wait_ge(zt_done, kc + 1)
                stt(two(Pp[:, kc % 2, :]), two(Tt[:, kc % 2, :]), 1.0, two(scaled[:, kc % 4, :]), ALU.add, ALU.mult) \
                    .then_inc(zp_done, 1)
                if kc >= 1:
                    z_low(kc - 1)
                    dve.drain()
            z_low(C - 1)
            for s in range(2):
                V.tensor_tensor(Ss[:, s * C:(s + 1) * C], MOD[:, 0, 5 * C:6 * C, s], par[:, 2, R_PW2B:R_PW2B + C], ALU.mult)
            dve.drain()
            for kc in range(C):
                for s in range(2):
                    x = (Xx, Xc)[s][:, kc, :]
                    V.tensor_scalar(x, x, Ss[:, s * C + kc:s * C + kc + 1], None, ALU.add)
            dve.drain()
            for j in range(4):
                u = Unit(q, K2_PW2 + j)
                lo(u.later(2), 0)
                dve.wait_ge(mm_done, u.mm_done(1))
                add_gated(u, j, 512, gate(1))
                if j < 3:
                    lo(u.later(2), 1)
            norm(11, 512, 10, gain(2), shift(0, 2), Unit(q, K2_FFN2 + 1))
            ffn(q, K2_FFN2, 5, 512, PLAIN_FULL, PLAIN_LAST, gate(2))
            dve.drain()
            layer_consts(1)
            norm(12, 512, 11, gain(0), shift(1, 0), Unit(q, K2_L1 + 1))
            ffn(q, K2_L1, 6, 512, PLAIN_FULL, PLAIN_LAST, gate(0))
            norm(13, 512, 12, gain(1), shift(1, 1), Unit(q, K2_Q + 1))
            cos, sin = ro[:, RO_COS:RO_COS + T], ro[:, RO_SIN:RO_SIN + T]

            def rotated(i, tiles):
                dve.wait_ge(rot_mm, i + 1)
                dve.drain()
                for t in range(2):
                    V.tensor_tensor(Ss[:, t * T:(t + 1) * T], ps[:, 4 + i % 2, t * T:(t + 1) * T], sin, ALU.mult)
                    V.tensor_tensor(Pp[:, 0, t * T:(t + 1) * T], tiles(t), cos, ALU.mult)
                dve.drain()
                for t in range(2):
                    ins = V.tensor_tensor(tiles(t), Pp[:, 0, t * T:(t + 1) * T], Ss[:, t * T:(t + 1) * T], ALU.add)
                ins.then_inc(rot_done, 1)

            for j in range(4):
                u = Unit(q, K2_Q + j)
                lo(u.later(2), 0)
                dve.wait_ge(mm_done, u.mm_done(1))
                V.tensor_scalar(Qb[:, 2 * j:2 * j + 2, :], pair(u), HD ** -0.5, None, ALU.mult) \
                    .then_inc(banks_free[u.par], 1)
                lo(u.later(2), 1)
                if j >= 1:
                    rotated(j - 1, lambda t, j=j: Qb[:, 2 * (j - 1) + t, :])
            u = Unit(q, K2_KV)
            lo(u.later(2), 0)
            dve.wait_ge(mm_done, u.mm_done(1))
            V.tensor_copy(kraw, ps[:, 2 * u.par:2 * u.par + 2, :]).then_inc(banks_free[u.par], 1)
            lo(u.later(2), 1)
            rotated(3, lambda t: Qb[:, 6 + t, :])
            u = u.later(1)
            lo(u.later(2), 0)
            dve.wait_ge(mm_done, u.mm_done(1))
            V.tensor_copy(v2, ps[:, 2 * u.par:2 * u.par + 2, :].rearrange("p b (t d) -> p (b t) d", t=2)) \
                .then_inc(banks_free[u.par], 1)
            lo(u.later(2), 1)
            rotated(4, lambda t: kraw[:, t, 0:T])

            def low2_out(tile):
                dve.wait_ge(oh2_done, tile + 1)
                V.tensor_tensor(Fl[:, 0, tile, :], ps[:, 6 + tile % 2, 0:T], Fh[:, 0, tile, :].bitcast(F32),
                                ALU.subtract).then_inc(o2_done, 1)

            def largest2(h):
                c = 8 * (h % 2)
                s = ps[:, 2 * (h % 2):2 * (h % 2) + 2, :]
                sink = tiny[:, 16 + h:17 + h]
                dve.wait_ge(s2_done, h + 1)
                V.tensor_tensor(s[:, 0, P:2 * P], s[:, 0, P:2 * P], low, ALU.add)
                V.tensor_tensor(s[:, 1, 0:P], s[:, 1, 0:P], up, ALU.add)
                dve.drain()
                V.tensor_reduce(tiny[:, 32:34], s, AX_X, ALU.max)
                dve.drain()
                V.tensor_scalar(tiny[:, c:c + 2], tiny[:, 32:34], sink, -1.0, ALU.max, ALU.mult)
                dve.drain()
                V.tensor_scalar(tiny[:, c + 4:c + 6], tiny[:, c:c + 2], sink, None, ALU.add).then_inc(nm2_done, 1)

            largest2(0)
            for h in range(QH):
                if h + 1 < QH:
                    largest2(h + 1)
                c = 8 * (h % 2)
                dve.wait_ge(e2_done, h + 1)
                V.tensor_tensor(tiny[:, 34:36], tiny[:, c + 2:c + 4], tiny[:, c + 4:c + 6], ALU.add)
                dve.drain()
                V.reciprocal(tiny[:, c + 6:c + 8], tiny[:, 34:36]).then_inc(r2_done, 1)
                if h % 2 == 1 and h >= 5:
                    low2_out(h // 2 - 2)
            low2_out(QH // 2 - 2)
            low2_out(QH // 2 - 1)
            for j in range(4):
                u = Unit(q, K2_WO + j)
                lo(u.later(2), 0)
                dve.wait_ge(mm_done, u.mm_done(1))
                add_gated(u, j, T, gate(1))
                if j < 3:
                    lo(u.later(2), 1)
            norm(14, T, 13, gain(2), shift(1, 2), Unit(q, K2_FFN4 + 1))
            ffn(q, K2_FFN4, 7, T, PLAIN_FULL, PLAIN_LAST, gate(2))
            rms(15, T)
            for kc in range(C):
                stt(Xx[:, kc, :], Xx[:, kc, :], par[:, 2, R_FING + kc:R_FING + kc + 1], Rr[:, 0:T], ALU.mult, ALU.mult) \
                    .then_inc(final_done, 1)


_INS = ["x", "p", "ffn1_norm", "ffn1_w_in", "ffn1_w_out", "mix_norm", "w_in", "merge_b", "conv_w", "conv_b", "rg_wa",
        "rg_ba", "rg_wx", "rg_bx", "rg_lambda", "f_b", "q_norm", "k_norm", "w_rnn_out", "w_attn_out", "w_o",
        "ffn2_norm", "ffn2_w_in", "ffn2_w_out", "ple_norm", "ple_w_gate", "ple_b_gate", "ple_w_proj", "final_norm",
        "c_2", "ctx_2", "c_ctx_2", "norm_g_2", "ada_w_2", "ada_b_2", "ffn1_wi_2", "ffn1_wo_2", "ffn2_wi_2",
        "ffn2_wo_2", "conv_pw1_w_2", "conv_pw1_b_2", "conv_dw_w_2", "conv_dw_b_2", "conv_ln_g_2", "conv_ln_b_2",
        "conv_pw2_w_2", "conv_pw2_b_2", "attn_w_qkv_2", "attn_w_o_2", "attn_sink_2", "final_g_2"]


def kernel(**inputs):
    import concourse.bacc as bacc
    from concourse.bass_utils import run_bass_kernel_spmd

    nc = bacc.Bacc("TRN2", target_bir_lowering=False, num_devices=1)
    arrays = {f"in_{n}": np.ascontiguousarray(inputs[n]) for n in _INS}
    arrays["in_co"], arrays["in_ro"] = shape_constants()
    aps = {n[3:]: nc.dram_tensor(n, a.shape, F32, kind="ExternalInput").ap() for n, a in arrays.items()}
    out = nc.dram_tensor("out", (1, T, D), F32, kind="ExternalOutput").ap()
    build(nc, aps, out)
    r = run_bass_kernel_spmd(nc, [arrays], core_ids=[0])
    return r.results[0]["out"]
```

```python
import numpy as np

import concourse.bass as bass
from concourse import mybir

F32 = mybir.dt.float32
F32R = mybir.dt.float32r
ALU = mybir.AluOpType
ACT = mybir.ActivationFunctionType
AX_X = mybir.AxisListType.X

P = 128
T = 256
D = 1024
C = D // P
DEPTH = 2
F = 2816
FC = F // P
GROUPS = (8, 8, 6)
HEADS = 8
PLE = 256
RNN_BW = 64
N_MOD = 9
QH, KVH, HD = 16, 4, 64
TAPS = 31
PAD = (TAPS - 1) // 2
PE_TAPS = (12, 9, 8, 9, 8, 9, 8, 14)
DIAGS = D // P * T // P
EPS = 1e-6
NEG = -3.0e38
GELU_C = 0.7978845608028654
GELU_A = 0.044715

ADA_UNITS = N_MOD * D // 256
GROUP_ADA = 8
FFN_A = 52
FFN_B = 34
K_MIX, K_FFN2, K_PLE, K_LAYER = FFN_A, FFN_A + 40, 2 * FFN_A + 40, 2 * FFN_A + 48
assert ADA_UNITS == 2 * (2 * GROUP_ADA + 2) and K_LAYER % 4 == 0
Q_LAYER = K_LAYER // 4
Q_SECOND = DEPTH * Q_LAYER
K2_CONV, K2_PW2, K2_FFN2, K2_L1 = FFN_B, FFN_B + 8, FFN_B + 12, 2 * FFN_B + 12
K2_KV, K2_Q, K2_WO, K2_FFN4 = K2_L1 + FFN_B, K2_L1 + FFN_B + 2, K2_L1 + FFN_B + 6, K2_L1 + FFN_B + 10
K2_END = K2_FFN4 + FFN_B


class Unit:

    def __init__(self, q, k):
        self.q, self.k = q, k
        self.slot = k % 4
        self.par = k % 2

    def later(self, by):
        return Unit(self.q, self.k + by)

    def last(self):
        return isinstance(self.q, int) and 4 * self.q + self.k >= 4 * Q_SECOND + K2_END

    def raw_full(self):
        return (self.q + (self.k // 4 + 1)) * 32

    def raw_free(self):
        return self.q * 8 + (2 * self.k + 2)

    def raw_used(self):
        return self.q * 8 + (2 * self.k + 2)

    def split_free(self, t):
        return self.q * 8 + (2 * self.k + t + 5)

    def hi_done(self, t):
        return self.q * 8 + (2 * self.k + t + 1)

    def lo_done(self, t):
        return self.q * 8 + (2 * self.k + t + 9)

    def mm_done(self, t):
        return self.q * 8 + (2 * self.k + t + 9)

    def banks_free(self):
        return self.q * 2 + (self.k // 2 + 1)

    def read_out(self):
        return self.q * 2 + (self.k // 2 + 2)


FULL_GROUP = [("G", 0)] + [x for i in range(1, 8) for x in (("G", i), ("A", i - 1))] \
    + [("O", 0), ("A", 7), ("O", 1), ("O", 2), ("O", 3)]
LAST_GROUP = [("G", 0), ("G", 1), ("A", 0)] + [("G", i) for i in range(2, 6)] + [("O", i) for i in range(4)] + [("A", 1)]
PLAIN_FULL = [x for x in FULL_GROUP if x[0] != "A"]
PLAIN_LAST = [x for x in LAST_GROUP if x[0] != "A"]

R_FFN1, R_MIX, R_MERGE, R_CONV, R_CONVB, R_BA, R_BX, R_LAM, R_FFN2, R_PLE, R_PLEB, R_QN, R_KN = (
    0, 8, 16, 32, 64, 72, 80, 88, 96, 104, 112, 120, 121)
R_LAYER = 122
R_FINAL, R_NORM, R_PW1B, R_DWB, R_LNG, R_LNB, R_PW2B, R_FING, R_C, R_CCTX = (
    0, 8, 56, 72, 80, 88, 96, 104, 112, 120)
PAR_TILES = 7
PAR_ROWS = (R_LAYER, R_LAYER, 128, 128, (TAPS - 16) * 8, 72, 72)
PAR_LOADS = 13 + 10 + 2 + 1

CO_IDENT, CO_LOW, CO_UP, CO_PICK, CO_SUM, CO_N = 0, 128, 256, 384, 416, 418
RO_COS, RO_SIN, RO_ROT, RO_DUP, RO_N = 0, 256, 512, 640, 896


def shape_constants():
    co = np.zeros((P, CO_N), np.float32)
    i = np.arange(P)
    co[:, CO_IDENT:CO_IDENT + P] = np.eye(P)
    co[:, CO_LOW:CO_LOW + P] = np.where(i[None, :] <= i[:, None], 0.0, NEG)
    co[:, CO_UP:CO_UP + P] = np.where(i[None, :] >= i[:, None], 0.0, NEG)
    for j in range(4):
        for r in range(2):
            co[32 * j + r, CO_SUM + r] = 1.0
    co[:, CO_PICK + 15] = 1.0
    ro = np.zeros((P, RO_N), np.float32)
    n_freq = HD // 4
    inv = (np.float32(10000.0) ** (-np.arange(n_freq, dtype=np.float32) / np.float32(n_freq))).astype(np.float32)
    tok = np.arange(T)
    d = i % HD
    place = np.where((d // 32)[:, None] == 0, (tok // 64)[None, :], (tok % 64)[None, :]).astype(np.float32)
    angle = (place * inv[d % n_freq][:, None]).astype(np.float32)
    ro[:, RO_COS:RO_COS + T] = np.cos(angle)
    ro[:, RO_SIN:RO_SIN + T] = np.sin(angle)
    for m in range(P):
        if m % 32 < 16:
            ro[m + 16, RO_ROT + m] = -1.0
        else:
            ro[m - 16, RO_ROT + m] = 1.0
        for e in range(2):
            ro[64 * e + m % 64, RO_DUP + 128 * e + m] = 1.0
    return co, ro


def build(nc, A, out):
    off = [(nc.sbuf_base + 31) // 32 * 32]

    def sb(name, shape, dt=F32, at=None):
        size = 4 * int(np.prod(shape[1:]))
        where = off[0] if at is None else at
        if at is None:
            off[0] += (size + 31) // 32 * 32
        return nc.alloc_sbuf_tensor_at(name, shape, dt, offset=where)

    from contextlib import ExitStack
    ctx = ExitStack()
    with ctx:
        Xx = sb("Xx", [P, C, T])
        Xc = sb("Xc", [P, C, T])
        Hh = sb("Hh", [P, 2, C, T], F32R)
        hh_ctx_at = off[0] - 4 * C * T
        Hl = sb("Hl", [P, 2, C, T], F32R)
        fh_at = off[0]
        Fh = sb("Fh", [P, 2, C, T], F32R)
        fl_at = off[0]
        Fl = sb("Fl", [P, 2, C, T], F32R)
        decay = sb("decay", [P, C, T], at=fh_at)
        keep = sb("keep", [P, C, T], at=fl_at)
        gateA = sb("gateA", [P, C, T], at=hh_ctx_at)
        raw = sb("raw", [P, 4, C, 256])
        wh = sb("wh", [P, 2, C, 256], F32R)
        wl = sb("wl", [P, 2, C, 256], F32R)
        Gb = sb("Gb", [P, C, T])
        QK = sb("QK", [P, 2, C, T])
        Qb, Kb = QK[:, 0], QK[:, 1]
        Vb = sb("Vb", [P, 2, D])
        Tt = sb("Tt", [P, 2, 512])
        Pp = sb("Pp", [P, 2, 512])
        Ss = sb("Ss", [P, 512])
        Rr = sb("Rr", [P, 512])
        par = sb("par", [P, PAR_TILES, P])
        cur = sb("cur", [P, R_LAYER])
        half = sb("half", [P, R_LAYER])
        co = sb("co", [P, CO_N])
        gate_at = off[0]
        wgate = sb("wgate", [P, 2, C, P])
        ro = sb("ro", [P, RO_N], at=gate_at)
        wf = sb("wf", [P, C, HEADS])
        ones = sb("ones", [P, P])
        MOD = sb("MOD", [P, DEPTH, N_MOD * C, 2])
        cs = sb("cs", [P, C, 16, 2])
        tiny = sb("tiny", [P, 64])
        S1 = sb("S1", [P, 3, C, 2])
        G1 = sb("G1", [P, 3, C, 2])
        eps = sb("eps", [P, 2])
        dmask = sb("dmask", [HEADS, T])
        rqk = sb("rqk", [2 * HEADS, T])
        fb = sb("fb", [HEADS, DEPTH])
        assert off[0] <= nc.sbuf_usable_end, (off[0], nc.sbuf_usable_end)
        ident, low, up = (co[:, a:a + P] for a in (CO_IDENT, CO_LOW, CO_UP))
        prow = Gb[:].rearrange("p c t -> p (c t)")[:, 0:PAR_TILES * P].rearrange("p (n f) -> p n f", f=P)
        xtok = Qb[:].rearrange("p c t -> p (c t)").rearrange("p (n d) -> p n d", n=2)
        ctok = Kb[:].rearrange("p c t -> p (c t)").rearrange("p (n d) -> p n d", n=2)
        ptok = Vb[:, :, 0:PLE]
        diag = Gb[:].rearrange("p c t -> p (c t)").rearrange("p (n f) -> p n f", f=P)
        scaled = Gb[:].rearrange("p c t -> p (c t)").rearrange("p (n f) -> p n f", f=2 * T)
        otok = Gb[:].rearrange("p c t -> p (c t)").rearrange("p (n d) -> p n d", n=2)
        upad = Vb[:].rearrange("p n d -> p (n d)")[:, 0:4 * (T + 2 * PAD)].rearrange(
            "p (b s t) -> p b s t", b=2, s=2)
        kraw = Gb[:].rearrange("p c t -> p (c t)")[:, 0:1024].rearrange("p (n t) -> p n t", n=2)
        kdup = Kb[:].rearrange("p c t -> p (c t)").rearrange("p (n t) -> p n t", n=KVH)
        v2 = Vb[:].rearrange("p n d -> p (n d)")[:, 0:4 * 256].rearrange("p (n d) -> p n d", n=4)
        probs2 = ((Pp[:, 0, :], Pp[:, 1, :]), (Ss[:], Rr[:]))
        probsT2 = (Tt[:], Gb[:].rearrange("p c t -> p (c t)")[:, 1024:2048].rearrange("p (n t) -> p n t", n=2))
        rmask = Rr[0:2 * HEADS, :]
        dmasks = (dmask[:], Ss[0:HEADS, 0:T])
        fz, fe, fa, fsq = (gateA[0:HEADS, i, :] for i in range(4))
        dneg = Tt[0:HEADS, :, 384:512]
        scores = Tt[:, 0, 0:384]
        probsT = Tt[:, 1, 0:384]

        ps = ctx.enter_context(nc.psum_tensor("ps", [P, 8, 512], F32))

        def sem(name):
            return ctx.enter_context(nc.semaphore(name))

        raw_full = [sem(f"raw_full{i}") for i in range(4)]
        hi_done, lo_done, mm_done = sem("hi_done"), sem("lo_done"), sem("mm_done")
        banks_free = [sem(f"banks_free{i}") for i in range(2)]
        par_in, tok_in, small_in = sem("par_in"), sem("tok_in"), sem("small_in")
        zeroed, ones_there, turned, turned_out = sem("zeroed"), sem("ones_there"), sem("turned"), sem("turned_out")
        eps_there, lam_in, lam_exp, c_tanh, c_there = (
            sem(n) for n in ("eps_there", "lam_in", "lam_exp", "c_tanh", "c_there"))
        sqa_done = sem("sqa_done")
        rs_done, rb_done = sem("rs_done"), sem("rb_done")
        sq_done, ss_done, std_done, hp_done, hh_done, h_done = (
            sem(n) for n in ("sq_done", "ss_done", "std_done", "hp_done", "hh_done", "h_done"))
        x_normed, final_done = sem("x_normed"), sem("final_done")
        tanh_done, fh_done, f_done = sem("tanh_done"), sem("fh_done"), sem("f_done")
        cur_there, wgate_in, wf_in, rg_mm, rg_tanh, la_done, rg_exp, keep_done, root_done = (
            sem(n) for n in ("cur_there", "wgate_in", "wf_in", "rg_mm", "rg_tanh", "la_done", "rg_exp",
                             "keep_done", "root_done"))
        gelu_sq, gelu_arg, gelu_tanh = sem("gelu_sq"), sem("gelu_arg"), sem("gelu_tanh")
        qk_sq, qk_ss, qk_std = sem("qk_sq"), sem("qk_ss"), sem("qk_std")
        f_mm, f_in, f_abs = sem("f_mm"), sem("f_in"), sem("f_abs")
        y_done, yh_done, ya_done = sem("y_done"), sem("yh_done"), sem("ya_done")
        rm_done, bc_done, qkn_done, s_done, nmax_done, exp_done, pn_done, tr_done, pt_done, pv_done, oh_done, \
            o_done = (sem(n) for n in ("rm_done", "bc_done", "qkn_done", "s_done", "nmax_done", "exp_done",
                                       "pn_done", "tr_done", "pt_done", "pv_done", "oh_done", "o_done"))
        mp_done, mh_done, m_done = sem("mp_done"), sem("mh_done"), sem("m_done")
        p_in, p_turned, pth_done, p_there = (
            sem(n) for n in ("p_in", "p_turned", "pth_done", "p_there"))
        mod_turned, mod_there, ro_in = sem("mod_turned"), sem("mod_there"), sem("ro_in")
        u_done, diag_there, diag_used = sem("u_done"), sem("diag_there"), sem("diag_used")
        cv_done, mu_mm, cen_done, csq_done, var_mm, cstd_done, z_done, zt_done, zp_done, zh_done, z_there = (
            sem(n) for n in ("cv_done", "mu_mm", "cen_done", "csq_done", "var_mm", "cstd_done",
                             "z_done", "zt_done", "zp_done", "zh_done", "z_there"))
        rot_mm, rot_done, dup_mm, dup_done, sink_mm, sink_done = (
            sem(n) for n in ("rot_mm", "rot_done", "dup_mm", "dup_done", "sink_mm", "sink_done"))
        r2_done = sem("r2_done")
        s2_done, nm2_done, e2_done, pn2_done, tr2_done, pt2_done, pv2_done, oh2_done, o2_done = (
            sem(n) for n in ("s2_done", "nm2_done", "e2_done", "pn2_done", "tr2_done", "pt2_done", "pv2_done",
                             "oh2_done", "o2_done"))
        out_mm, out_copied, stored = sem("out_mm"), sem("out_copied"), sem("stored")

        def bank(u, t, n=512):
            return ps[:, 2 * u.par + t, 0:n]

        def pair(u):
            return ps[:, 2 * u.par:2 * u.par + 2, 0:T]

        def two(ap):
            return ap.rearrange("p (s n) -> p s n", s=2)

        def number(norm):
            return norm + 2 if isinstance(norm, int) and norm > 10 else norm + 1

        def tile_of(w, t):
            return w[:, :, P * t:P * t + P]

        def squares_of(i, n, roomy=False):
            if n == T:
                return Tt[:, min(i, 1), :].rearrange("p (s t n) -> p s t n", s=1, t=2)
            if roomy and i in (1, 2):
                return Gb[:, 4 * (i - 1):4 * i, :].rearrange("p (s t) n -> p s t n", s=2)
            return (Pp if i == 0 else Tt)[:].rearrange("p s (t n) -> p s t n", t=2)

        def quarter(ap, g, n):
            return ap[:, g // 2, P * (g % 2):P * (g % 2) + P] if n > T else ap[:, 0, T // 4 * g:T // 4 * (g + 1)]

        def groups_of(eng, q, k, order, last):
            with eng.Fori(0, 2) as g:
                yield g, [(kind, i, Unit(q + g * (len(order) // 4), k + j)) for j, (kind, i) in enumerate(order)]
            yield 2, [(kind, i, Unit(q, k + 2 * len(order) + j)) for j, (kind, i) in enumerate(last)]

        def ada_index(s, g, i):
            return g * GROUP_ADA + (s * (ADA_UNITS // 2) + i)

        block = ctx.enter_context(nc.Block())

        @block.sync
        def _(sp):
            sp.dma_start(co[:], A["co"]).then_inc(tok_in, 16)
            sp.dma_start(xtok, A["x"][0].rearrange("(n p) d -> p n d", p=P)).then_inc(tok_in, 16)

            def row(tile, r, src):
                n = src.shape[0]
                sp.dma_start(prow[r:r + n, tile, :], src).then_inc(par_in, 16)

            def rows_of_layers(tile, r, src):
                n = src.shape[0]
                sp.dma_start(prow[r:r + n, tile:tile + DEPTH, :], src).then_inc(par_in, 16)

            for r, name in ((R_FFN1, "ffn1_norm"), (R_MIX, "mix_norm"), (R_MERGE, "merge_b"), (R_CONVB, "conv_b"),
                            (R_BA, "rg_ba"), (R_BX, "rg_bx"), (R_LAM, "rg_lambda"), (R_FFN2, "ffn2_norm"),
                            (R_PLE, "ple_norm"), (R_PLEB, "ple_b_gate"), (R_QN, "q_norm"), (R_KN, "k_norm")):
                rows_of_layers(0, r, A[name].rearrange("l (c p) -> c l p", p=P))
            rows_of_layers(0, R_CONV, A["conv_w"].rearrange("l k (c p) -> (k c) l p", p=P))
            for r, src in ((R_FINAL, A["final_norm"]), (R_PW1B, A["conv_pw1_b_2"][0]), (R_DWB, A["conv_dw_b_2"][0]),
                           (R_LNG, A["conv_ln_g_2"][0]), (R_LNB, A["conv_ln_b_2"][0]), (R_PW2B, A["conv_pw2_b_2"][0]),
                           (R_FING, A["final_g_2"]), (R_C, A["c_2"][0]), (R_CCTX, A["c_ctx_2"])):
                row(2, r, src.rearrange("(c p) -> c p", p=P))
            row(2, R_NORM, A["norm_g_2"].rearrange("l n (c p) -> (l n c) p", p=P))
            row(3, 0, A["conv_dw_w_2"][0, 0:16].rearrange("k (c p) -> (k c) p", p=P))
            row(4, 0, A["conv_dw_w_2"][0, 16:TAPS].rearrange("k (c p) -> (k c) p", p=P))
            rows_of_layers(5, 0, A["ada_b_2"].rearrange("l (c p) -> c l p", p=P))
            with nc.allow_non_contiguous_dma(reason="sixteen values"):
                sp.dma_start(fb[:], A["f_b"].rearrange("l h -> h l")).then_inc(small_in, 16)
            sp.dma_start(tiny[0:1, 48:64], A["attn_sink_2"]).then_inc(small_in, 16)

            def load_pair(u, halves, after_a=False):
                if after_a:
                    sp.wait_ge(mm_done, u.raw_used())
                else:
                    sp.wait_ge(lo_done, u.raw_free())
                for h in range(2):
                    sp.dma_start(raw[:, u.slot, :, P * h:P * h + P], halves[:, :, h, :]) \
                        .then_inc(raw_full[u.slot], 16)

            def load_cols(u, w, col, kc=C, k0=0, after_a=False):
                rows = w.rearrange("(c p) n -> p c n", p=P)
                cols = bass.ds(col, 256) if not isinstance(col, int) else slice(col, col + 256)
                if after_a:
                    sp.wait_ge(mm_done, u.raw_used())
                else:
                    sp.wait_ge(lo_done, u.raw_free())
                for h in (1, 0):
                    a, n = h * (kc // 2), kc // 2
                    chunks = slice(k0 + a, k0 + a + n) if isinstance(k0, int) else bass.ds(k0 + a, n)
                    sp.dma_start(raw[:, u.slot, a:a + n, :], rows[:, chunks, cols]).then_inc(raw_full[u.slot], 16)

            def load_ffn(q, k, w_in, w_out, order, last, ada=None):
                gu = w_in.rearrange("(c p) (h n) -> p c h n", p=P, h=2)
                for g, units in groups_of(sp, q, k, order, last):
                    for j, (kind, i, u) in enumerate(units):
                        after_a = ada is not None and (units[j - 4][0] if j >= 4 else order[j - 4][0]) == "A"
                        if kind == "G":
                            f = g * (8 * P) + i * P
                            cols = slice(f, f + P) if isinstance(f, int) else bass.ds(f, P)
                            load_pair(u, gu[:, :, :, cols], after_a)
                        elif kind == "O":
                            load_cols(u, w_out, 256 * i, GROUPS[2] if isinstance(g, int) else 8, g * 8, after_a)
                        else:
                            l, s = ada
                            load_cols(u, A["ada_w_2"][l], ada_index(s, g, i) * 256, after_a=after_a)

            with sp.Fori(0, DEPTH) as l:
                q = l * Q_LAYER
                load_ffn(q, 0, A["ffn1_w_in"][l], A["ffn1_w_out"][l], FULL_GROUP, LAST_GROUP, (l, 0))
                sp.wait_ge(zeroed, 1)
                sp.wait_ge(rg_mm, l * C + 1)
                for g, name in enumerate(("rg_wa", "rg_wx")):
                    blocks = A[name][l].rearrange("(j e) c d -> e c j d", e=2)
                    for e in range(2):
                        sl = slice(RNN_BW * e, RNN_BW * (e + 1))
                        sp.dma_start(wgate[sl, g, :, sl], blocks[e]).then_inc(wgate_in, 16)
                sp.wait_ge(f_mm, l + 1)
                with nc.allow_non_contiguous_dma(reason="eight columns"):
                    sp.dma_start(wf[:], A["w_in"][l].rearrange("(c p) n -> p c n", p=P)[:, :, 5 * D:5 * D + HEADS]) \
                        .then_inc(wf_in, 16)
                w_in = A["w_in"][l]
                k = K_MIX
                for j in range(8):
                    load_cols(Unit(q, k + j), w_in, 256 * j, after_a=j == 3)
                for i in range(8):
                    load_cols(Unit(q, k + 8 + i), w_in, 2 * D + (i % 2) * D + 256 * (i // 2))
                for j in range(4):
                    load_cols(Unit(q, k + 16 + j), w_in, 4 * D + 256 * j)
                for j in range(8):
                    load_cols(Unit(q, k + 20 + j), w_in, 5 * D + HEADS + 256 * j)
                for j in range(4):
                    load_cols(Unit(q, k + 28 + j), A["w_rnn_out"][l], 256 * j)
                for j in range(4):
                    load_cols(Unit(q, k + 32 + j), A["w_attn_out"][l], 256 * j)
                for j in range(4):
                    load_cols(Unit(q, k + 36 + j), A["w_o"][l], 256 * j)
                sp.wait_ge(pv_done, l * HEADS + HEADS)
                sp.dma_start(ptok, A["p"][l, 0].rearrange("(n p) d -> p n d", p=P)).then_inc(p_in, 16)
                load_ffn(q, K_FFN2, A["ffn2_w_in"][l], A["ffn2_w_out"][l], FULL_GROUP, LAST_GROUP, (l, 1))
                for j in range(4):
                    load_cols(Unit(q, K_PLE + 2 * j), A["ple_w_gate"][l], 256 * j)
                    load_cols(Unit(q, K_PLE + 2 * j + 1), A["ple_w_proj"][l], 256 * j, PLE // P, after_a=j == 1)

            q = Q_SECOND
            sp.wait_ge(rg_mm, DEPTH * C + 1)
            sp.dma_start(ro[:], A["ro"]).then_inc(ro_in, 16)
            sp.wait_ge(s_done, DEPTH * HEADS)
            sp.dma_start(ctok, A["ctx_2"][0].rearrange("(n p) d -> p n d", p=P)).then_inc(tok_in, 16)
            load_ffn(q, 0, A["ffn1_wi_2"][0], A["ffn1_wo_2"][0], PLAIN_FULL, PLAIN_LAST)
            pw1 = A["conv_pw1_w_2"][0].rearrange("(c p) (h n) -> p c h n", p=P, h=2)
            for j in range(C):
                load_pair(Unit(q, K2_CONV + j), pw1[:, :, :, P * j:P * j + P])
            for j in range(4):
                load_cols(Unit(q, K2_PW2 + j), A["conv_pw2_w_2"][0], 256 * j)
            load_ffn(q, K2_FFN2, A["ffn2_wi_2"][0], A["ffn2_wo_2"][0], PLAIN_FULL, PLAIN_LAST)
            load_ffn(q, K2_L1, A["ffn1_wi_2"][1], A["ffn1_wo_2"][1], PLAIN_FULL, PLAIN_LAST)
            for i, j in enumerate((4, 5, 0, 1, 2, 3)):
                load_cols(Unit(q, K2_KV + i), A["attn_w_qkv_2"][0], 256 * j)
            for j in range(4):
                load_cols(Unit(q, K2_WO + j), A["attn_w_o_2"][0], 256 * j)
            load_ffn(q, K2_FFN4, A["ffn2_wi_2"][1], A["ffn2_wo_2"][1], PLAIN_FULL, PLAIN_LAST)
            for n in range(2):
                sp.wait_ge(out_copied, 2 * (n + 1))
                sp.dma_start(out[0, n * P:(n + 1) * P, :], otok[:, n, :]).then_inc(stored, 16)
            sp.wait_ge(stored, 32)

        @block.gpsimd
        def _(pool):
            nc.gpsimd.memset(wgate[:], 0.0).then_inc(zeroed, 1)

        @block.tensor
        def _(pe):
            pe.sem_inc(mm_done, 8)
            pe.sem_inc(rg_mm, 1)
            pe.sem_inc(f_mm, 1)

            def out_of(u, t, n):
                return bank(u, t, n) if n == T else two(bank(u, t))

            def linear(u, xh, xl, n, kc_n=C, ready=None, tiles=(0, 1), together=True):
                def products(kc, t):
                    w = slice(P * t, P * t + P)
                    o = out_of(u, t, n)
                    nc.tensor.matmul(o, wh[:, u.par, kc, w], xh(kc), start=(kc == 0), stop=False)
                    nc.tensor.matmul(o, wh[:, u.par, kc, w], xl(kc), start=False, stop=False)
                    return nc.tensor.matmul(o, wl[:, u.par, kc, w], xh(kc), start=False, stop=(kc == kc_n - 1))

                if ready is not None and len(tiles) == 2 and together:
                    pe.wait_ge(lo_done, u.lo_done(1))
                    pe.wait_ge(banks_free[u.par], u.banks_free())
                    for kc in range(kc_n):
                        ready(kc)
                        for t in tiles:
                            mm = products(kc, t)
                            if kc == kc_n - 1:
                                mm.then_inc(mm_done, 1)
                    return
                for t in tiles:
                    pe.wait_ge(lo_done, u.lo_done(t))
                    if t == 0:
                        pe.wait_ge(banks_free[u.par], u.banks_free())
                    for kc in range(kc_n):
                        if ready is not None and t == 0:
                            ready(kc)
                        mm = products(kc, t)
                    mm.then_inc(mm_done, 1)

            def part(buf, n, s=0):
                if n == T:
                    return lambda kc: buf[:, s, kc, :]
                return lambda kc: buf[:, 0:2, kc, :]

            def h_ready(norm):
                return lambda kc: pe.wait_ge(h_done, norm * C + (kc + 1))

            def sum_rows(b, ap, n, start, stop):
                for g in range(4):
                    mm = nc.tensor.matmul(ps[32 * g:32 * g + 32, b, 0:n // 4], ones[:, 0:32], quarter(ap, g, n),
                                          start=start, stop=stop)
                return mm

            def sums(norm, last, n):
                if last:
                    pe.wait_ge(sq_done, norm * 4 + 4)
                else:
                    pe.wait_ge(sqa_done, norm * 2 + 2)
                for t in range(2):
                    mm = sum_rows(4, squares_of(3 if last else 0, n)[:, :, t], n, not last and t == 0, last and t == 1)
                if last:
                    mm.then_inc(ss_done, 1)

            def spread_roots(b, count, n):
                pe.wait_ge(rs_done, count)
                for g in range(4):
                    one_row = ident[:, 32 * g:32 * g + 1].to_broadcast([P, P])
                    mm = nc.tensor.matmul(ps[:, b, n // 4 * g:n // 4 * (g + 1)], one_row, Rr[:, 0:n // 4], start=True,
                                          stop=True)
                mm.then_inc(rb_done, 1)

            def modulation(u):
                pe.wait_ge(raw_full[u.slot], u.raw_full())
                pe.wait_ge(banks_free[u.par], u.banks_free())
                for kc in range(C):
                    j = kc % 4
                    mm = nc.tensor.matmul(ps[32 * j:32 * j + 32, 2 * u.par, 0:256],
                                          cs[:, kc].rearrange("p m s -> p (m s)"), raw[:, u.slot, kc, :],
                                          start=(kc < 4), stop=(kc >= 4))
                mm.then_inc(mm_done, 2)

            def turn_modulation(u, i):
                pe.wait_ge(banks_free[u.par], u.read_out())
                for t in range(2):
                    mm = nc.tensor.matmul(ps[:, 5 + i % 2, 2 * t:2 * t + 2], Pp[:, u.par, T + P * t:T + P * (t + 1)],
                                          co[:, CO_SUM:CO_SUM + 2], start=True, stop=True)
                mm.then_inc(mod_turned, 1)

            def ffn(q, k, fi, hn, n, order, last, after, layer=None):
                for g, units in groups_of(pe, q, k, order, last):
                    held = 8 if not isinstance(g, int) else GROUPS[2]
                    for j, (kind, i, u) in enumerate(units):
                        if kind == "G":
                            linear(u, part(Hh, n), part(Hl, n), n, ready=h_ready(hn) if i == 0 else None)
                        elif kind == "O":
                            done = fi * FC + g * 8

                            def ready(kc, done=done):
                                pe.wait_ge(f_done, done + (kc + 1))
                            linear(u, part(Fh, n), part(Fl, n), n, held, ready if i == 0 else None,
                                   together=units[j - 1][0] != "A")
                        else:
                            if i == 0:
                                pe.wait_ge(c_there, layer + 1)
                            modulation(u)
                        if j >= 1 and units[j - 1][0] == "A":
                            turn_modulation(units[j - 1][2], units[j - 1][1])
                        if isinstance(g, int) and (kind, i) == ("O", 3):
                            sums(after, False, n)
                        if isinstance(g, int) and j == len(units) - 1:
                            sums(after, True, n)
                            spread_roots(4, number(after), n)
                if units[-1][0] == "A":
                    turn_modulation(units[-1][2], units[-1][1])

            def turn_tokens(src, bank0):
                for b in range(4):
                    for i in range(4):
                        mm = nc.tensor.transpose(ps[:, bank0 + b, i * P:(i + 1) * P],
                                                 src[:, i % 2, (2 * b + i // 2) * P:(2 * b + i // 2 + 1) * P], ident)
                    mm.then_inc(turned, 1)

            pe.wait_ge(tok_in, 32)
            turn_tokens(xtok, 0)
            pe.wait_ge(ones_there, 1)
            sums(0, False, T)
            sums(0, True, T)
            pe.wait_ge(par_in, 16 * PAR_LOADS)
            for i, n in enumerate(PAR_ROWS):
                mm = nc.tensor.transpose(ps[:, 5 + i // 4, (i % 4) * P:(i % 4) * P + n], prow[0:n, i, :],
                                         ident[0:n, 0:n])
            mm.then_inc(turned, 1)
            pe.wait_ge(small_in, 32)
            nc.tensor.matmul(ps[:, 7, 0:QH], ones[0:1, :], tiny[0:1, 48:64], start=True, stop=True) \
                .then_inc(sink_mm, 1)
            spread_roots(4, 1, T)

            with pe.Fori(0, DEPTH) as l:
                q = l * Q_LAYER
                ffn(q, 0, l * 2, l * 4, T, FULL_GROUP, LAST_GROUP, l * 4 + 1, l)

                k = K_MIX
                for j in range(8):
                    linear(Unit(q, k + j), part(Hh, T), part(Hl, T), T, ready=h_ready(l * 4 + 1) if j == 0 else None)
                pe.wait_ge(wf_in, l * 16 + 16)
                for kc in range(C):
                    nc.tensor.matmul(ps[0:HEADS, 4, 0:T], wf[:, kc, :], Hh[:, 0, kc, :].bitcast(F32),
                                     start=(kc == 0), stop=False)
                    mm = nc.tensor.matmul(ps[0:HEADS, 4, 0:T], wf[:, kc, :], Hl[:, 0, kc, :].bitcast(F32),
                                          start=False, stop=(kc == C - 1))
                mm.then_inc(f_mm, 1)

                def qk_sums(idx):
                    pe.wait_ge(qk_sq, l * 8 + (idx + 1))
                    for t in range(2):
                        r = (idx % 2) * HEADS + 2 * (idx // 2) + t
                        mm = nc.tensor.matmul(ps[0:2 * HEADS, 5, 0:T], co[:, CO_PICK + 15 - r:CO_PICK + 31 - r],
                                              Tt[:, idx % 2, t * T:(t + 1) * T], start=(idx == 0 and t == 0),
                                              stop=(idx == 7 and t == 1), skip_group_check=True)
                    mm.then_inc(qk_ss, 1)

                def gates(j):
                    rx = Unit(q, k + j // 2)
                    pe.wait_ge(banks_free[rx.par], rx.read_out())
                    if j == 0:
                        pe.wait_ge(wgate_in, l * 64 + 64)
                    if j >= 2:
                        pe.wait_ge(rg_tanh, l * 8 + (j - 1))
                    for g in range(2):
                        mm = nc.tensor.matmul(ps[:, 6 + j % 2, g * T:(g + 1) * T], wgate[:, g, j, :], Xc[:, j, :],
                                              start=True, stop=True)
                    mm.then_inc(rg_mm, 1)

                for i in range(12):
                    u = Unit(q, k + 8 + i)
                    if i < 8:
                        gates(i)
                        linear(u, part(Hh, T), part(Hl, T), T)
                    else:
                        for t in range(2):
                            pe.wait_ge(lo_done, u.lo_done(1))
                            if t == 0:
                                pe.wait_ge(banks_free[u.par], u.banks_free())
                            tok = slice(t * P, t * P + P)
                            for kc in range(C):
                                o = bank(u, t, T)
                                nc.tensor.matmul(o, Hh[:, 0, kc, tok], wh[:, u.par, kc, :], start=(kc == 0), stop=False)
                                nc.tensor.matmul(o, Hl[:, 0, kc, tok], wh[:, u.par, kc, :], start=False, stop=False)
                                mm = nc.tensor.matmul(o, Hh[:, 0, kc, tok], wl[:, u.par, kc, :], start=False,
                                                      stop=(kc == C - 1))
                        mm.then_inc(mm_done, 2)
                    if 1 <= i <= 8:
                        qk_sums(i - 1)

                def turn_probs(h):
                    pe.wait_ge(pn_done, l * HEADS + (h + 1))
                    for b in range(3):
                        mm = nc.tensor.transpose(ps[:, 6, b * P:(b + 1) * P], scores[:, b * P:(b + 1) * P], ident)
                    mm.then_inc(tr_done, 1)

                def spread(h):
                    pe.wait_ge(rm_done, l * HEADS + (h + 1))
                    nc.tensor.matmul(ps[:, 4, :], ones[0:2 * HEADS, :], rmask, start=True, stop=True) \
                        .then_inc(bc_done, 1)

                def head_scores(h):
                    pe.wait_ge(qkn_done, l * HEADS + (h + 1))
                    for b in range(2):
                        o = ps[:, 5, b * P:b * P + (b + 1) * P]
                        nc.tensor.matmul(o, Qb[:, h, b * P:(b + 1) * P], Kb[:, h, 0:(b + 1) * P], start=True, stop=False)
                        mm = nc.tensor.matmul(o, ones[0:HEADS, :], dmasks[h % 2][:, 0:(b + 1) * P], start=False, stop=True)
                    mm.then_inc(s_done, 1)

                def head_values(h):
                    pe.wait_ge(pt_done, l * HEADS + (h + 1))
                    if h >= 1:
                        pe.wait_ge(o_done, l * HEADS + h)
                    v = slice(h * P, h * P + P)
                    nc.tensor.matmul(ps[:, 7, 0:T], Vb[:, 0, v], probsT[:, 0:T], start=True, stop=False)
                    nc.tensor.matmul(ps[:, 7, P:T], Vb[:, 1, v], probsT[:, T:T + P], start=False, stop=True) \
                        .then_inc(pv_done, 1)

                def ya_ready(kc):
                    pe.wait_ge(ya_done, l * C + (kc + 1))

                for st in range(HEADS):
                    u = Unit(q, k + 20 + st)
                    linear(u, part(Hh, T), part(Hl, T), T, tiles=(0,))
                    if st >= 2:
                        head_values(st - 2)
                    spread(st)
                    linear(u, part(Hh, T), part(Hl, T), T, tiles=(1,))
                    if st >= 1:
                        turn_probs(st - 1)
                    head_scores(st)

                def o_ready(kc):
                    pe.wait_ge(o_done, l * HEADS + (kc + 1))

                for j in range(4):
                    u = Unit(q, k + 28 + j)
                    linear(u, part(Fh, T), part(Fl, T), T, ready=ya_ready if j == 0 else None, tiles=(0,))
                    if j < 2:
                        head_values(HEADS - 2 + j)
                    linear(u, part(Fh, T), part(Fl, T), T, tiles=(1,))
                    if j == 0:
                        turn_probs(HEADS - 1)
                for j in range(4):
                    linear(Unit(q, k + 32 + j), part(Fh, T, 1), part(Fl, T, 1), T, ready=o_ready if j == 0 else None)

                def m_ready(kc):
                    pe.wait_ge(m_done, l * 4 + (kc // 2 + 1))

                for j in range(4):
                    linear(Unit(q, k + 36 + j), part(Hh, T, 1), part(Hl, T, 1), T, ready=m_ready if j == 0 else None)
                sums(l * 4 + 2, False, T)
                sums(l * 4 + 2, True, T)
                spread_roots(4, l * 4 + 3, T)
                ffn(q, K_FFN2, l * 2 + 1, l * 4 + 2, T, FULL_GROUP, LAST_GROUP, l * 4 + 3, l)

                pe.wait_ge(p_in, l * 16 + 16)
                for i in range(4):
                    mm = nc.tensor.transpose(ps[:, 7, i * P:(i + 1) * P], ptok[:, i % 2, (i // 2) * P:(i // 2 + 1) * P],
                                             ident)
                mm.then_inc(p_turned, 1)
                for j in range(4):
                    u = Unit(q, K_PLE + 2 * j)
                    linear(u, part(Hh, T), part(Hl, T), T, ready=h_ready(l * 4 + 3) if j == 0 else None)
                    if j == 0:
                        pe.wait_ge(p_there, l + 1)
                    linear(u.later(1), part(Fh, T, 1), part(Fl, T, 1), T, PLE // P)
                sums(l * 4 + 4, False, T)
                sums(l * 4 + 4, True, T)
                spread_roots(4, l * 4 + 5, T)

            q = Q_SECOND
            pe.wait_ge(tok_in, 48)
            turn_tokens(ctok, 0)
            sums(9, False, 512)
            sums(9, True, 512)
            spread_roots(4, 10, 512)
            pe.wait_ge(turned_out, 8)
            ffn(q, 0, 4, 8, 512, PLAIN_FULL, PLAIN_LAST, 10)
            def taps(j):
                pe.wait_ge(u_done, j + 1)
                if j >= 2:
                    pe.wait_ge(cv_done, j - 1)
                for i in range(PE_TAPS[j]):
                    n, tap = sum(PE_TAPS[:j]) + i, TAPS - PE_TAPS[j] + i
                    pe.wait_ge(diag_there, n + 1)
                    nc.tensor.matmul(two(ps[:, 4 + j % 2, :]), diag[:, n % DIAGS, :], upad[:, j % 2, :, tap:tap + T],
                                     start=(i == 0), stop=(i == PE_TAPS[j] - 1)).then_inc(diag_used, 1)

            def mean_sums(j):
                pe.wait_ge(cv_done, j + 1)
                return nc.tensor.matmul(two(ps[:, 6, :]), ones[:], QK[:, :, j, :], start=(j == 0), stop=(j == C - 1))

            for j in range(C):
                linear(Unit(q, K2_CONV + j), part(Hh, 512), part(Hl, 512), 512, ready=h_ready(9) if j == 0 else None)
                if j >= 1:
                    taps(j - 1)
                if j >= 2:
                    mean_sums(j - 2)
            taps(C - 1)
            mean_sums(C - 2)
            mean_sums(C - 1).then_inc(mu_mm, 1)
            for kc in range(C):
                pe.wait_ge(csq_done, kc + 1)
                sum_rows(7, two(Tt[:, kc % 2, :]), 512, kc == 0, kc == C - 1).then_inc(var_mm, 1)
            spread_roots(7, 12, 512)

            def z_ready(kc):
                pe.wait_ge(z_there, kc + 1)

            for j in range(4):
                linear(Unit(q, K2_PW2 + j), part(Fh, 512), part(Fl, 512), 512, ready=z_ready if j == 0 else None)
            sums(11, False, 512)
            sums(11, True, 512)
            spread_roots(4, number(11), 512)
            ffn(q, K2_FFN2, 5, 10, 512, PLAIN_FULL, PLAIN_LAST, 12)
            ffn(q, K2_L1, 6, 11, 512, PLAIN_FULL, PLAIN_LAST, 13)
            pe.wait_ge(ro_in, 16)

            def rotate(i, src):
                ue = Unit(q, K2_KV if i == 0 else K2_Q + i - 1)
                pe.wait_ge(banks_free[ue.par], ue.read_out())
                if i >= 2:
                    pe.wait_ge(rot_done, i - 1)
                nc.tensor.matmul(two(ps[:, 4 + i % 2, :]), ro[:, RO_ROT:RO_ROT + P], src, start=True, stop=True) \
                    .then_inc(rot_mm, 1)

            def q_tiles(i):
                return Qb[:, 2 * i:2 * i + 2, :]

            u = Unit(q, K2_KV)
            linear(u, part(Hh, 512), part(Hl, 512), 512, ready=h_ready(12))
            u = u.later(1)
            pe.wait_ge(lo_done, u.lo_done(1))
            pe.wait_ge(banks_free[u.par], u.banks_free())
            for t in range(4):
                tok = slice((t % 2) * P, (t % 2) * P + P)
                o = ps[:, 2 * u.par + t // 2, (t % 2) * T:(t % 2 + 1) * T]
                for kc in range(C):
                    nc.tensor.matmul(o, Hh[:, t // 2, kc, tok], wh[:, u.par, kc, :], start=(kc == 0), stop=False)
                    nc.tensor.matmul(o, Hl[:, t // 2, kc, tok], wh[:, u.par, kc, :], start=False, stop=False)
                    mm = nc.tensor.matmul(o, Hh[:, t // 2, kc, tok], wl[:, u.par, kc, :], start=False,
                                          stop=(kc == C - 1))
            mm.then_inc(mm_done, 2)
            rotate(0, kraw[:, :, 0:T])
            for j in range(4):
                linear(Unit(q, K2_Q + j), part(Hh, T), part(Hl, T), T)
                if j >= 1:
                    rotate(j, q_tiles(j - 1))
                    continue
                pe.wait_ge(rot_done, 1)
                for kv in range(KVH):
                    if kv >= 2:
                        pe.wait_ge(dup_done, kv - 1)
                    nc.tensor.matmul(ps[:, 6 + kv % 2, :], ro[:, RO_DUP + P * (kv % 2):RO_DUP + P * (kv % 2 + 1)],
                                     kraw[:, kv // 2, :], start=True, stop=True).then_inc(dup_mm, 1)
            rotate(4, q_tiles(3))
            pe.wait_ge(dup_done, KVH)

            def scores2(h):
                half_p = slice(HD * (h % 2), HD * (h % 2) + HD)
                if h % 4 == 0:
                    pe.wait_ge(rot_done, h // 4 + 2)
                if h >= 2:
                    pe.wait_ge(e2_done, h - 1)
                for b in range(2):
                    mm = nc.tensor.matmul(ps[:, 2 * (h % 2) + b, :], Qb[half_p, h // 2, b * P:(b + 1) * P],
                                          kdup[half_p, h // 4, :], start=True, stop=True)
                mm.then_inc(s2_done, 1)

            def turn_probs2(h):
                pe.wait_ge(pn2_done, h + 1)
                if h >= 1:
                    pe.wait_ge(pt2_done, h)
                for b in range(2):
                    for kb in range(4):
                        mm = nc.tensor.transpose(ps[:, 4 + kb // 2, (kb % 2) * T + b * P:(kb % 2) * T + (b + 1) * P],
                                                 probs2[h % 2][b][:, kb * P:(kb + 1) * P], ident)
                mm.then_inc(tr2_done, 1)

            def head_values2(h):
                pe.wait_ge(pt2_done, h + 1)
                if h % 2 == 0 and h >= 4:
                    pe.wait_ge(o2_done, h // 2 - 1)
                for kb in range(4):
                    o = ps[HD * (h % 2):HD * (h % 2) + HD, 6 + (h // 2) % 2, 0:T]
                    mm = nc.tensor.matmul(o, v2[:, kb, HD * (h // 4):HD * (h // 4) + HD],
                                          probsT2[h % 2][:, kb // 2, (kb % 2) * T:(kb % 2 + 1) * T], start=(kb == 0),
                                          stop=(kb == 3))
                mm.then_inc(pv2_done, 1)

            for back in (1, 2):
                ue = Unit(q, K2_WO - back)
                pe.wait_ge(banks_free[ue.par], ue.read_out())
            scores2(0)
            pe.wait_ge(rot_done, 5)
            for i in range(QH + 2):
                if i + 1 < QH:
                    scores2(i + 1)
                if i >= 2:
                    head_values2(i - 2)
                if 1 <= i <= QH:
                    turn_probs2(i - 1)

            def o2_ready(kc):
                pe.wait_ge(o2_done, kc + 1)

            for j in range(4):
                linear(Unit(q, K2_WO + j), part(Fh, T), part(Fl, T), T, ready=o2_ready if j == 0 else None)
            sums(14, False, T)
            sums(14, True, T)
            spread_roots(4, number(14), T)
            ffn(q, K2_FFN4, 7, 13, T, PLAIN_FULL, PLAIN_LAST, 15)
            for n in range(2):
                for b in range(2):
                    for i in range(4):
                        kc = 4 * b + i
                        pe.wait_ge(final_done, kc + 1)
                        mm = nc.tensor.transpose(ps[:, 2 * n + b, i * P:(i + 1) * P],
                                                 Xx[:, kc, n * P:(n + 1) * P], ident)
                    mm.then_inc(out_mm, 1)

        @block.scalar
        def _(act):
            def hi(u, t, mod=False):
                if u.last():
                    return
                if mod:
                    if t == 1:
                        act.drain().then_inc(hi_done, 2)
                    return
                if t == 0:
                    act.wait_ge(raw_full[u.slot], u.raw_full())
                act.wait_ge(mm_done, u.split_free(t))
                nc.scalar.activation(tile_of(wh[:, u.par], t), tile_of(raw[:, u.slot], t), ACT.Copy) \
                    .then_inc(hi_done, 1)

            def tanh_table():
                nc.scalar.activation(eps[:, 1:2], eps[:, 0:1], ACT.Tanh)

            def root_table():
                nc.scalar.activation(eps[:, 1:2], eps[:, 0:1], ACT.Sqrt)

            def stream(u):
                hi(u.later(2), 0)
                hi(u.later(2), 1)

            def squares(norm_i, i, n, u=None, roomy=False):
                if i == 3:
                    root_table()
                if u is not None:
                    act.wait_ge(banks_free[u.par], u.read_out())
                if i >= 2 and not roomy:
                    act.wait_ge(sqa_done, norm_i * 2 + (i - 1))
                dst = squares_of(i, n, roomy)
                for s in reversed(range(n // T)):
                    ins = nc.scalar.activation(dst[:, s], (Xx, Xc)[s][:, 2 * i:2 * i + 2, :], ACT.Square)
                ins.then_inc(sq_done, 1)

            def norm(norm_i, n, with_h=None, shift=None, late=None):
                act.wait_ge(ss_done, norm_i + 1)
                nc.scalar.activation(Rr[:, 0:n // 4], ps[:, 4, 0:n // 4], ACT.Sqrt, bias=eps[:, 0:1], scale=1.0 / D) \
                    .then_inc(std_done, 1)
                if with_h is None:
                    tanh_table()
                    return
                for kc in range(C):
                    act.wait_ge(hp_done, with_h * C + (kc + 1))
                    for s in range(n // T):
                        src = Pp[:, kc % 2, s * T:(s + 1) * T]
                        if shift is None:
                            ins = nc.scalar.activation(Hh[:, s, kc, :], src, ACT.Copy)
                        else:
                            ins = nc.scalar.activation(Hh[:, s, kc, :], src, ACT.Identity, bias=shift(kc, s))
                    ins.then_inc(hh_done, 1)
                tanh_table()
                hi(late, 1)

            def ffn(q, k, fi, n, order, last, after):
                for g, units in groups_of(act, q, k, order, last):
                    for j, (kind, i, u) in enumerate(units):
                        mod = j + 2 < len(units) and units[j + 2][0] == "A"
                        hi(u.later(2), 0, mod)
                        if kind == "G":
                            act.wait_ge(mm_done, u.mm_done(0))
                            nc.scalar.activation(Tt[:, u.par, 0:n], bank(u, 0, n), ACT.Tanh, scale=0.5) \
                                .then_inc(tanh_done, 1)
                        if isinstance(g, int) and (kind, i) == ("O", 3):
                            squares(after, i, n, u)
                        if not isinstance(g, int) or j < len(units) - 1:
                            hi(u.later(2), 1, mod)
                        if isinstance(g, int) and kind == "O" and i < 3:
                            squares(after, i, n, u)
                        if kind == "A":
                            act.wait_ge(mm_done, u.mm_done(1))
                            nc.scalar.activation(Pp[:, u.par, T:2 * T], ps[:, 2 * u.par, 0:256], ACT.Copy) \
                                .then_inc(banks_free[u.par], 1)
                        if kind == "G":
                            act.wait_ge(banks_free[u.par], u.read_out())
                            dst = Fh[:, 0, i, :] if n == T else Fh[:, 0:2, i, :]
                            src = Pp[:, u.par, 0:n] if n == T else two(Pp[:, u.par, :])
                            nc.scalar.activation(dst, src, ACT.Copy).then_inc(fh_done, 1)

            act.wait_ge(eps_there, 1)
            for i in range(4):
                act.wait_ge(turned_out, i + 1)
                squares(0, i, T)
            hi(Unit(0, 0), 0)
            hi(Unit(0, 0), 1)
            hi(Unit(0, 1), 0)

            with act.Fori(0, DEPTH) as l:
                q = l * Q_LAYER
                act.wait_ge(cur_there, l + 1)
                norm(l * 4, T, l * 4, late=Unit(q, 1))
                nc.scalar.activation(tiny[:, 32:48], par[:, 2, R_C:R_C + 16], ACT.Tanh, scale=0.5).then_inc(c_tanh, 1)
                ffn(q, 0, l * 2, T, FULL_GROUP, LAST_GROUP, l * 4 + 1)

                k = K_MIX
                norm(l * 4 + 1, T, l * 4 + 1, late=Unit(q, k + 1))
                for j in range(4):
                    stream(Unit(q, k + j))
                    if j == 0:
                        act.wait_ge(lam_in, l + 1)
                        nc.scalar.activation(tiny[:, 32:40], tiny[:, 40:48], ACT.Exp, scale=-1.0).then_inc(lam_exp, 1)
                for j in range(4):
                    u = Unit(q, k + 4 + j)
                    hi(u.later(2), 0)
                    act.wait_ge(mm_done, u.mm_done(1))
                    nc.scalar.activation(two(Tt[:, u.par, :]), pair(u), ACT.Square).then_inc(gelu_sq, 1)
                    hi(u.later(2), 1)
                    act.wait_ge(gelu_arg, l * 4 + (j + 1))
                    nc.scalar.activation(Tt[:, u.par, :], Pp[:, u.par, :], ACT.Tanh, scale=GELU_C) \
                        .then_inc(gelu_tanh, 1)
                for i in range(12):
                    u = Unit(q, k + 8 + i)
                    if i < 8:
                        j = i
                        act.wait_ge(rg_mm, l * C + (j + 2))
                        if j >= 1:
                            act.wait_ge(la_done, l * C + j)
                        nc.scalar.activation(Rr[:, 0:T], ps[:, 6 + j % 2, 0:T], ACT.Tanh, scale=0.5,
                                             bias=half[:, R_BA + j:R_BA + j + 1])
                        nc.scalar.activation(Rr[:, T:2 * T], ps[:, 6 + j % 2, T:2 * T], ACT.Tanh, scale=0.5,
                                             bias=half[:, R_BX + j:R_BX + j + 1]).then_inc(rg_tanh, 1)
                        hi(u.later(2), 0)
                        act.wait_ge(la_done, l * C + (j + 1))
                        nc.scalar.activation(decay[:, j, :], Ss[:, 0:T], ACT.Exp)
                        nc.scalar.activation(Pp[:, j % 2, 0:T], Ss[:, 0:T], ACT.Tanh).then_inc(rg_exp, 1)
                        act.wait_ge(mm_done, u.mm_done(1))
                        if j >= 2:
                            act.wait_ge(qk_ss, l * 8 + (j - 1))
                        nc.scalar.activation(two(Tt[:, j % 2, :]), pair(u), ACT.Square).then_inc(qk_sq, 1)
                        hi(u.later(2), 1)
                    else:
                        hi(u.later(2), 0)
                        if i == 8:
                            act.wait_ge(f_in, l + 1)
                            nc.scalar.activation(fe, fz, ACT.Abs).then_inc(f_abs, 1)
                            act.wait_ge(f_abs, l * 2 + 1)
                            nc.scalar.activation(fe, fe, ACT.Exp, scale=-1.0).then_inc(f_abs, 1)
                        if i == 9:
                            act.wait_ge(qk_ss, l * 8 + 8)
                            nc.scalar.activation(rqk[:], ps[0:2 * HEADS, 5, 0:T], ACT.Sqrt, bias=eps[0:2 * HEADS, 0:1],
                                                 scale=1.0 / P).then_inc(qk_std, 1)
                            act.wait_ge(keep_done, l * C + C)
                            nc.scalar.activation(keep[:], keep[:], ACT.Sqrt, scale=-1.0).then_inc(root_done, 1)
                            tanh_table()
                        hi(u.later(2), 1)

                def copy_probs(h):
                    act.wait_ge(tr_done, l * HEADS + (h + 1))
                    nc.scalar.activation(probsT, ps[:, 6, 0:384], ACT.Copy).then_inc(pt_done, 1)

                def head_out(h):
                    act.wait_ge(pv_done, l * HEADS + (h + 1))
                    nc.scalar.activation(Fh[:, 1, h, :], ps[:, 7, 0:T], ACT.Copy).then_inc(oh_done, 1)

                def head_exp(h):
                    act.wait_ge(nmax_done, l * HEADS + (h + 1))
                    for b, sl in enumerate((slice(0, P), slice(P, 3 * P))):
                        ins = nc.scalar.activation(scores[:, sl], scores[:, sl], ACT.Exp, bias=tiny[:, b:b + 1],
                                                   accum_out=tiny[:, 2 + b:3 + b])
                    ins.then_inc(exp_done, 1)

                for st in range(HEADS):
                    u = Unit(q, k + 20 + st)
                    hi(u.later(2), 0)
                    if st >= 2:
                        head_out(st - 2)
                    hi(u.later(2), 1)
                    if st >= 1:
                        copy_probs(st - 1)
                    head_exp(st)
                    if st < 4:
                        for j in (2 * st, 2 * st + 1):
                            act.wait_ge(y_done, l * C + (j + 1))
                            nc.scalar.activation(Fh[:, 0, j, :], Pp[:, j % 2, T:2 * T], ACT.Copy).then_inc(yh_done, 1)
                    act.wait_ge(mm_done, u.mm_done(1))
                    for t in range(2):
                        c, r = 2 * (st % 4) + t, R_MERGE + 2 * st + t
                        ins = nc.scalar.activation((gateA if st < 4 else Gb)[:, c, :], bank(u, t, T), ACT.Tanh, scale=0.5,
                                                   bias=half[:, r:r + 1])
                    ins.then_inc(banks_free[u.par], 1)
                for j in range(4):
                    u = Unit(q, k + 28 + j)
                    hi(u.later(2), 0)
                    if j < 2:
                        head_out(HEADS - 2 + j)
                    hi(u.later(2), 1)
                    if j == 0:
                        copy_probs(HEADS - 1)
                for j in range(4):
                    stream(Unit(q, k + 32 + j))
                    act.wait_ge(mp_done, l * 4 + (j + 1))
                    nc.scalar.activation(Hh[:, 1, 2 * j:2 * j + 2, :], two(Pp[:, j % 2, :]), ACT.Copy) \
                        .then_inc(mh_done, 1)
                for j in range(4):
                    u = Unit(q, k + 36 + j)
                    hi(u.later(2), 0)
                    if j < 3:
                        hi(u.later(2), 1)
                    squares(l * 4 + 2, j, T, u)

                norm(l * 4 + 2, T, l * 4 + 2, late=Unit(q, K_FFN2 + 1))
                ffn(q, K_FFN2, l * 2 + 1, T, FULL_GROUP, LAST_GROUP, l * 4 + 3)
                norm(l * 4 + 3, T, l * 4 + 3, late=Unit(q, K_PLE + 1))
                act.wait_ge(p_turned, l + 1)
                nc.scalar.activation(Fh[:, 1, 0:2, :], two(ps[:, 7, :]), ACT.Copy).then_inc(pth_done, 1)
                for j in range(4):
                    u = Unit(q, K_PLE + 2 * j)
                    hi(u.later(2), 0)
                    hi(u.later(2), 1)
                    act.wait_ge(mm_done, u.mm_done(1))
                    for t in range(2):
                        r = R_PLEB + 2 * j + t
                        ins = nc.scalar.activation(Pp[:, j % 2, t * T:(t + 1) * T], bank(u, t, T), ACT.Tanh, scale=0.5,
                                                   bias=half[:, r:r + 1])
                    ins.then_inc(banks_free[u.par], 1)
                    u = u.later(1)
                    hi(u.later(2), 0)
                    if j < 3:
                        hi(u.later(2), 1)
                    squares(l * 4 + 4, j, T, u)

            q = Q_SECOND

            def shift(l, i):
                return lambda kc, s: MOD[:, l, (3 * i) * C + kc, s:s + 1]

            norm(8, T)
            for b in range(4):
                act.wait_ge(turned, b + 6)
                nc.scalar.activation(Xc[:, 2 * b:2 * b + 2, :], two(ps[:, b, :]), ACT.Copy).then_inc(turned_out, 1)
            act.wait_ge(turned_out, 8)
            for i in range(4):
                act.wait_ge(x_normed, i + 1)
                squares(9, i, 512, roomy=True)
            norm(9, 512, 8, shift(0, 0), late=Unit(q, 1))
            ffn(q, 0, 4, 512, PLAIN_FULL, PLAIN_LAST, 10)
            norm(10, 512, 9, shift(0, 1), late=Unit(q, K2_CONV + 1))
            def tap_column(tap, j):
                return par[:, 3 + tap // 16, (tap % 16) * 8 + j:(tap % 16) * 8 + j + 1]

            for j in range(C):
                u = Unit(q, K2_CONV + j)
                hi(u.later(2), 0)
                act.wait_ge(mm_done, u.mm_done(1))
                if j >= 1:
                    act.wait_ge(u_done, j)
                nc.scalar.activation(Ss[:], bank(u, 0), ACT.Identity, bias=par[:, 2, R_PW1B + j:R_PW1B + j + 1])
                nc.scalar.activation(Tt[:, u.par, :], bank(u, 1), ACT.Tanh, scale=0.5, bias=tiny[:, 40 + j:41 + j]) \
                    .then_inc(banks_free[u.par], 1)
                hi(u.later(2), 1)
                for i in range(PE_TAPS[j]):
                    n, tap = sum(PE_TAPS[:j]) + i, TAPS - PE_TAPS[j] + i
                    if n >= DIAGS:
                        act.wait_ge(diag_used, n - DIAGS + 1)
                    nc.scalar.activation(diag[:, n % DIAGS, :], ident, ACT.Copy, scale=tap_column(tap, j)) \
                        .then_inc(diag_there, 1)
            for kc in range(C):
                act.wait_ge(cen_done, kc + 1)
                if kc == C - 1:
                    root_table()
                if kc >= 2:
                    act.wait_ge(var_mm, kc - 1)
                nc.scalar.activation(two(Tt[:, kc % 2, :]), QK[:, :, kc, :], ACT.Square).then_inc(csq_done, 1)
            act.wait_ge(var_mm, C)
            nc.scalar.activation(Rr[:, 0:P], ps[:, 7, 0:P], ACT.Sqrt, bias=eps[:, 0:1], scale=1.0 / D) \
                .then_inc(cstd_done, 1)
            tanh_table()

            def z_high(kc):
                act.wait_ge(zp_done, kc + 1)
                nc.scalar.activation(Fh[:, 0:2, kc, :], two(Pp[:, kc % 2, :]), ACT.Copy).then_inc(zh_done, 1)

            for kc in range(C):
                act.wait_ge(z_done, kc + 1)
                if kc >= 2:
                    act.wait_ge(zp_done, kc - 1)
                nc.scalar.activation(two(Tt[:, kc % 2, :]), QK[:, :, kc, :], ACT.Tanh, scale=tiny[:, kc:kc + 1],
                                     bias=tiny[:, 8 + kc:9 + kc])
                nc.scalar.activation(two(scaled[:, kc % 4, :]), QK[:, :, kc, :], ACT.Identity,
                                     scale=par[:, 2, R_LNG + kc:R_LNG + kc + 1],
                                     bias=par[:, 2, R_LNB + kc:R_LNB + kc + 1]).then_inc(zt_done, 1)
                if kc >= 1:
                    z_high(kc - 1)
            z_high(C - 1)

            def adding_units(k, n, after):
                for j in range(4):
                    u = Unit(q, k + j)
                    hi(u.later(2), 0)
                    if j < 3:
                        hi(u.later(2), 1)
                    squares(after, j, n, u)

            adding_units(K2_PW2, 512, 11)
            norm(11, 512, 10, shift(0, 2), late=Unit(q, K2_FFN2 + 1))
            ffn(q, K2_FFN2, 5, 512, PLAIN_FULL, PLAIN_LAST, 12)
            act.wait_ge(mod_there, 2)
            norm(12, 512, 11, shift(1, 0), late=Unit(q, K2_L1 + 1))
            ffn(q, K2_L1, 6, 512, PLAIN_FULL, PLAIN_LAST, 13)
            norm(13, 512, 12, shift(1, 1), late=Unit(q, K2_KV + 1))
            for j in range(6):
                stream(Unit(q, K2_KV + j))
                if j == 2:
                    for kv in range(KVH):
                        act.wait_ge(dup_mm, kv + 1)
                        nc.scalar.activation(kdup[:, kv, :], ps[:, 6 + kv % 2, :], ACT.Copy).then_inc(dup_done, 1)

            def head2_out(tile):
                act.wait_ge(pv2_done, 2 * tile + 2)
                nc.scalar.activation(Fh[:, 0, tile, :], ps[:, 6 + tile % 2, 0:T], ACT.Copy).then_inc(oh2_done, 1)

            def exp2(h):
                act.wait_ge(nm2_done, h + 1)
                c = 8 * (h % 2)
                nc.scalar.activation(tiny[:, c + 4:c + 6], tiny[:, c + 4:c + 6], ACT.Exp)
                for b in range(2):
                    ins = nc.scalar.activation(probs2[h % 2][b], ps[:, 2 * (h % 2) + b, :], ACT.Exp,
                                               bias=tiny[:, c + b:c + b + 1], accum_out=tiny[:, c + 2 + b:c + 3 + b])
                ins.then_inc(e2_done, 1)

            def normalise2(h):
                act.wait_ge(r2_done, h + 1)
                c = 8 * (h % 2)
                for b in range(2):
                    p = probs2[h % 2][b]
                    ins = nc.scalar.activation(p, p, ACT.Copy, scale=tiny[:, c + 6 + b:c + 7 + b])
                ins.then_inc(pn2_done, 1)

            def copy_probs2(h):
                act.wait_ge(tr2_done, h + 1)
                for i in range(2):
                    ins = nc.scalar.activation(probsT2[h % 2][:, i, :], ps[:, 4 + i, :], ACT.Copy)
                ins.then_inc(pt2_done, 1)

            for i in range(QH + 2):
                if i >= 2:
                    copy_probs2(i - 2)
                if 1 <= i <= QH:
                    normalise2(i - 1)
                if i < QH:
                    exp2(i)
                if i % 2 == 0 and i >= 4:
                    head2_out(i // 2 - 2)
            head2_out(QH // 2 - 1)
            adding_units(K2_WO, T, 14)
            norm(14, T, 13, shift(1, 2), late=Unit(q, K2_FFN4 + 1))
            ffn(q, K2_FFN4, 7, T, PLAIN_FULL, PLAIN_LAST, 15)
            norm(15, T)
            for n in range(2):
                for b in range(2):
                    act.wait_ge(out_mm, 2 * n + b + 1)
                    nc.scalar.activation(otok[:, n, 512 * b:512 * (b + 1)], ps[:, 2 * n + b, :], ACT.Copy) \
                        .then_inc(out_copied, 1)

        @block.vector
        def _(dve):
            dve.sem_inc(lo_done, 8)
            dve.sem_inc(banks_free[0], 1)
            dve.sem_inc(banks_free[1], 1)
            V = nc.vector

            def stt(o, in0, scalar, in1, op0, op1):
                return V.scalar_tensor_tensor(out=o, in0=in0, scalar=scalar, in1=in1, op0=op0, op1=op1)

            def lo(u, t, mod=False):
                if u.last():
                    return
                if mod:
                    if t == 1:
                        dve.drain().then_inc(lo_done, 2)
                    return
                dve.wait_ge(hi_done, u.hi_done(t))
                V.tensor_tensor(tile_of(wl[:, u.par], t), tile_of(raw[:, u.slot], t),
                                tile_of(wh[:, u.par], t).bitcast(F32), ALU.subtract).then_inc(lo_done, 1)

            def stream(u):
                lo(u.later(2), 0)
                lo(u.later(2), 1)

            def rms(norm_i, n):
                dve.wait_ge(std_done, norm_i + 1)
                V.reciprocal(Rr[:, 0:n // 4], Rr[:, 0:n // 4]).then_inc(rs_done, 1)
                dve.wait_ge(rb_done, number(norm_i))

            def add_squares(norm_i, i, n, roomy=False):
                dve.wait_ge(sq_done, norm_i * 4 + (i + 1))
                acc, new = squares_of(0, n), squares_of(i, n, roomy)
                for s in range(n // T):
                    ins = V.tensor_tensor(acc[:, s], acc[:, s], new[:, s], ALU.add)
                ins.then_inc(sqa_done, 1)

            def norm(norm_i, n, hn, gain, shift=None, late=None):
                rms(norm_i, n)

                def product(kc):
                    for s in range(n // T):
                        x = (Xx, Xc)[s]
                        ins = stt(Pp[:, kc % 2, s * T:(s + 1) * T], x[:, kc, :], gain(kc, s), ps[:, 4, s * T:(s + 1) * T],
                                  ALU.mult, ALU.mult)
                    ins.then_inc(hp_done, 1)

                product(0)
                product(1)
                for kc in range(C):
                    dve.wait_ge(hh_done, hn * C + (kc + 1))
                    for s in range(n // T):
                        p, h = Pp[:, kc % 2, s * T:(s + 1) * T], Hh[:, s, kc, :].bitcast(F32)
                        if shift is None:
                            ins = V.tensor_tensor(Hl[:, s, kc, :], p, h, ALU.subtract)
                        else:
                            ins = stt(Hl[:, s, kc, :], p, shift(kc, s), h, ALU.add, ALU.subtract)
                    ins.then_inc(h_done, 1)
                    if kc + 2 < C:
                        dve.drain()
                        product(kc + 2)
                lo(late, 1)

            def keep_modulation(l, idx, i):
                dve.wait_ge(mod_turned, l * ADA_UNITS + (idx + 1))
                V.tensor_scalar(MOD[:, bass.ds(l, 1), bass.ds(idx * 2, 2), :].rearrange("p l t s -> p (l t) s"),
                                ps[:, 5 + i % 2, 0:4].rearrange("p (t s) -> p t s", t=2), 1.0, None,
                                ALU.mult)

            def ffn(q, k, fi, n, order, last, after, gate=None, ada=None):
                for g, units in groups_of(dve, q, k, order, last):
                    for j, (kind, i, u) in enumerate(units):
                        mod = j + 2 < len(units) and units[j + 2][0] == "A"
                        lo(u.later(2), 0, mod)
                        if j >= 2 and units[j - 2][0] == "A":
                            keep_modulation(ada[0], ada_index(ada[1], g, units[j - 2][1]), units[j - 2][1])
                        if isinstance(g, int) and kind == "O" and i >= 2:
                            add_squares(after, i - 1, n)
                        if kind == "A":
                            pass
                        elif kind == "G":
                            done = fi * FC + g * 8
                            dve.wait_ge(tanh_done, done + (i + 1))
                            stt(Ss[:, 0:n], Tt[:, u.par, 0:n], 1.0, bank(u, 0, n), ALU.add, ALU.mult)
                            dve.drain()
                            dve.wait_ge(mm_done, u.mm_done(1))
                            V.tensor_tensor(Pp[:, u.par, 0:n], Ss[:, 0:n], bank(u, 1, n), ALU.mult) \
                                .then_inc(banks_free[u.par], 1)
                        elif gate is None:
                            dve.wait_ge(mm_done, u.mm_done(1))
                            x = Xx[:, 2 * i:2 * i + 2, :]
                            stt(x, pair(u), 0.25, x, ALU.mult, ALU.add).then_inc(banks_free[u.par], 1)
                        else:
                            dve.wait_ge(mm_done, u.mm_done(1))
                            add_gated(u, i, n, gate)
                        if not isinstance(g, int) or j < len(units) - 1:
                            lo(u.later(2), 1, mod)
                        if kind == "G":
                            dve.wait_ge(fh_done, done + (i + 1))
                            if n == T:
                                o, p, h = Fl[:, 0, i, :], Pp[:, u.par, 0:n], Fh[:, 0, i, :]
                            else:
                                o, p, h = Fl[:, 0:2, i, :], two(Pp[:, u.par, :]), Fh[:, 0:2, i, :]
                            V.tensor_tensor(o, p, h.bitcast(F32), ALU.subtract).then_inc(f_done, 1)

            def add_gated(u, i, n, gate):
                for t in range(2):
                    kc = 2 * i + t
                    for s in range(n // T):
                        x = (Xx, Xc)[s][:, kc, :]
                        ins = stt(x, ps[:, 2 * u.par + t, s * T:(s + 1) * T], gate(kc, s), x, ALU.mult, ALU.add)
                ins.then_inc(banks_free[u.par], 1)

            def log1p_start(o, e, z2, acc):
                V.tensor_scalar(acc, e, 2.0, None, ALU.add)
                dve.drain()
                V.reciprocal(acc, acc)
                dve.drain()
                V.tensor_tensor(o, e, acc, ALU.mult)
                dve.drain()
                V.tensor_tensor(z2, o, o, ALU.mult)
                dve.drain()
                V.tensor_scalar(acc, z2, 2.0 / 17, None, ALU.mult)
                dve.drain()

            def log1p_terms(z2, acc, odd):
                for j in odd:
                    stt(acc, acc, 2.0 / j, z2, ALU.add, ALU.mult)
                    dve.drain()

            def log1p_end(o, acc):
                stt(o, acc, 2.0, o, ALU.add, ALU.mult)
                dve.drain()

            V.memset(ones[:], 1.0)
            V.memset(eps[:], EPS).then_inc(eps_there, 1)
            dve.drain().then_inc(ones_there, 1)
            for b in range(4):
                dve.wait_ge(turned, b + 1)
                V.tensor_copy(Xx[:, 2 * b:2 * b + 2, :], two(ps[:, b, :])).then_inc(turned_out, 1)
            for i in (1, 2):
                add_squares(0, i, T)
            dve.wait_ge(turned, 5)
            for i, n in enumerate(PAR_ROWS):
                V.tensor_copy(par[:, i, 0:n], ps[:, 5 + i // 4, (i % 4) * P:(i % 4) * P + n])
            dve.wait_ge(sink_mm, 1)
            V.tensor_copy(tiny[:, 16:32], ps[:, 7, 0:QH])
            dve.drain()
            lo(Unit(0, 0), 0)
            lo(Unit(0, 0), 1)
            lo(Unit(0, 1), 0)

            def layer_gain(r):
                return lambda kc, s: cur[:, r + kc:r + kc + 1]

            with dve.Fori(0, DEPTH) as l:
                q = l * Q_LAYER
                V.tensor_copy(cur[:], par[:, bass.ds(l, 1), 0:R_LAYER].rearrange("p l f -> p (l f)"))
                V.tensor_copy(tiny[0:HEADS, 12:13], fb[:, bass.ds(l, 1)])
                dve.drain()
                V.tensor_scalar(half[:], cur[:], 0.5, None, ALU.mult).then_inc(cur_there, 1)
                norm(l * 4, T, l * 4, layer_gain(R_FFN1), late=Unit(q, 1))
                dve.wait_ge(c_tanh, l + 1)
                stt(Ss[:, 0:16], tiny[:, 32:48], 1.0, par[:, 2, R_C:R_C + 16], ALU.add, ALU.mult)
                dve.drain()
                V.tensor_scalar(cs[:], Ss[:, 0:16].rearrange("p (s m c) -> p c m s", s=2, m=1)
                                .to_broadcast([P, C, 16, 2]), 0.5, None, ALU.mult).then_inc(c_there, 1)
                dve.drain()
                ffn(q, 0, l * 2, T, FULL_GROUP, LAST_GROUP, l * 4 + 1, ada=(l, 0))

                k = K_MIX
                norm(l * 4 + 1, T, l * 4 + 1, layer_gain(R_MIX), late=Unit(q, k + 1))
                keep_modulation(l, ada_index(0, 2, 1), 1)
                lam = cur[:, R_LAM:R_LAM + C]
                z2, e, acc, neg, o = (tiny[:, a:a + C] for a in (0, 32, 40, 48, 56))
                for j in range(4):
                    u = Unit(q, k + j)
                    lo(u.later(2), 0)
                    if j == 0:
                        V.tensor_scalar(neg, lam, -1.0, None, ALU.mult)
                        V.tensor_scalar(cur[:, R_QN:R_QN + 1], cur[:, R_QN:R_QN + 1], float(P) ** -0.5, None, ALU.mult)
                        dve.drain()
                        V.tensor_tensor(acc, lam, neg, ALU.max).then_inc(lam_in, 1)
                    elif j == 1:
                        dve.wait_ge(lam_exp, l + 1)
                        log1p_start(o, e, z2, acc)
                        log1p_terms(z2, acc, (15, 13))
                    elif j == 2:
                        log1p_terms(z2, acc, (11, 9, 7, 5, 3))
                    else:
                        log1p_end(o, acc)
                        stt(o, neg, 0.0, o, ALU.max, ALU.add)
                        dve.drain()
                        V.tensor_scalar(lam, o, -4.0, None, ALU.mult)
                    dve.wait_ge(mm_done, u.mm_done(1))
                    for s in range(4):
                        for t in range(2):
                            kc = 2 * j + t
                            tap = cur[:, R_CONV + 8 * (3 - s) + kc:R_CONV + 8 * (3 - s) + kc + 1]
                            if s == 0:
                                ins = V.tensor_scalar(Xc[:, kc, :], bank(u, t, T), tap,
                                                      cur[:, R_CONVB + kc:R_CONVB + kc + 1], ALU.mult, ALU.add)
                            else:
                                ins = stt(Xc[:, kc, s:T], bank(u, t, T - s), tap, Xc[:, kc, s:T], ALU.mult, ALU.add)
                        if s < 3:
                            dve.drain()
                    ins.then_inc(banks_free[u.par], 1)
                    lo(u.later(2), 1)
                for j in range(4):
                    u = Unit(q, k + 4 + j)
                    lo(u.later(2), 0)
                    dve.wait_ge(gelu_sq, l * 4 + (j + 1))
                    V.tensor_scalar(Ss[:], Tt[:, u.par, :], GELU_A, 1.0, ALU.mult, ALU.add)
                    dve.drain()
                    V.tensor_tensor(two(Pp[:, u.par, :]), two(Ss[:]), pair(u), ALU.mult).then_inc(gelu_arg, 1)
                    lo(u.later(2), 1)
                    dve.wait_ge(gelu_tanh, l * 4 + (j + 1))
                    stt(Gb[:, 2 * j:2 * j + 2, :], two(Tt[:, u.par, :]), 1.0, pair(u), ALU.add, ALU.mult) \
                        .then_inc(banks_free[u.par], 1)
                for i in range(12):
                    u = Unit(q, k + 8 + i)
                    if i < 8:
                        j, hp, what = i, i // 2, i % 2
                        dve.wait_ge(rg_tanh, l * C + (j + 1))
                        stt(Xc[:, j, :], Rr[:, T:2 * T], 1.0, Xc[:, j, :], ALU.add, ALU.mult)
                        V.tensor_scalar(Ss[:, 0:T], Rr[:, 0:T], 1.0, cur[:, R_LAM + j:R_LAM + j + 1], ALU.add, ALU.mult) \
                            .then_inc(la_done, 1)
                        lo(u.later(2), 0)
                        dve.wait_ge(rg_exp, l * C + (j + 1))
                        V.tensor_tensor(Ss[:, T:2 * T], decay[:, j, :], decay[:, j, :], ALU.mult)
                        dve.drain()
                        stt(keep[:, j, :], Ss[:, T:2 * T], 1.0, Pp[:, j % 2, 0:T], ALU.add, ALU.mult) \
                            .then_inc(keep_done, 1)
                        dve.wait_ge(qk_sq, l * 8 + (j + 1))
                        dst = (Qb, Kb)[what][:, 2 * hp:2 * hp + 2, :]
                        V.tensor_scalar(dst, pair(u), cur[:, R_QN + what:R_QN + what + 1], None, ALU.mult) \
                            .then_inc(banks_free[u.par], 1)
                        lo(u.later(2), 1)
                    else:
                        hp = i - 8
                        lo(u.later(2), 0)
                        if hp == 0:
                            dve.wait_ge(f_mm, l + 2)
                            V.tensor_scalar(fz, ps[0:HEADS, 4, 0:T], tiny[0:HEADS, 12:13], None, ALU.add).then_inc(f_in, 1)
                        elif hp == 1:
                            dve.wait_ge(f_abs, l * 2 + 2)
                            log1p_start(fa, fe, fsq, dmask[:])
                            log1p_terms(fsq, dmask[:], (15,))
                        elif hp == 2:
                            dve.wait_ge(qk_std, l + 1)
                            V.reciprocal(rqk[:], rqk[:])
                            log1p_terms(fsq, dmask[:], (13, 11, 9, 7, 5, 3))
                        else:
                            log1p_end(fa, dmask[:])
                            stt(fa, fz, 0.0, fa, ALU.min, ALU.subtract)
                            V.memset(fe, 1.0)
                            dve.drain()
                            V.tensor_tensor_scan(fz, fe, fa, 0.0, ALU.mult, ALU.add)
                            dve.drain()
                            V.tensor_scalar(dneg, two(fz), -1.0, None, ALU.mult)
                            dve.drain()
                        dve.wait_ge(mm_done, u.mm_done(1))
                        V.tensor_copy(Vb[:, :, T * hp:T * (hp + 1)], pair(u)).then_inc(banks_free[u.par], 1)
                        lo(u.later(2), 1)
                def masks(h):
                    V.tensor_scalar(rmask[:, 0:T], rqk[:], ident[0:2 * HEADS, h:h + 1], None, ALU.mult)
                    V.tensor_scalar(rmask[:, T:2 * T], rqk[:], ident[0:2 * HEADS, HEADS + h:HEADS + h + 1], None,
                                    ALU.mult)
                    V.tensor_scalar(two(dmasks[h % 2]), dneg, ident[0:HEADS, h:h + 1], None, ALU.mult).then_inc(rm_done, 1)

                def low_out(h):
                    dve.wait_ge(oh_done, l * HEADS + (h + 1))
                    V.tensor_tensor(Fl[:, 1, h, :], ps[:, 7, 0:T], Fh[:, 1, h, :].bitcast(F32), ALU.subtract) \
                        .then_inc(o_done, 1)

                masks(0)
                for st in range(HEADS):
                    u = Unit(q, k + 20 + st)
                    lo(u.later(2), 0)
                    if st >= 2:
                        low_out(st - 2)
                    dve.wait_ge(bc_done, l * HEADS + (st + 1))
                    V.tensor_tensor(Qb[:, st, :], Qb[:, st, :], ps[:, 4, 0:T], ALU.mult)
                    V.tensor_tensor(Kb[:, st, :], Kb[:, st, :], ps[:, 4, T:2 * T], ALU.mult).then_inc(qkn_done, 1)
                    if st + 1 < HEADS:
                        masks(st + 1)
                    lo(u.later(2), 1)
                    dve.wait_ge(s_done, l * HEADS + (st + 1))
                    V.tensor_tensor(scores[:, 0:P], ps[:, 5, 0:P], low, ALU.add)
                    V.tensor_copy(scores[:, P:2 * P], ps[:, 5, P:2 * P])
                    V.tensor_tensor(scores[:, 2 * P:3 * P], ps[:, 5, 2 * P:3 * P], low, ALU.add)
                    dve.drain()
                    V.tensor_reduce(tiny[:, 6:7], scores[:, 0:P], AX_X, ALU.max)
                    V.tensor_reduce(tiny[:, 7:8], scores[:, P:3 * P], AX_X, ALU.max)
                    dve.drain()
                    V.tensor_scalar(tiny[:, 0:2], tiny[:, 6:8], -1.0, None, ALU.mult).then_inc(nmax_done, 1)
                    two_chunks = (2 * st, 2 * st + 1)
                    if st < 4:
                        if st == 0:
                            dve.wait_ge(root_done, l + 1)
                        for j in two_chunks:
                            stt(Xc[:, j, :], Xc[:, j, :], 0.5, keep[:, j, :], ALU.mult, ALU.mult)
                    dve.wait_ge(exp_done, l * HEADS + (st + 1))
                    V.reciprocal(tiny[:, 4:6], tiny[:, 2:4])
                    dve.drain()
                    V.tensor_scalar(scores[:, 0:P], scores[:, 0:P], tiny[:, 4:5], None, ALU.mult)
                    V.tensor_scalar(scores[:, P:3 * P], scores[:, P:3 * P], tiny[:, 5:6], None, ALU.mult) \
                        .then_inc(pn_done, 1)
                    if st < 4:
                        for j in two_chunks:
                            V.tensor_tensor_scan(Pp[:, j % 2, 0:T], decay[:, j, :], Xc[:, j, :], 0.0, ALU.mult, ALU.add)
                        dve.drain()
                        for j in two_chunks:
                            V.tensor_tensor(Pp[:, j % 2, T:2 * T], Pp[:, j % 2, 0:T], Gb[:, j, :], ALU.mult) \
                                .then_inc(y_done, 1)
                        for j in two_chunks:
                            dve.wait_ge(yh_done, l * C + (j + 1))
                            V.tensor_tensor(Fl[:, 0, j, :], Pp[:, j % 2, T:2 * T], Fh[:, 0, j, :].bitcast(F32),
                                            ALU.subtract).then_inc(ya_done, 1)
                for j in range(4):
                    u = Unit(q, k + 28 + j)
                    lo(u.later(2), 0)
                    if j < 2:
                        low_out(HEADS - 2 + j)
                    dve.wait_ge(mm_done, u.mm_done(1))
                    ga = gateA[:, 2 * j:2 * j + 2, :]
                    stt(ga, ga, 1.0, pair(u), ALU.add, ALU.mult).then_inc(banks_free[u.par], 1)
                    lo(u.later(2), 1)
                for j in range(4):
                    u = Unit(q, k + 32 + j)
                    lo(u.later(2), 0)
                    dve.wait_ge(mm_done, u.mm_done(1))
                    stt(two(Ss[:]), Gb[:, 2 * j:2 * j + 2, :], 1.0, pair(u), ALU.add, ALU.mult) \
                        .then_inc(banks_free[u.par], 1)
                    dve.drain()
                    stt(two(Pp[:, j % 2, :]), two(Ss[:]), 2.0, gateA[:, 2 * j:2 * j + 2, :], ALU.mult, ALU.add) \
                        .then_inc(mp_done, 1)
                    lo(u.later(2), 1)
                    dve.wait_ge(mh_done, l * 4 + (j + 1))
                    V.tensor_tensor(Hl[:, 1, 2 * j:2 * j + 2, :], two(Pp[:, j % 2, :]),
                                    Hh[:, 1, 2 * j:2 * j + 2, :].bitcast(F32), ALU.subtract).then_inc(m_done, 1)
                for j in range(4):
                    u = Unit(q, k + 36 + j)
                    lo(u.later(2), 0)
                    if j >= 2:
                        add_squares(l * 4 + 2, j - 1, T)
                    dve.wait_ge(mm_done, u.mm_done(1))
                    x = Xx[:, 2 * j:2 * j + 2, :]
                    stt(x, pair(u), 0.25, x, ALU.mult, ALU.add).then_inc(banks_free[u.par], 1)
                    if j < 3:
                        lo(u.later(2), 1)

                norm(l * 4 + 2, T, l * 4 + 2, layer_gain(R_FFN2), late=Unit(q, K_FFN2 + 1))
                ffn(q, K_FFN2, l * 2 + 1, T, FULL_GROUP, LAST_GROUP, l * 4 + 3, ada=(l, 1))
                norm(l * 4 + 3, T, l * 4 + 3, layer_gain(R_PLE), late=Unit(q, K_PLE + 1))
                keep_modulation(l, ada_index(1, 2, 1), 1)
                dve.wait_ge(pth_done, l + 1)
                V.tensor_tensor(Fl[:, 1, 0:2, :], two(ps[:, 7, :]), Fh[:, 1, 0:2, :].bitcast(F32), ALU.subtract) \
                    .then_inc(p_there, 1)
                for j in range(4):
                    u = Unit(q, K_PLE + 2 * j)
                    stream(u)
                    ue, u = u, u.later(1)
                    lo(u.later(2), 0)
                    if j >= 2:
                        add_squares(l * 4 + 4, j - 1, T)
                    dve.wait_ge(banks_free[ue.par], ue.read_out())
                    dve.wait_ge(mm_done, u.mm_done(1))
                    stt(two(Ss[:]), two(Pp[:, j % 2, :]), 1.0, pair(u), ALU.add, ALU.mult)
                    dve.drain()
                    x = Xx[:, 2 * j:2 * j + 2, :]
                    stt(x, two(Ss[:]), 0.5, x, ALU.mult, ALU.add).then_inc(banks_free[u.par], 1)
                    if j < 3:
                        lo(u.later(2), 1)

            q = Q_SECOND
            def layer_consts(l):
                for s in range(2):
                    V.tensor_tensor(MOD[:, l, :, s], MOD[:, l, :, s], par[:, 5 + l, 0:N_MOD * C], ALU.add)
                dve.drain()
                for i in range(3):
                    r = R_NORM + (3 * l + i) * C
                    for s in range(2):
                        stt(S1[:, i, :, s], MOD[:, l, (3 * i + 1) * C:(3 * i + 2) * C, s], 1.0, par[:, 2, r:r + C],
                            ALU.add, ALU.mult)
                    factor = 0.25 if i != 1 else (0.5 if l == 0 else 1.0)
                    V.tensor_scalar(G1[:, i], MOD[:, l, (3 * i + 2) * C:(3 * i + 3) * C, :], factor, None, ALU.mult)
                dve.drain().then_inc(mod_there, 1)

            def gain(i):
                return lambda kc, s: S1[:, i, kc, s:s + 1]

            def gate(i):
                return lambda kc, s: G1[:, i, kc, s:s + 1]

            def shift(l, i):
                return lambda kc, s: MOD[:, l, (3 * i) * C + kc, s:s + 1]

            layer_consts(0)
            rms(8, T)
            for kc in range(C):
                ins = stt(Xx[:, kc, :], Xx[:, kc, :], par[:, 2, R_FINAL + kc:R_FINAL + kc + 1], ps[:, 4, 0:T], ALU.mult,
                          ALU.mult)
                if kc % 2:
                    ins.then_inc(x_normed, 1)
            for i in (1, 2):
                add_squares(9, i, 512, roomy=True)
                dve.drain()
            norm(9, 512, 8, gain(0), shift(0, 0), Unit(q, 1))
            V.tensor_scalar(tiny[:, 40:48], par[:, 2, R_PW1B + C:R_PW1B + 2 * C], 0.5, None, ALU.mult)
            V.tensor_scalar(tiny[:, 0:16], par[:, 2, R_LNG:R_LNG + 16], 0.5, None, ALU.mult)
            V.tensor_scalar(par[:, 3, :], par[:, 3, :], 0.5, None, ALU.mult)
            V.tensor_scalar(par[:, 4, 0:PAR_ROWS[4]], par[:, 4, 0:PAR_ROWS[4]], 0.5, None, ALU.mult)
            V.memset(upad[:], 0.0)
            dve.drain()
            ffn(q, 0, 4, 512, PLAIN_FULL, PLAIN_LAST, 10, gate(0))
            norm(10, 512, 9, gain(1), shift(0, 1), Unit(q, K2_CONV + 1))
            def add_tap_sums(j):
                dve.wait_ge(diag_used, sum(PE_TAPS[:j + 1]))
                V.tensor_tensor(QK[:, :, j, :], QK[:, :, j, :], two(ps[:, 4 + j % 2, :]), ALU.add).then_inc(cv_done, 1)

            for j in range(C):
                u = Unit(q, K2_CONV + j)
                lo(u.later(2), 0)
                dve.wait_ge(banks_free[u.par], u.read_out())
                pb = upad[:, u.par]
                stt(pb[:, :, PAD:PAD + T], two(Tt[:, u.par, :]), 1.0, two(Ss[:]), ALU.add, ALU.mult).then_inc(u_done, 1)
                lo(u.later(2), 1)
                dve.drain()
                for tap in range(TAPS - PE_TAPS[j]):
                    w = par[:, 3 + tap // 16, (tap % 16) * 8 + j:(tap % 16) * 8 + j + 1]
                    acc, src = two(Pp[:, tap % 2, :]), pb[:, :, tap:tap + T]
                    if tap == 0:
                        V.tensor_scalar(acc, src, w, par[:, 2, R_DWB + j:R_DWB + j + 1], ALU.mult, ALU.add)
                    elif tap == 1:
                        V.tensor_scalar(acc, src, w, None, ALU.mult)
                    else:
                        stt(acc, src, w, acc, ALU.mult, ALU.add)
                    if tap % 2:
                        dve.drain()
                dve.drain()
                V.tensor_tensor(QK[:, :, j, :], two(Pp[:, 0, :]), two(Pp[:, 1, :]), ALU.add)
                if j >= 1:
                    add_tap_sums(j - 1)
            dve.drain()
            add_tap_sums(C - 1)
            dve.wait_ge(mu_mm, 1)
            V.tensor_scalar(Ss[:], ps[:, 6, :], -1.0 / D, None, ALU.mult)
            dve.drain()
            for kc in range(C):
                V.tensor_tensor(QK[:, :, kc, :], QK[:, :, kc, :], two(Ss[:]), ALU.add).then_inc(cen_done, 1)
            dve.wait_ge(cstd_done, 1)
            V.reciprocal(Rr[:, 0:P], Rr[:, 0:P]).then_inc(rs_done, 1)
            dve.wait_ge(rb_done, 12)

            def z_of(kc):
                V.tensor_tensor(QK[:, :, kc, :], QK[:, :, kc, :], two(ps[:, 7, :]), ALU.mult).then_inc(z_done, 1)

            def z_low(kc):
                dve.wait_ge(zh_done, kc + 1)
                V.tensor_tensor(Fl[:, 0:2, kc, :], two(Pp[:, kc % 2, :]), Fh[:, 0:2, kc, :].bitcast(F32), ALU.subtract) \
                    .then_inc(z_there, 1)

            z_of(0)
            z_of(1)
            for kc in range(C):
                dve.wait_ge(zt_done, kc + 1)
                stt(two(Pp[:, kc % 2, :]), two(Tt[:, kc % 2, :]), 1.0, two(scaled[:, kc % 4, :]), ALU.add, ALU.mult) \
                    .then_inc(zp_done, 1)
                if kc + 2 < C:
                    z_of(kc + 2)
                if kc >= 1:
                    z_low(kc - 1)
                    dve.drain()
            z_low(C - 1)
            for s in range(2):
                V.tensor_tensor(Ss[:, s * C:(s + 1) * C], MOD[:, 0, 5 * C:6 * C, s], par[:, 2, R_PW2B:R_PW2B + C], ALU.mult)
            dve.drain()
            for kc in range(C):
                for s in range(2):
                    x = (Xx, Xc)[s][:, kc, :]
                    V.tensor_scalar(x, x, Ss[:, s * C + kc:s * C + kc + 1], None, ALU.add)
            dve.drain()
            for j in range(4):
                u = Unit(q, K2_PW2 + j)
                lo(u.later(2), 0)
                if j >= 2:
                    add_squares(11, j - 1, 512)
                dve.wait_ge(mm_done, u.mm_done(1))
                add_gated(u, j, 512, gate(1))
                if j < 3:
                    lo(u.later(2), 1)
            norm(11, 512, 10, gain(2), shift(0, 2), Unit(q, K2_FFN2 + 1))
            ffn(q, K2_FFN2, 5, 512, PLAIN_FULL, PLAIN_LAST, 12, gate(2))
            dve.drain()
            layer_consts(1)
            norm(12, 512, 11, gain(0), shift(1, 0), Unit(q, K2_L1 + 1))
            ffn(q, K2_L1, 6, 512, PLAIN_FULL, PLAIN_LAST, 13, gate(0))
            norm(13, 512, 12, gain(1), shift(1, 1), Unit(q, K2_KV + 1))
            cos, sin = ro[:, RO_COS:RO_COS + T], ro[:, RO_SIN:RO_SIN + T]

            def rotated(i, tiles):
                dve.wait_ge(rot_mm, i + 1)
                dve.drain()
                for t in range(2):
                    V.tensor_tensor(Ss[:, t * T:(t + 1) * T], ps[:, 4 + i % 2, t * T:(t + 1) * T], sin, ALU.mult)
                    V.tensor_tensor(Pp[:, 0, t * T:(t + 1) * T], tiles(t), cos, ALU.mult)
                dve.drain()
                for t in range(2):
                    ins = V.tensor_tensor(tiles(t), Pp[:, 0, t * T:(t + 1) * T], Ss[:, t * T:(t + 1) * T], ALU.add)
                ins.then_inc(rot_done, 1)

            u = Unit(q, K2_KV)
            lo(u.later(2), 0)
            dve.wait_ge(mm_done, u.mm_done(1))
            V.tensor_copy(kraw, ps[:, 2 * u.par:2 * u.par + 2, :]).then_inc(banks_free[u.par], 1)
            lo(u.later(2), 1)
            u = u.later(1)
            lo(u.later(2), 0)
            dve.wait_ge(mm_done, u.mm_done(1))
            V.tensor_copy(v2, ps[:, 2 * u.par:2 * u.par + 2, :].rearrange("p b (t d) -> p (b t) d", t=2)) \
                .then_inc(banks_free[u.par], 1)
            lo(u.later(2), 1)
            rotated(0, lambda t: kraw[:, t, 0:T])
            for j in range(4):
                u = Unit(q, K2_Q + j)
                lo(u.later(2), 0)
                dve.wait_ge(mm_done, u.mm_done(1))
                V.tensor_scalar(Qb[:, 2 * j:2 * j + 2, :], pair(u), HD ** -0.5, None, ALU.mult) \
                    .then_inc(banks_free[u.par], 1)
                lo(u.later(2), 1)
                if j >= 1:
                    rotated(j, lambda t, j=j: Qb[:, 2 * (j - 1) + t, :])
            rotated(4, lambda t: Qb[:, 6 + t, :])

            def low2_out(tile):
                dve.wait_ge(oh2_done, tile + 1)
                V.tensor_tensor(Fl[:, 0, tile, :], ps[:, 6 + tile % 2, 0:T], Fh[:, 0, tile, :].bitcast(F32),
                                ALU.subtract).then_inc(o2_done, 1)

            def largest2(h):
                c = 8 * (h % 2)
                s = ps[:, 2 * (h % 2):2 * (h % 2) + 2, :]
                sink = tiny[:, 16 + h:17 + h]
                dve.wait_ge(s2_done, h + 1)
                V.tensor_tensor(s[:, 0, P:2 * P], s[:, 0, P:2 * P], low, ALU.add)
                V.tensor_tensor(s[:, 1, 0:P], s[:, 1, 0:P], up, ALU.add)
                dve.drain()
                V.tensor_reduce(tiny[:, 32:34], s, AX_X, ALU.max)
                dve.drain()
                V.tensor_scalar(tiny[:, c:c + 2], tiny[:, 32:34], sink, -1.0, ALU.max, ALU.mult)
                dve.drain()
                V.tensor_scalar(tiny[:, c + 4:c + 6], tiny[:, c:c + 2], sink, None, ALU.add).then_inc(nm2_done, 1)

            largest2(0)
            for h in range(QH):
                if h + 1 < QH:
                    largest2(h + 1)
                c = 8 * (h % 2)
                dve.wait_ge(e2_done, h + 1)
                V.tensor_tensor(tiny[:, 34:36], tiny[:, c + 2:c + 4], tiny[:, c + 4:c + 6], ALU.add)
                dve.drain()
                V.reciprocal(tiny[:, c + 6:c + 8], tiny[:, 34:36]).then_inc(r2_done, 1)
                if h % 2 == 1 and h >= 5:
                    low2_out(h // 2 - 2)
            low2_out(QH // 2 - 2)
            low2_out(QH // 2 - 1)
            for j in range(4):
                u = Unit(q, K2_WO + j)
                lo(u.later(2), 0)
                if j >= 2:
                    add_squares(14, j - 1, T)
                dve.wait_ge(mm_done, u.mm_done(1))
                add_gated(u, j, T, gate(1))
                if j < 3:
                    lo(u.later(2), 1)
            norm(14, T, 13, gain(2), shift(1, 2), Unit(q, K2_FFN4 + 1))
            ffn(q, K2_FFN4, 7, T, PLAIN_FULL, PLAIN_LAST, 15, gate(2))
            rms(15, T)
            for kc in range(C):
                stt(Xx[:, kc, :], Xx[:, kc, :], par[:, 2, R_FING + kc:R_FING + kc + 1], ps[:, 4, 0:T], ALU.mult, ALU.mult) \
                    .then_inc(final_done, 1)


_INS = ["x", "p", "ffn1_norm", "ffn1_w_in", "ffn1_w_out", "mix_norm", "w_in", "merge_b", "conv_w", "conv_b", "rg_wa",
        "rg_ba", "rg_wx", "rg_bx", "rg_lambda", "f_b", "q_norm", "k_norm", "w_rnn_out", "w_attn_out", "w_o",
        "ffn2_norm", "ffn2_w_in", "ffn2_w_out", "ple_norm", "ple_w_gate", "ple_b_gate", "ple_w_proj", "final_norm",
        "c_2", "ctx_2", "c_ctx_2", "norm_g_2", "ada_w_2", "ada_b_2", "ffn1_wi_2", "ffn1_wo_2", "ffn2_wi_2",
        "ffn2_wo_2", "conv_pw1_w_2", "conv_pw1_b_2", "conv_dw_w_2", "conv_dw_b_2", "conv_ln_g_2", "conv_ln_b_2",
        "conv_pw2_w_2", "conv_pw2_b_2", "attn_w_qkv_2", "attn_w_o_2", "attn_sink_2", "final_g_2"]


def kernel(**inputs):
    import concourse.bacc as bacc
    from concourse.bass_utils import run_bass_kernel_spmd

    nc = bacc.Bacc("TRN2", target_bir_lowering=False, num_devices=1)
    arrays = {f"in_{n}": np.ascontiguousarray(inputs[n]) for n in _INS}
    arrays["in_co"], arrays["in_ro"] = shape_constants()
    aps = {n[3:]: nc.dram_tensor(n, a.shape, F32, kind="ExternalInput").ap() for n, a in arrays.items()}
    out = nc.dram_tensor("out", (1, T, D), F32, kind="ExternalOutput").ap()
    build(nc, aps, out)
    r = run_bass_kernel_spmd(nc, [arrays], core_ids=[0])
    return r.results[0]["out"]
```
